# Optimizing a Trainium2 kernel written in Bass

```python
import math
import jax, jax.numpy as jnp
from jax import lax
import numpy as np

D_MODEL = 1024
BATCH = 1
SEQ = 256
DEPTH = 1

GRID_W = 64
CTX_LEN = 256
EPS = 1e-6
ROPE_THETA = 10000.0
Q_BLOCK = 128

DIFF_HEADS = 4
DIFF_HEAD_DIM = 64
DIFF_V_DIM = 2 * DIFF_HEAD_DIM
DIFF_WIDTH = DIFF_HEADS * DIFF_V_DIM
DIFF_SCALE = DIFF_HEAD_DIM ** -0.5

MLA_HEADS = 4
MLA_NOPE = 128
MLA_ROPE = 64
MLA_V = 128
MLA_Q_RANK = 256
MLA_KV_RANK = 128
MLA_WIDTH = MLA_HEADS * MLA_V
MLA_SCALE = (MLA_NOPE + MLA_ROPE) ** -0.5

MIX_WIDTH = DIFF_WIDTH + MLA_WIDTH
ROPE_PAIRS = DIFF_HEAD_DIM // 4

IN_SPLITS = (DIFF_HEADS * 2 * DIFF_HEAD_DIM,
             DIFF_HEADS * 2 * DIFF_HEAD_DIM,
             DIFF_HEADS * DIFF_V_DIM,
             MLA_Q_RANK,
             MLA_KV_RANK,
             MLA_ROPE)
IN_COLS = sum(IN_SPLITS)

N_EXPERTS = 32
TOP_K = 4
D_FF = 1024
SWIGLU_LIMIT = 7.0
SWIGLU_ALPHA = 1.702
MOE_BLOCK = 128


def rmsnorm(x, w):
    xf = x.astype(jnp.float32)
    y = xf * lax.rsqrt(jnp.mean(xf * xf, axis=-1, keepdims=True) + EPS)
    return (y * w.astype(jnp.float32)).astype(x.dtype)

def modulate(h, shift, scale):
    return h * (1 + scale) + shift

def axial_angles(n):
    rows = n // GRID_W
    row = jnp.repeat(jnp.arange(rows, dtype=jnp.float32), GRID_W)
    col = jnp.tile(jnp.arange(GRID_W, dtype=jnp.float32), rows)
    inv = ROPE_THETA ** (-jnp.arange(ROPE_PAIRS, dtype=jnp.float32) / ROPE_PAIRS)
    return jnp.stack([row[:, None] * inv, col[:, None] * inv], axis=1)

def apply_axial_rope(x, ang):
    p = x.shape[-1] // 4
    xf = x.astype(jnp.float32).reshape(*x.shape[:-1], 2, 2, p)
    x1, x2 = xf[..., 0, :], xf[..., 1, :]
    cos, sin = jnp.cos(ang), jnp.sin(ang)
    out = jnp.stack([x1 * cos - x2 * sin, x2 * cos + x1 * sin], axis=-2)
    return out.reshape(x.shape).astype(x.dtype)

def mixer_inputs(h, w_in, q_norm_w, kv_norm_w, w_uq, w_ukv, ang):
    B, n, _ = h.shape
    proj = h @ w_in
    cuts = list(np.cumsum(IN_SPLITS)[:-1])
    dq, dk, dv, cq, ckv, kr = jnp.split(proj, cuts, axis=-1)
    dq = dq.reshape(B, n, DIFF_HEADS, 2, DIFF_HEAD_DIM)
    dk = dk.reshape(B, n, DIFF_HEADS, 2, DIFF_HEAD_DIM)
    dv = dv.reshape(B, n, DIFF_HEADS, DIFF_V_DIM)
    q = (rmsnorm(cq, q_norm_w) @ w_uq).reshape(B, n, MLA_HEADS, MLA_NOPE + MLA_ROPE)
    kv = (rmsnorm(ckv, kv_norm_w) @ w_ukv).reshape(B, n, MLA_HEADS, MLA_NOPE + MLA_V)
    q_nope, q_rope = q[..., :MLA_NOPE], q[..., MLA_NOPE:]
    k_nope, mv = kv[..., :MLA_NOPE], kv[..., MLA_NOPE:]
    if ang is not None:
        dq = apply_axial_rope(dq, ang[:, None, None])
        dk = apply_axial_rope(dk, ang[:, None, None])
        q_rope = apply_axial_rope(q_rope, ang[:, None])
        kr = apply_axial_rope(kr, ang)
    return (dq, dk, dv, q_nope, q_rope, k_nope, kr, mv)

def diff_attend(q, k, v, lam):
    s = jnp.einsum('bqhcd,bkhcd->bchqk', q, k).astype(jnp.float32) * DIFF_SCALE
    p = jax.nn.softmax(s, axis=-1)
    p = p[:, 0] - lam * p[:, 1]
    return jnp.einsum('bhqk,bkhe->bqhe', p.astype(v.dtype), v)

def mla_attend(q_nope, q_rope, k_nope, k_rope, v):
    s = (jnp.einsum('bqhd,bkhd->bhqk', q_nope, k_nope)
         + jnp.einsum('bqhr,bkr->bhqk', q_rope, k_rope)).astype(jnp.float32) * MLA_SCALE
    p = jax.nn.softmax(s, axis=-1)
    return jnp.einsum('bhqk,bkhe->bqhe', p.astype(v.dtype), v)

def to_blocks(t):
    B, n = t.shape[:2]
    return jnp.moveaxis(t.reshape(B, n // Q_BLOCK, Q_BLOCK, *t.shape[2:]), 1, 0)

def from_blocks(t):
    t = jnp.moveaxis(t, 0, 1)
    return t.reshape(t.shape[0], -1, *t.shape[3:])

def merge_heads(o_diff, o_mla, subln_w, lam_init, w_out):
    B, n = o_diff.shape[:2]
    o_diff = rmsnorm(o_diff, subln_w) * (1.0 - lam_init)
    mix = jnp.concatenate([o_diff.reshape(B, n, DIFF_WIDTH), o_mla.reshape(B, n, MLA_WIDTH)], axis=-1)
    return mix @ w_out

def clamped_swiglu(g, u):
    g = jnp.minimum(g, SWIGLU_LIMIT)
    u = jnp.clip(u, -SWIGLU_LIMIT, SWIGLU_LIMIT)
    return g * jax.nn.sigmoid(SWIGLU_ALPHA * g) * (u + 1)

def moe(h, router_w, router_b, w1, b1, w2, b2):
    T, D = h.shape
    logits = (h @ router_w + router_b).astype(jnp.float32)
    top_v, top_i = lax.top_k(logits, TOP_K)
    gates = jax.nn.softmax(top_v, axis=-1).astype(h.dtype)
    flat_e = top_i.reshape(-1)
    flat_tok = jnp.repeat(jnp.arange(T, dtype=jnp.int32), TOP_K)
    order = jnp.argsort(flat_e)
    e_sorted = flat_e[order]
    tok_sorted = flat_tok[order]
    gate_sorted = gates.reshape(-1)[order]
    counts = jnp.bincount(flat_e, length=N_EXPERTS)
    padded = ((counts + MOE_BLOCK - 1) // MOE_BLOCK) * MOE_BLOCK
    ends = jnp.cumsum(padded)
    pad_start = ends - padded
    grp_start = jnp.cumsum(counts) - counts
    n_assign = T * TOP_K
    rank = jnp.arange(n_assign, dtype=jnp.int32) - grp_start[e_sorted]
    dest = pad_start[e_sorted] + rank
    n_blocks = (n_assign + N_EXPERTS * (MOE_BLOCK - 1) + MOE_BLOCK - 1) // MOE_BLOCK
    row_tok = jnp.full((n_blocks * MOE_BLOCK,), T, jnp.int32).at[dest].set(tok_sorted)
    h_pad = jnp.concatenate([h, jnp.zeros((1, D), h.dtype)], axis=0)
    xs = h_pad[row_tok].reshape(n_blocks, MOE_BLOCK, D)
    blk_e = jnp.minimum(jnp.searchsorted(ends, jnp.arange(n_blocks) * MOE_BLOCK, side='right'),
                        N_EXPERTS - 1)

    def expert_block(args):
        xb, e = args
        hid = xb @ w1[e] + b1[e]
        return clamped_swiglu(hid[:, :D_FF], hid[:, D_FF:]) @ w2[e] + b2[e]

    ys = lax.map(expert_block, (xs, blk_e)).reshape(-1, D)
    contrib = ys[dest] * gate_sorted[:, None]
    return jax.ops.segment_sum(contrib, tok_sorted, num_segments=T)

def first_inputs(seed: int = 0) -> dict:
    key = jax.random.key(seed)
    ks = jax.random.split(key, 32)
    f32 = jnp.float32
    L = DEPTH

    def nrm(k, shape, scale):
        return jax.random.normal(k, shape, f32) * scale

    def gain(k, shape):
        return 1.0 + 0.05 * jax.random.normal(k, shape, f32)

    return {
        'x': nrm(ks[0], (BATCH, SEQ, D_MODEL), 1.0),
        'c': nrm(ks[1], (BATCH, D_MODEL), 1.0),
        'ctx': nrm(ks[2], (BATCH, CTX_LEN, D_MODEL), 1.0),
        'c_ctx': nrm(ks[3], (D_MODEL,), 1.0),
        'w_ada': nrm(ks[4], (L, D_MODEL, 6 * D_MODEL), 0.5 * D_MODEL ** -0.5),
        'b_ada': nrm(ks[5], (L, 6 * D_MODEL), 0.02),
        'attn_norm_w': gain(ks[6], (L, D_MODEL)),
        'w_in': nrm(ks[7], (L, D_MODEL, IN_COLS), D_MODEL ** -0.5),
        'q_norm_w': gain(ks[8], (L, MLA_Q_RANK)),
        'kv_norm_w': gain(ks[9], (L, MLA_KV_RANK)),
        'w_uq': nrm(ks[10], (L, MLA_Q_RANK, MLA_HEADS * (MLA_NOPE + MLA_ROPE)), MLA_Q_RANK ** -0.5),
        'w_ukv': nrm(ks[11], (L, MLA_KV_RANK, MLA_HEADS * (MLA_NOPE + MLA_V)), MLA_KV_RANK ** -0.5),
        'lambda_q1': nrm(ks[12], (L, DIFF_HEAD_DIM), 0.1),
        'lambda_k1': nrm(ks[13], (L, DIFF_HEAD_DIM), 0.1),
        'lambda_q2': nrm(ks[14], (L, DIFF_HEAD_DIM), 0.1),
        'lambda_k2': nrm(ks[15], (L, DIFF_HEAD_DIM), 0.1),
        'subln_w': gain(ks[16], (L, DIFF_V_DIM)),
        'w_out': nrm(ks[17], (L, MIX_WIDTH, D_MODEL), MIX_WIDTH ** -0.5),
        'ffn_norm_w': gain(ks[18], (L, D_MODEL)),
        'router_w': nrm(ks[19], (L, D_MODEL, N_EXPERTS), D_MODEL ** -0.5),
        'router_b': nrm(ks[20], (L, N_EXPERTS), 0.01),
        'w1': nrm(ks[21], (L, N_EXPERTS, D_MODEL, 2 * D_FF), D_MODEL ** -0.5),
        'b1': nrm(ks[22], (L, N_EXPERTS, 2 * D_FF), 0.02),
        'w2': nrm(ks[23], (L, N_EXPERTS, D_FF, D_MODEL), D_FF ** -0.5),
        'b2': nrm(ks[24], (L, N_EXPERTS, D_MODEL), 0.02),
        'final_norm_w': gain(ks[25], (D_MODEL,)),
    }

def first_block(x, c, ctx, c_ctx, w_ada, b_ada, attn_norm_w, w_in, q_norm_w, kv_norm_w, w_uq, w_ukv,
              lambda_q1, lambda_k1, lambda_q2, lambda_k2, subln_w, w_out, ffn_norm_w,
              router_w, router_b, w1, b1, w2, b2, final_norm_w):
    B, n, D = x.shape
    ang = axial_angles(n)
    for l in range(DEPTH):
        last = l == DEPTH - 1
        lam_init = 0.8 - 0.6 * math.exp(-0.3 * l)
        mod_lat = (jax.nn.silu(c) @ w_ada[l] + b_ada[l])[:, None, :]
        mod_ctx = (jax.nn.silu(c_ctx) @ w_ada[l] + b_ada[l])[None, None, :]
        sa, sca, ga, sf, scf, gf = jnp.split(mod_lat, 6, axis=-1)
        csa, csca, cga, csf, cscf, cgf = jnp.split(mod_ctx, 6, axis=-1)
        lam = (jnp.exp(jnp.sum(lambda_q1[l].astype(jnp.float32) * lambda_k1[l].astype(jnp.float32)))
               - jnp.exp(jnp.sum(lambda_q2[l].astype(jnp.float32) * lambda_k2[l].astype(jnp.float32)))
               + lam_init)
        mp = (w_in[l], q_norm_w[l], kv_norm_w[l], w_uq[l], w_ukv[l])

        l_dq, l_dk, l_dv, l_qn, l_qr, l_kn, l_kr, l_v = mixer_inputs(
            modulate(rmsnorm(x, attn_norm_w[l]), sa, sca), *mp, ang)
        c_dq, c_dk, c_dv, c_qn, c_qr, c_kn, c_kr, c_v = mixer_inputs(
            modulate(rmsnorm(ctx, attn_norm_w[l]), csa, csca), *mp, None)
        dk_all = jnp.concatenate([c_dk, l_dk], axis=1)
        dv_all = jnp.concatenate([c_dv, l_dv], axis=1)
        kn_all = jnp.concatenate([c_kn, l_kn], axis=1)
        kr_all = jnp.concatenate([c_kr, l_kr], axis=1)
        v_all = jnp.concatenate([c_v, l_v], axis=1)
        o_diff = from_blocks(lax.map(lambda qb: diff_attend(qb, dk_all, dv_all, lam), to_blocks(l_dq)))
        o_mla = from_blocks(lax.map(lambda qs: mla_attend(qs[0], qs[1], kn_all, kr_all, v_all),
                                    (to_blocks(l_qn), to_blocks(l_qr))))
        x_new = x + ga * merge_heads(o_diff, o_mla, subln_w[l], lam_init, w_out[l])
        if not last:
            oc_diff = diff_attend(c_dq, c_dk, c_dv, lam)
            oc_mla = mla_attend(c_qn, c_qr, c_kn, c_kr, c_v)
            ctx = ctx + cga * merge_heads(oc_diff, oc_mla, subln_w[l], lam_init, w_out[l])
        x = x_new

        hf = modulate(rmsnorm(x, ffn_norm_w[l]), sf, scf)
        x = x + gf * moe(hf.reshape(B * n, D), router_w[l], router_b[l], w1[l], b1[l], w2[l], b2[l]).reshape(B, n, D)
        if not last:
            hc = modulate(rmsnorm(ctx, ffn_norm_w[l]), csf, cscf)
            ctx = ctx + cgf * moe(hc.reshape(-1, D), router_w[l], router_b[l], w1[l], b1[l], w2[l], b2[l]).reshape(ctx.shape)
    return rmsnorm(x, final_norm_w)


PLE_DIM = 256
MIX_WIDTH_2 = D_MODEL
POOL_WIDTH = MIX_WIDTH_2 // 2
POOL_WINDOWS = (2, 4, 8, 16)
N_POOL_GROUPS = len(POOL_WINDOWS)
POOL_GROUP = POOL_WIDTH // N_POOL_GROUPS
HEAD_DIM = 64
ATTN_WIDTH = MIX_WIDTH_2 - POOL_WIDTH
N_Q_HEADS = ATTN_WIDTH // HEAD_DIM
N_KV_HEADS = 2
GQA_GROUP = N_Q_HEADS // N_KV_HEADS
KV_WIDTH = N_KV_HEADS * HEAD_DIM
IN_WIDTH = POOL_WIDTH + ATTN_WIDTH + 2 * KV_WIDTH
WINDOW = 128
BLOCK = 128
D_FF_2 = 4 * D_MODEL
LN_EPS = 1e-5
DEEPNORM_ALPHA = (2 * DEPTH) ** 0.25
DEEPNORM_BETA = (8 * DEPTH) ** -0.25
NEG_INF = -1e30


def layer_norm(x, g, b):
    xf = x.astype(jnp.float32)
    mu = jnp.mean(xf, axis=-1, keepdims=True)
    xc = xf - mu
    var = jnp.mean(xc * xc, axis=-1, keepdims=True)
    y = xc * lax.rsqrt(var + LN_EPS) * g.astype(jnp.float32) + b.astype(jnp.float32)
    return y.astype(x.dtype)

def alibi_slopes(n_heads):
    h = jnp.arange(1, n_heads + 1, dtype=jnp.float32)
    return jnp.exp2(-8.0 * h / n_heads)

def pool_mixer(u, w_pool, pool_scale):
    B, S, _ = u.shape
    uf = u.astype(jnp.float32)
    cs = jnp.pad(jnp.cumsum(uf, axis=1), ((0, 0), (1, 0), (0, 0)))
    t = jnp.arange(S)
    outs = []
    for g, w in enumerate(POOL_WINDOWS):
        sl = slice(g * POOL_GROUP, (g + 1) * POOL_GROUP)
        c = cs[..., sl]
        lo = jnp.maximum(t + 1 - w, 0)
        win_sum = c[:, 1:] - c[:, lo]
        count = (t + 1 - lo).astype(jnp.float32)[None, :, None]
        outs.append(win_sum / count - uf[..., sl])
    d = jnp.stack(outs, axis=2).astype(u.dtype)
    y = jnp.einsum('bsgc,gcd->bsgd', d, w_pool).reshape(B, S, POOL_WIDTH)
    return y * pool_scale

def sliding_window_attention(q, k, v, sinks):
    B, S = q.shape[:2]
    nb = S // BLOCK
    qb = q.reshape(B, nb, BLOCK, N_KV_HEADS, GQA_GROUP, HEAD_DIM)

    def band(a):
        ab = a.reshape(B, nb, BLOCK, N_KV_HEADS, HEAD_DIM)
        prev = jnp.pad(ab, ((0, 0), (1, 0), (0, 0), (0, 0), (0, 0)))[:, :-1]
        return jnp.concatenate([prev, ab], axis=2)

    kb, vb = band(k), band(v)
    scale = 1.0 / math.sqrt(HEAD_DIM)
    scores = jnp.einsum('bnqkgd,bnjkd->bnkgqj', qb, kb).astype(jnp.float32) * scale

    qi = jnp.arange(BLOCK)
    kj = jnp.arange(2 * BLOCK)
    dist = (qi[:, None] + BLOCK - kj[None, :])
    in_band = (dist >= 0) & (dist < WINDOW)
    key_pos = jnp.arange(nb)[:, None] * BLOCK - BLOCK + kj[None, :]
    mask = in_band[None] & (key_pos >= 0)[:, None, :]

    slopes = alibi_slopes(N_Q_HEADS).reshape(N_KV_HEADS, GQA_GROUP)
    bias = -slopes[:, :, None, None] * dist.astype(jnp.float32)[None, None]
    scores = jnp.where(mask[None, :, None, None], scores + bias[None, None], NEG_INF)

    sink = sinks.astype(jnp.float32).reshape(1, 1, N_KV_HEADS, GQA_GROUP, 1, 1)
    m = jnp.maximum(jnp.max(scores, axis=-1, keepdims=True), sink)
    e = jnp.exp(scores - m)
    denom = jnp.sum(e, axis=-1, keepdims=True) + jnp.exp(sink - m)
    probs = (e / denom).astype(v.dtype)
    out = jnp.einsum('bnkgqj,bnjkd->bnqkgd', probs, vb)
    return out.reshape(B, S, ATTN_WIDTH)

def second_inputs(seed: int = 0) -> dict:
    key = jax.random.key(seed)
    ks = jax.random.split(key, 16)
    f32 = jnp.float32

    def nrm(k, shape, std):
        return jax.random.normal(k, shape, f32) * std

    return {
        "x": nrm(ks[0], (BATCH, SEQ, D_MODEL), 1.0),
        "p": nrm(ks[1], (DEPTH, BATCH, SEQ, PLE_DIM), 1.0),
        "w_in": nrm(ks[2], (DEPTH, D_MODEL, IN_WIDTH), D_MODEL ** -0.5),
        "w_pool": nrm(ks[3], (DEPTH, N_POOL_GROUPS, POOL_GROUP, POOL_GROUP), POOL_GROUP ** -0.5),
        "pool_scale": 1.0 + nrm(ks[4], (DEPTH, POOL_WIDTH), 0.1),
        "attn_sinks": nrm(ks[5], (DEPTH, N_Q_HEADS), 0.5),
        "w_out": nrm(ks[6], (DEPTH, MIX_WIDTH_2, D_MODEL), MIX_WIDTH_2 ** -0.5 * DEEPNORM_BETA),
        "ln1_g": 1.0 + nrm(ks[7], (DEPTH, D_MODEL), 0.05),
        "ln1_b": nrm(ks[8], (DEPTH, D_MODEL), 0.02),
        "w_ff1": nrm(ks[9], (DEPTH, D_MODEL, D_FF_2), D_MODEL ** -0.5),
        "w_ff2": nrm(ks[10], (DEPTH, D_FF_2, D_MODEL), D_FF_2 ** -0.5 * DEEPNORM_BETA),
        "ln2_g": 1.0 + nrm(ks[11], (DEPTH, D_MODEL), 0.05),
        "ln2_b": nrm(ks[12], (DEPTH, D_MODEL), 0.02),
        "w_ple": nrm(ks[13], (DEPTH, PLE_DIM, D_MODEL), PLE_DIM ** -0.5),
        "w_ple_gate": nrm(ks[14], (DEPTH, D_MODEL, D_MODEL), D_MODEL ** -0.5),
        "b_ple_gate": nrm(ks[15], (DEPTH, D_MODEL), 0.02),
    }

def second_block(x, p, w_in, w_pool, pool_scale, attn_sinks, w_out, ln1_g, ln1_b,
              w_ff1, w_ff2, ln2_g, ln2_b, w_ple, w_ple_gate, b_ple_gate):
    B, S, _ = x.shape
    h = x
    for i in range(DEPTH):
        z = h @ w_in[i]
        u_pool = z[..., :POOL_WIDTH]
        q = z[..., POOL_WIDTH:POOL_WIDTH + ATTN_WIDTH].reshape(B, S, N_Q_HEADS, HEAD_DIM)
        k = z[..., POOL_WIDTH + ATTN_WIDTH:POOL_WIDTH + ATTN_WIDTH + KV_WIDTH].reshape(B, S, N_KV_HEADS, HEAD_DIM)
        v = z[..., POOL_WIDTH + ATTN_WIDTH + KV_WIDTH:].reshape(B, S, N_KV_HEADS, HEAD_DIM)

        y_pool = pool_mixer(u_pool, w_pool[i], pool_scale[i])
        y_attn = sliding_window_attention(q, k, v, attn_sinks[i])
        mix = jnp.concatenate([y_pool, y_attn], axis=-1) @ w_out[i]
        h = layer_norm(DEEPNORM_ALPHA * h + mix, ln1_g[i], ln1_b[i])

        ff = jnp.square(jax.nn.relu(h @ w_ff1[i])) @ w_ff2[i]
        h = layer_norm(DEEPNORM_ALPHA * h + ff, ln2_g[i], ln2_b[i])

        gate = jax.nn.sigmoid(h @ w_ple_gate[i] + b_ple_gate[i])
        h = h + gate * (p[i] @ w_ple[i])
    return h


def setup_inputs(seed=0):
    out = dict(first_inputs(seed))
    for name, value in second_inputs(seed + 1).items():
        if name != "x":
            out[name + "_2"] = value
    return out


def reference(
    x, c, ctx, c_ctx, w_ada, b_ada, attn_norm_w, w_in, q_norm_w, kv_norm_w, w_uq, w_ukv,
    lambda_q1, lambda_k1, lambda_q2, lambda_k2, subln_w, w_out, ffn_norm_w, router_w, router_b,
    w1, b1, w2, b2, final_norm_w, p_2, w_in_2, w_pool_2, pool_scale_2, attn_sinks_2, w_out_2,
    ln1_g_2, ln1_b_2, w_ff1_2, w_ff2_2, ln2_g_2, ln2_b_2, w_ple_2, w_ple_gate_2, b_ple_gate_2,
):
    x = first_block(
        x, c, ctx, c_ctx, w_ada, b_ada, attn_norm_w, w_in, q_norm_w, kv_norm_w, w_uq, w_ukv,
        lambda_q1, lambda_k1, lambda_q2, lambda_k2, subln_w, w_out, ffn_norm_w, router_w,
        router_b, w1, b1, w2, b2, final_norm_w,
    )
    return second_block(
        x, p_2, w_in_2, w_pool_2, pool_scale_2, attn_sinks_2, w_out_2, ln1_g_2, ln1_b_2,
        w_ff1_2, w_ff2_2, ln2_g_2, ln2_b_2, w_ple_2, w_ple_gate_2, b_ple_gate_2,
    )


_drawn_inputs = setup_inputs


def setup_inputs(seed=0):
    import zlib

    import numpy as np

    out = dict(_drawn_inputs(seed))
    spreads = {}
    factors = {'attn_norm_w': 3.856,
     'q_norm_w': 8.0,
     'kv_norm_w': 8.0,
     'lambda_q1': 4.064,
     'lambda_q2': 64.0,
     'lambda_k2': 3.886,
     'subln_w': 12.773,
     'router_b': 26.702,
     'b1': 28.535,
     'b2': 35.641,
     'attn_sinks_2': 5.295,
     'ln1_b_2': 2.892,
     'ln2_b_2': 3.158,
     'b_ple_gate_2': 8.0,
     'ffn_norm_w': 4.26}
    for name, (base, spread) in spreads.items():
        noise = np.random.default_rng([zlib.crc32(name.encode()), seed]).standard_normal(out[name].shape)
        drawn = base * np.exp(spread * noise) if base else spread * noise
        out[name] = __import__('jax').numpy.asarray(drawn.astype(out[name].dtype))
    for name, factor in factors.items():
        out[name] = (out[name] * factor).astype(out[name].dtype)
    return out
```

```python
from contextlib import ExitStack

import concourse.bass as bass
from concourse import mybir

F32 = mybir.dt.float32
I32 = mybir.dt.int32
U32 = mybir.dt.uint32
ALU = mybir.AluOpType
ACT = mybir.ActivationFunctionType
AX = mybir.AxisListType.X

P = 128
D = 1024
KD = D // P
T = 256
NT = T // P
EPS = 1e-6

H = 4
DQ, DK, DV, CQ, CKV, KR = 0, 512, 1024, 1536, 1792, 1920
IN_COLS = 1984
Q_RANK, KV_RANK, NOPE, ROPE = 256, 128, 128, 64
DIFF_SCALE = 64 ** -0.5
MLA_SCALE = (NOPE + ROPE) ** -0.5
LAM_INIT = 0.8 - 0.6
KEYS = 2 * T

E = 32
TOP_K = 4
FF = 1024
CAP = 64
ROUNDS = T // CAP
LIMIT = 7.0
ALPHA = 1.702

IN2 = 1280
LN_EPS = 1e-5
DEEPNORM = 2.0 ** 0.25
FF2 = 4096
QH, KVH, HD = 8, 2, 64
SLOPES = [2.0 ** (-8.0 * (h + 1) / QH) for h in range(QH)]

SLOTS = 12
SLOT = 2048

ADA0 = [("ada0", k) for k in range(KD)]
W_IN = [("w_in", k) for k in range(KD)]
MLA = [("w_uq", 0), ("w_ukv", 0)]
ADA12 = [(f"ada{t}", k) for t in (1, 2) for k in range(KD)]
W_OUT = [("w_out", j) for j in range(4)]
FRONT = ADA0 + W_IN + MLA + ADA12 + W_OUT
PAIRS = E // 2
PAIR = [("w1", k, i) for k in range(KD) for i in range(2)] + [("w2", j, i) for j in range(4) for i in range(2)]
N_FRONT = len(FRONT)
N_MOE = PAIRS * len(PAIR)
assert len(PAIR) == 2 * SLOTS
BACK = ([("w_in2", k) for k in range(KD)] + [("w_out2", j) for j in range(4)]
        + [("ff1", 0)] + [c for j in range(15) for c in (("ff1", j + 1), ("ff2", j))] + [("ff2", 15)]
        + [("w_ple", 0)] + [("gate", j) for j in range(4)])
CHUNK = {c: n for n, c in enumerate(FRONT)}
CHUNK.update({c: N_FRONT + N_MOE + n for n, c in enumerate(BACK)})

FRONT_TILES = (
    ["smallT", "ada0", "modT"] + [f"hT{k}" for k in range(KD)]
    + [f"proj{t}_{c}" for t in range(4) for c in ((1, 2, 3) if t < 2 else (0, 1, 2, 3))]
    + ["ckvT", "krT", "cqT"] + [f"dkT{h}" for h in range(H)] + ["dqT0", "dqT1"]
    + ["qrope", "qnope0", "qnope1"] + [f"knope{h}" for h in range(H)] + [f"mv{t}" for t in range(4)] + ["qrT"]
)
UNITS = [("d", h, t) for h in range(H) for t in range(NT)] + [("m", h, t) for h in range(H) for t in range(NT)]


def attention_order(n_units):
    order = []
    for i in range(n_units + 2):
        if i < n_units:
            order.append(("score", i))
        if 1 <= i <= n_units:
            order.append(("turn", i - 1))
        if i >= 2:
            order.append(("value", i - 2))
    return order


for _what, _u in attention_order(len(UNITS)):
    if _what == "score":
        FRONT_TILES += [f"s{_u}_{c}" for c in range(2 if UNITS[_u][0] == "d" else 1)]
    else:
        FRONT_TILES.append(f"{'pT' if _what == 'turn' else 'av'}{_u}")
    if _what == "value" and _u == 3:
        FRONT_TILES += ["ada1", "ada2"] + [f"bc{n}" for n in range(8)]
FRONT_TILES += [f"mixT{j}" for j in range(4)] + [f"wo{t}_{n}" for t in range(NT) for n in range(2)]
FRONT_TILES += [f"hfT{j}" for j in range(4)] + ["logits", "rank", "gatesT"]
FRONT_TILES += [f"yb{t}_{n}" for t in range(NT) for n in range(2)]

UNITS2 = [(h, b) for h in range(QH) for b in range(NT)]

BACK_TILES = [f"xT{j}" for j in range(4)] + [f"in{t}_{n}" for t in range(NT) for n in range(3)]
BACK_TILES += ["kT", "qT0", "qT1", "pd0", "pd1", "py0", "py1"]
BACK_TILES += [{"score": "sw", "turn": "tw", "value": "vw"}[w] + str(u) for w, u in attention_order(len(UNITS2))]
BACK_TILES += ["oT0", "oT1"] + [f"wo2{t}_{n}" for t in range(NT) for n in range(2)] + ["plT"]
BACK_TILES += [f"h1T{j}" for j in range(4)]


def place_tiles():
    held, at = [0] * 8, {}

    def put(name, bank):
        at[name] = (bank, held[bank])
        held[bank] += 1

    for part in (FRONT_TILES, BACK_TILES):
        for n, name in enumerate(part):
            put(name, n % 8)
    for n, name in enumerate([f"wide{t}_{c}" for t in range(NT) for c in range(2)]):
        put(name, n)
    for j in range(16):
        put(f"part{j}", 4 + j % 4)
    for n, name in enumerate([f"h2T{j}" for j in range(4)] + [f"ple{t}_{c}" for t in range(NT) for c in range(2)]
                             + [f"gate{t}_{c}" for t in range(NT) for c in range(2)]):
        put(name, (n + 4) % 8)
    return at


GATE_BANKS, UP_BANKS, GATHER_BANKS, OUT_BANKS = (0, 1), (2, 3), (4, 5), (6, 7)
TURN_BANKS, SHARE_BANK, MIX_BANKS = GATE_BANKS, UP_BANKS[0], GATHER_BANKS


def build(nc, a, out):
    with ExitStack() as ctx:
        def sb(name, shape, dt=F32):
            return ctx.enter_context(nc.sbuf_tensor(name, shape, dt))

        sems, count = {}, {}

        def sem(name):
            if name not in sems:
                sems[name] = ctx.enter_context(nc.semaphore(name))
                count[name] = 0
            return sems[name]

        banks = [ctx.enter_context(nc.psum_tensor(f"bank{i}", [P, 512], F32)) for i in range(8)]

        ring = sb("ring", [P, SLOTS, SLOT])
        ident = sb("ident", [P, P])
        ones = sb("ones", [P, P])
        xc = sb("xc", [P, 4, D])
        xn = sb("xn", [P, 4, D])
        hT = sb("hT", [P, KD, KEYS])
        small = sb("small", [32, P])
        csig = sb("csig", [16, P])
        cT = sb("cT", [P, KD, 32])
        vecT = sb("vecT", [P, 16])
        mrows = sb("mrows", [P, 3, 512])
        modT = sb("modT", [P, 2, 16])
        scol = sb("scol", [P, 2, KD])
        lamv = sb("lamv", [P, 4, 64])
        lam = sb("lam", [P, 8])
        rope_cos = sb("rope_cos", [P, NT, 64])
        rope_sin = sb("rope_sin", [P, NT, 32])
        stat = sb("stat", [P, 64])
        sq = sb("sq", [P, D])
        ropet = sq[:].rearrange("p (a c) -> p a c", a=2)
        dq = sb("dq", [P, NT, 512])
        dk = sb("dk", [P, 4, 512])
        dv = sb("dv", [P, 4, 512])
        cq = sb("cq", [P, NT, Q_RANK])
        ckv = sb("ckv", [P, 4, KV_RANK])
        kr = sb("kr", [P, 4, 2, ROPE])
        dkT = xc[:, 0:2, :].rearrange("p a (h k) -> p (a h) k", h=2)
        dqT = sb("dqT", [P, H, T])
        cqT = cq[:]
        ckvT = ckv[:].rearrange("p t c -> p (t c)")
        krT = kr[:].rearrange("p t a c -> p (t a c)")
        qnT = xn[:, 0, :].rearrange("p (h t) -> p h t", h=H)
        qrT = xn[:, 1, 0:512].rearrange("p (j t) -> p j t", j=2)
        qr = xn[:, 1, 512:1024].rearrange("p (t c) -> p t c", t=NT)
        knT = hT[:, 0:4, :]
        mv = hT[:, 4:8, :]
        prob = xn[:, 2:4, :].rearrange("p a (c k) -> p a c k", c=2)
        probT = dq[:]
        psum_sum = sb("psum_sum", [P, len(UNITS), 8])
        o = dk[:].rearrange("p (t a) c -> p t (a c)", t=NT)
        mixT = hT[:, 0:4, :].rearrange("p k (a t) -> p (k a) t", a=2)
        bc = sb("bc", [P, 4, D])

        hf = xn[:, 2:4, :]
        hfT = hT[:, 4:8, :].rearrange("p k (a t) -> p (k a) t", a=2)
        y = hT[:, 0:4, :].rearrange("p (t a) c -> p t (a c)", t=NT)
        rw = xc[:, 1, 0:KD * E].rearrange("p (k e) -> p k e", k=KD)
        rb = sb("rb", [1, E])
        b2 = xc[0:E, 0, :]
        logit = sb("logit", [P, NT, E])
        top = sb("top", [P, NT, 8])
        top_at = sb("top_at", [P, NT, 8], U32)
        top_atf = sb("top_atf", [P, NT, 8])
        topx = sb("topx", [P, NT, 8])
        gate4 = sb("gate4", [P, NT, TOP_K])
        hot = sq[:, 0:NT * TOP_K * E].rearrange("p (t k e) -> p t k e", t=NT, k=TOP_K)
        gates = sb("gates", [P, NT, E + 2])
        chosen = sb("chosen", [P, NT, E])
        slots = sb("slots", [P, NT, E + 2])
        gatesT = sq[0:E, 512:512 + T]
        iota_i = ropet[:, 1, 256:256 + CAP].bitcast(I32)
        iota_e = sb("iota_e", [P, E])
        iota_s = mrows[:, 0, P:P + CAP]
        below = mrows[:, 0, 0:P]
        most = sb("most", [P, 2])
        most_i = sb("most_i", [P, 1], I32)
        sel = xn[:, 0, 768:1024].rearrange("p (t s) -> p t s", t=NT)
        selg = xn[:, 0, 0:256].rearrange("p (t s) -> p t s", t=NT)
        gathered = xn[:, 1, :].rearrange("p (k s) -> p k s", k=KD)
        selgT = xn[:, 0, 512:768]
        b1rows = dv[0:2, :, :].rearrange("p t c -> p (t c)")
        pick = small[0:2, :]
        out2 = o[:, 0, :]
        gs = mrows[:, 1:3, :].rearrange("p a n -> p (a n)")
        us = o[:, 1, :]
        sg = sq[:]
        actT = dq[:].rearrange("p a (j s) -> p (a j) s", j=4)

        final_w, ln1g, ln1b, gf = (bc[:, n, :] for n in range(4))
        ln2g, ln2b = xc[:, 0, :], xc[:, 1, :]
        bands = hT[:, 4:8, :].rearrange("p g (k t) -> p g k t", k=NT)
        w_pool = cq[:].rearrange("p t (g c) -> p (t g) c", g=2)
        p_tok = ckv[:].rearrange("p (t a) c -> p t (a c)", t=NT)
        neg_dist = kr[:, 0:2, :, :].rearrange("p t a c -> p (t a c)")
        sinks = kr[:, 2, 0, 0:QH]
        b_gate = dv[:, 0:2, :].rearrange("p t c -> p (t c)")
        x2 = xc[:, 2:4, :]
        x2T = hf.rearrange("p a (k t) -> p (a k) t", t=T)
        u_tok, q_tok = dk[:, 0:2, :], dk[:, 2:4, :]
        k_tok = dq[:, 0, :].rearrange("p (t h a c) -> p t h a c", t=NT, h=KVH, a=2)
        v_tok = dq[:, 1, 0:2 * KVH * HD].rearrange("p (t c) -> p t c", t=NT)
        pool_dT = xn[:, 0, :].rearrange("p (g t) -> p g t", g=4)
        q2T = xn[:, 1, :].rearrange("p (j t) -> p j t", j=4)
        k2T = sq[:, 0:KVH * T].rearrange("p (h t) -> p h t", h=KVH)
        mix2T = hT[:, 0:4, :].rearrange("p k (a t) -> p (k a) t", a=2)
        prob2 = dv[:, 2, :].rearrange("p (a k) -> p a k", a=2)
        prob2T = dv[:, 3, :].rearrange("p (a k) -> p a k", a=2)
        soft = psum_sum
        o2 = u_tok
        wide = hT[:, 0:4, :]
        pT = sq[:, 512:1024].rearrange("p (k t) -> p k t", k=2)
        bn = sb("bn", [P, NT, 2, 6])
        gate_z = hT[:, 0:4, :]

        tile_at = place_tiles()

        def full(name):
            return sem(f"bank_full{tile_at[name][0]}")

        def drained(name):
            return sem(f"bank_drained{tile_at[name][0]}")

        def use(name):
            return tile_at[name][1]

        def bank(name):
            return banks[tile_at[name][0]]

        def claim(pe, name):
            if use(name):
                pe.wait_ge(drained(name), use(name))
            return bank(name)

        def take(eng, name):
            eng.wait_ge(full(name), use(name) + 1)
            return bank(name)

        def wait_read(eng, name):
            eng.wait_ge(drained(name), use(name) + 1)

        def stepper(eng, link):
            def step(ins, name=None, tile=None, wait=True):
                if tile is not None:
                    s, v = drained(tile), use(tile) + 1
                else:
                    s = sem(name or link)
                    count[name or link] += 1
                    v = count[name or link]
                ins.then_inc(s, 1)
                if wait:
                    eng.wait_ge(s, v)
            return step

        def ring_wait(eng, n):
            eng.wait_ge(sem(f"landed{n % SLOTS}"), 16 * (n // SLOTS + 1))

        def slot(n):
            return ring[:, n % SLOTS, :]

        def source(kind, k, expert=None):
            if kind[:3] == "ada":
                t = int(kind[3])
                return a["w_ada"][0, k * P:(k + 1) * P, t * SLOT:(t + 1) * SLOT], slice(0, SLOT), None
            if kind == "w_in":
                return a["w_in"][0, k * P:(k + 1) * P, :], slice(0, IN_COLS), None
            if kind == "w_uq":
                return a["w_uq"][0].rearrange("(k p) n -> p k n", p=P), slice(0, 2 * 768), 2
            if kind == "w_ukv":
                return a["w_ukv"][0], slice(0, 1024), None
            if kind == "w1":
                return a["w1"][0, expert, k * P:(k + 1) * P, :], slice(0, SLOT), None
            if kind == "w2":
                return (a["w2"][0, expert, k * 2 * P:(k + 1) * 2 * P, :].rearrange("(k p) n -> p k n", p=P),
                        slice(0, SLOT), 2)
            if kind == "w_in2":
                return a["w_in_2"][0, k * P:(k + 1) * P, :], slice(0, IN2), None
            if kind == "ff1":
                return a["w_ff1_2"][0, :, k * 256:(k + 1) * 256].rearrange("(k p) n -> p k n", p=P), slice(0, SLOT), KD
            pairs = {"w_out2": "w_out_2", "ff2": "w_ff2_2", "w_ple": "w_ple_2", "gate": "w_ple_gate_2"}
            if kind in pairs:
                return (a[pairs[kind]][0, k * 2 * P:(k + 1) * 2 * P, :].rearrange("(k p) n -> p k n", p=P),
                        slice(0, SLOT), 2)
            if kind == "w_out":
                return a["w_out"][0, k * 2 * P:(k + 1) * 2 * P, :].rearrange("(k p) n -> p k n", p=P), slice(0, SLOT), 2

        def load_chunk(sp, n, chunk):
            src, cols, parts = source(*chunk)
            dst = slot(n)[:, cols]
            if parts:
                dst = dst.rearrange("p (k n) -> p k n", k=parts)
            if n >= SLOTS:
                sp.wait_ge(sem("ring_freed"), n - SLOTS + 1)
            sp.dma_start(dst, src).then_inc(sem(f"landed{n % SLOTS}"), 16)

        def max_no(u, c):
            return sum(2 if k == "d" else 1 for k, _, _ in UNITS[:u]) + c + 1

        MAIN, OVER = "", "over_"

        def moe(name, which):
            return sem(which + name)

        def mine(i):
            return slice(CAP * i, CAP * i + CAP)

        def freed_by(n, i, which):
            return n * len(PAIR) + ((N_FRONT if which == MAIN else SLOTS) + i + 1)

        def pair_slot(i):
            return (N_FRONT + i) % SLOTS

        def load_most(eng):
            wait_read(eng, "rank")
            return eng.value_load(most_i[0:1, 0:1], min_val=0, max_val=T)

        def pair_loads(sp, n, pair, which):
            for i, (kind, k, second) in enumerate(PAIR):
                src, cols, parts = source(kind, k, pair * 2 + second)
                s = pair_slot(i)
                dst = ring[:, s, cols]
                if parts:
                    dst = dst.rearrange("p (k n) -> p k n", k=parts)
                sp.wait_ge(moe("ring_freed", which),
                           n * len(PAIR) + ((N_FRONT if which == MAIN else SLOTS) + i + 1 - SLOTS))
                sp.dma_start(dst, src).then_inc(moe(f"landed{s}", which), 16)

        def sp_overflow(sp):
            count_ = load_most(sp)
            for r in range(1, ROUNDS):
                with sp.If(count_ > r * CAP):
                    sp.wait_ge(sem("ring_freed"), N_FRONT + N_MOE)
                    with sp.Fori(0, PAIRS) as pair:
                        pair_loads(sp, pair + (r - 1) * PAIRS, pair, OVER)
                    sp.wait_ge(moe("ring_freed", OVER), SLOTS + r * N_MOE)
            return count_

        def pair_landed(pe, n, i, which):
            before = (N_FRONT + i) // SLOTS if which == MAIN else i // SLOTS
            pe.wait_ge(moe(f"landed{pair_slot(i)}", which), (n * 2 + (before + 1)) * 16)

        def gather(pe, n, which, y_read):
            pe.wait_ge(moe("sel_ready", which), n + 1)
            if y_read is not None:
                pe.wait_ge(moe("y_added", which), y_read)
            for k in range(KD):
                for t in range(NT):
                    m = pe.matmul(banks[GATHER_BANKS[k // 4]][:, k % 4 * P:(k % 4 + 1) * P], hf[:, t, k * P:(k + 1) * P],
                                  sel[:, t, :], start=t == 0, stop=t == 1, skip_group_check=True)
            m.then_inc(moe("xt_full", which), 1)

        def hidden(pe, n, which):
            pe.wait_ge(moe("xt_read", which), n + 1)
            for k in range(KD):
                for i in range(2):
                    pair_landed(pe, n, 2 * k + i, which)
                for q, bank_no in enumerate(GATE_BANKS + UP_BANKS):
                    for i in range(2):
                        m = pe.matmul(banks[bank_no][mine(i), :], gathered[:, k, mine(i)],
                                      ring[:, pair_slot(2 * k + i), q * 512:(q + 1) * 512],
                                      start=k == 0, stop=k == KD - 1, skip_group_check=True)
                    if k == KD - 1 and q == 1:
                        m.then_inc(moe("gate_full", which), 1)
                m.then_inc(moe("ring_freed", which), 2)
                if k == 5:
                    pe.wait_ge(moe("b1_in", which), (n + 1) * 16)
                    for q, bank_no in enumerate(GATE_BANKS + UP_BANKS):
                        m = pe.matmul(banks[bank_no][:], pick, b1rows[:, q * 512:(q + 1) * 512],
                                      start=False, stop=False, skip_group_check=True)

        def pe_rest(pe, n, which, ahead):
            for half in range(2):
                pe.wait_ge(moe("gated", which), n * 2 + (half + 1))
                for j in range(4):
                    m = pe.transpose(banks[TURN_BANKS[half]][:, j * P:(j + 1) * P],
                                     us[:, half * 512 + j * P:half * 512 + (j + 1) * P], ident[:])
                m.then_inc(moe("turned", which), 1)
                if half == 0:
                    pe.wait_ge(moe("selg_ready", which), n + 1)
                    for t in range(NT):
                        m = pe.transpose(banks[SHARE_BANK][:, t * P:(t + 1) * P], selg[:, t, :], ident[:])
                    m.then_inc(moe("share_full", which), 1)
            for j in range(4):
                if j % 2 == 0:
                    pe.wait_ge(moe("act_read", which), n * 2 + (j // 2 + 1))
                for i in range(2):
                    pair_landed(pe, n, 2 * KD + 2 * j + i, which)
                for c in range(2):
                    for kk in range(2):
                        for i in range(2):
                            w = ring[:, pair_slot(2 * KD + 2 * j + i), :].rearrange("p (k n) -> p k n", k=2)
                            k = 2 * j + kk
                            m = pe.matmul(banks[OUT_BANKS[c]][mine(i), :], actT[:, k, mine(i)],
                                          w[:, kk, c * 512:(c + 1) * 512],
                                          start=k == 0, stop=k == KD - 1, skip_group_check=True)
                    if j == 3 and c == 0:
                        m.then_inc(moe("out_half", which), 1)
                m.then_inc(moe("ring_freed", which), 2)
            pe.wait_ge(moe("share_read", which), n + 1)
            pe.wait_ge(moe("xt_read", which), n + (1 + ahead))
            for q in range(4):
                t, c = divmod(q, 2)
                if q < 2:
                    pe.wait_ge(moe("out_read", which), n * 2 + (c + 1))
                else:
                    pe.wait_ge(moe("y_added", which), n * 4 + q)
                pe.matmul(banks[MIX_BANKS[c]][:], selgT[:, t * P:(t + 1) * P], out2[:, c * 512:(c + 1) * 512],
                          start=True, stop=True, skip_group_check=True).then_inc(moe("mixed", which), 1)

        def load_b1(act, n, pair, which):
            act.dma_start(b1rows, a["b1"][0, bass.ds(pair * 2, 2), :]).then_inc(moe("b1_in", which), 16)

        def gather_out(act, n, which):
            act.wait_ge(moe("xt_full", which), n + 1)
            for j in range(2):
                m = act.activation(gathered[:, 4 * j:4 * j + 4, :],
                                   banks[GATHER_BANKS[j]][:].rearrange("p (k s) -> p k s", k=4), ACT.Copy)
            m.then_inc(moe("xt_read", which), 1)

        def sigmoids(act, n, which):
            for half in range(2):
                cols = slice(half * 512, half * 512 + 512)
                act.wait_ge(moe("gate_clipped", which), n * 2 + (half + 1))
                act.activation(sg[:, cols], gs[:, cols], ACT.Sigmoid, scale=ALPHA).then_inc(moe("sigmoid", which), 1)

        def act_rest(act, n, which):
            for half in range(2):
                act.wait_ge(moe("turned", which), n * 2 + (half + 1))
                act.activation(actT[:, 4 * half:4 * half + 4, :],
                               banks[TURN_BANKS[half]][:].rearrange("p (j s) -> p j s", j=4), ACT.Copy)\
                    .then_inc(moe("act_read", which), 1)
            act.wait_ge(moe("share_full", which), n + 1)
            act.activation(selgT, banks[SHARE_BANK][:, 0:T], ACT.Copy).then_inc(moe("share_read", which), 1)
            for c in range(2):
                if c == 0:
                    act.wait_ge(moe("out_half", which), n + 1)
                else:
                    act.wait_ge(moe("ring_freed", which), freed_by(n, len(PAIR) - 1, which))
                act.activation(out2[:, c * 512:(c + 1) * 512], banks[OUT_BANKS[c]][:], ACT.Copy)\
                    .then_inc(moe("out_read", which), 1)

        def select(dve, n, pair, which):
            for t in range(NT):
                for i in range(2):
                    m = dve.tensor_scalar(sel[:, t, mine(i)], iota_s, slots[:, t, bass.ds(pair * 2 + i, 1)], None,
                                          ALU.is_equal)
            m.then_inc(moe("sel_ready", which), 1)

        def dve_pair(dve, n, pair, which):
            for t in range(NT):
                for i in range(2):
                    m = dve.tensor_scalar(selg[:, t, mine(i)], iota_s, slots[:, t, bass.ds(pair * 2 + i, 1)],
                                          gates[:, t, bass.ds(pair * 2 + i, 1)], ALU.is_equal, ALU.mult)
            m.then_inc(moe("selg_ready", which), 1)
            dve.wait_ge(moe("gate_full", which), n + 1)
            for half in range(2):
                dve.tensor_scalar(gs[:, half * 512:half * 512 + 512], banks[GATE_BANKS[half]][:], LIMIT, None, ALU.min)\
                    .then_inc(moe("gate_clipped", which), 1)
            dve.wait_ge(moe("ring_freed", which), freed_by(n, 2 * KD - 1, which))
            for half in range(2):
                cols = slice(half * 512, half * 512 + 512)
                dve.tensor_scalar(us[:, cols], banks[UP_BANKS[half]][:], LIMIT, -LIMIT, ALU.min, ALU.max)\
                    .then_inc(moe("up_clipped", which), 1)
            for half in range(2):
                cols = slice(half * 512, half * 512 + 512)
                dve.wait_ge(moe("gate_clipped", which), n * 2 + (half + 1))
                dve.wait_ge(moe("up_clipped", which), n * 2 + (half + 1))
                dve.scalar_tensor_tensor(out=us[:, cols], in0=us[:, cols], scalar=1.0, in1=gs[:, cols],
                                         op0=ALU.add, op1=ALU.mult).then_inc(moe("up_gate", which), 1)
                dve.wait_ge(moe("up_gate", which), n * 2 + (half + 1))
                dve.wait_ge(moe("sigmoid", which), n * 2 + (half + 1))
                dve.tensor_tensor(us[:, cols], us[:, cols], sg[:, cols], ALU.mult).then_inc(moe("gated", which), 1)
            for q in range(4):
                t, c = divmod(q, 2)
                dve.wait_ge(moe("mixed", which), n * 4 + (q + 1))
                cols = slice(c * 512, c * 512 + 512)
                dve.tensor_tensor(y[:, t, cols], y[:, t, cols], banks[MIX_BANKS[c]][:], ALU.add)\
                    .then_inc(moe("y_added", which), 1)

        block = ctx.enter_context(nc.Block())

        @block.sync
        def _(sp):
            for n, chunk in enumerate(FRONT):
                load_chunk(sp, n, chunk)
            with sp.Fori(0, PAIRS) as pair:
                pair_loads(sp, pair, pair, MAIN)
            sp_overflow(sp)
            for chunk in BACK:
                load_chunk(sp, CHUNK[chunk], chunk)
            for t in range(NT):
                for c in range(2):
                    sp.wait_ge(sem("out_done"), 2 * t + c + 1)
                    sp.dma_start(out[0, t * P:(t + 1) * P, c * 512:(c + 1) * 512], x2[:, t, c * 512:(c + 1) * 512])\
                        .then_inc(sem("stored"), 16)
            sp.wait_ge(sem("stored"), 64)

        @block.gpsimd
        def _(pool):
            step = stepper(pool, "pool_link")
            step(pool.memset(ident[:], 0.0))
            step(pool.affine_select(out=ident[:], in_=ident[:], compare_op=ALU.not_equal, fill=1.0, base=0,
                                    pattern=[[-1, P]], channel_multiplier=1), "consts")
            step(pool.memset(ones[:], 1.0), "consts")
            step(pool.memset(cT[:], 0.0), "consts")
            step(pool.memset(mrows[:], 0.0), "consts")
            for t in range(3):
                for i in range(2):
                    src = a["b_ada"][0, t * SLOT:(t + 1) * SLOT].rearrange("(q n) -> q n", q=4)
                    pool.dma_start(mrows[i:97 + i:32, t, :], src).then_inc(sem("bada_in"), 16)
            pool.dma_start(rb[:], a["router_b"]).then_inc(sem("router_in"), 16)
            pool.wait_ge(sem("x1_done"), 4)
            step(pool.memset(below, 1.0))
            step(pool.affine_select(out=below, in_=below, compare_op=ALU.is_gt, fill=0.0, base=0,
                                    pattern=[[1, P]], channel_multiplier=-1), "below_done")
            step(pool.iota(iota_i, pattern=[[1, CAP]], base=0, channel_multiplier=0), "iota_done")
            step(pool.memset(pick, 1.0))
            step(pool.affine_select(out=pick, in_=pick, compare_op=ALU.is_gt, fill=0.0, base=1,
                                    pattern=[[1, P]], channel_multiplier=-CAP))
            step(pool.affine_select(out=pick, in_=pick, compare_op=ALU.is_gt, fill=0.0, base=CAP,
                                    pattern=[[-1, P]], channel_multiplier=CAP), "pick_done")
            wait_read(pool, "mixT0")
            pool.dma_start(rw, a["router_w"][0].rearrange("(k p) e -> p k e", p=P)).then_inc(sem("router_in"), 16)
            pool.dma_start(b2, a["b2"][0]).then_inc(sem("b2_in"), 16)
            pool.wait_ge(sem("hf_done"), NT)
            for dst, name in ((final_w, "final_norm_w"), (ln1g, "ln1_g_2"), (ln1b, "ln1_b_2")):
                src = a[name] if name != "final_norm_w" else a[name].rearrange("(a n) -> a n", a=1)
                pool.dma_start(dst, src.broadcast_to([P, D])).then_inc(sem("norm_in"), 16)
            pool.dma_start(w_pool, a["w_pool_2"][0].rearrange("g c d -> c g d")).then_inc(sem("mix_in"), 16)
            pool.dma_start(p_tok, a["p_2"][0, 0].rearrange("(t p) c -> p t c", p=P)).then_inc(sem("mix_in"), 16)
            pool.dma_start(neg_dist, a["neg_dist"]).then_inc(sem("mix_in"), 16)
            pool.dma_start(sinks, a["attn_sinks_2"].broadcast_to([P, QH])).then_inc(sem("mix_in"), 16)
            wait_read(pool, "logits")
            pool.dma_start(bands, a["pool_bands"].rearrange("g (k p) t -> p g k t", p=P)).then_inc(sem("mix_in"), 16)
            wait_read(pool, "yb1_1")
            pool.dma_start(ln2g, a["ln2_g_2"].broadcast_to([P, D])).then_inc(sem("norm2_in"), 16)
            pool.dma_start(ln2b, a["ln2_b_2"].broadcast_to([P, D])).then_inc(sem("norm2_in"), 16)
            pool.wait_ge(sem("moe_done"), 1)
            pool.dma_start(b_gate, a["b_ple_gate_2"].broadcast_to([P, D])).then_inc(sem("b_gate_in"), 16)

        @block.scalar
        def _(act):
            step = stepper(act, "act_link")

            def load(dst, src, name, inc=16):
                act.dma_start(dst, src).then_inc(sem(name), 16)

            load(small[0:8, :], a["c"][0].rearrange("(r n) -> r n", n=P), "c_in")
            load(small[8:16, :], a["c_ctx"].rearrange("(r n) -> r n", n=P), "c_in")
            load(small[16:24, :], a["attn_norm_w"][0].rearrange("(r n) -> r n", n=P), "c_in")
            load(small[24:26, :], a["q_norm_w"][0].rearrange("(r n) -> r n", n=P), "c_in")
            load(small[26:27, :], a["kv_norm_w"][0].rearrange("(r n) -> r n", n=P), "c_in")
            load(small[27:28, :], a["subln_w"][0].rearrange("(r n) -> r n", n=P), "c_in")
            load(small[28:32, :], a["pool_scale_2"][0].rearrange("(r n) -> r n", n=P), "c_in")
            load(xc[:, 0:2, :], a["ctx"][0].rearrange("(t p) d -> p t d", p=P), "ctx_in")
            load(xc[:, 2:4, :], a["x"][0].rearrange("(t p) d -> p t d", p=P), "x_in")
            for n, name in enumerate(("lambda_q1", "lambda_k1", "lambda_q2", "lambda_k2")):
                load(lamv[:, n, :], a[name].broadcast_to([P, 64]), "lam_in")
            load(rope_cos[:], a["rope_cos"].rearrange("(t p) c -> p t c", p=P), "rope_in")
            load(rope_sin[:], a["rope_sin"].rearrange("(t p) c -> p t c", p=P), "rope_in")
            load(bc[:, 2, :], a["ffn_norm_w"].broadcast_to([P, D]), "ffnw_in")

            act.wait_ge(sem("c_in"), 16 * 7)
            step(act.activation(csig[:], small[0:16, :], ACT.Sigmoid), "csig_done")
            act.wait_ge(sem("ctx_in"), 16)
            for t in range(4):
                if t == 2:
                    act.wait_ge(sem("x_in"), 16)
                step(act.activation(sq[:], xc[:, t, :], ACT.Square, accum_out=stat[:, t:t + 1]), "ss_done")
            act.wait_ge(sem("ms_done"), 1)
            step(act.activation(stat[:, 8:12], stat[:, 4:8], ACT.Sqrt), "root_done")
            act.wait_ge(sem("lam_sums"), 1)
            step(act.activation(lam[:, 2:4], lam[:, 0:2], ACT.Exp), "lam_exp")

            for t in range(4):
                for c in ((1, 2, 3) if t < 2 else (0, 1, 2, 3)):
                    if c == 2:
                        step(act.activation(dv[:, t, :], take(act, f"proj{t}_2")[:], ACT.Copy), tile=f"proj{t}_2")
                    elif c == 1 and t < 2:
                        step(act.activation(dk[:, t, :], take(act, f"proj{t}_1")[:], ACT.Copy), tile=f"proj{t}_1")
            act.wait_ge(sem("lat_ms"), 1)
            step(act.activation(stat[:, 24:30], stat[:, 18:24], ACT.Sqrt), "lat_root")
            for h in range(H):
                b = take(act, f"dkT{h}")
                step(act.activation(dkT[:, h, :], b[:], ACT.Copy), tile=f"dkT{h}")
            for j in range(2):
                b = take(act, f"dqT{j}")
                step(act.activation(dqT[:, 2 * j:2 * j + 2, :], b[:].rearrange("p (h t) -> p h t", h=2),
                                    ACT.Copy, scale=DIFF_SCALE), tile=f"dqT{j}")
            for j in range(2):
                b = take(act, f"qnope{j}")
                if j == 0:
                    act.wait_ge(sem("hT_done"), KD)
                    act.wait_ge(full("hT7"), use("hT7") + 1)
                step(act.activation(qnT[:, 2 * j:2 * j + 2, :], b[:].rearrange("p (h t) -> p h t", h=2),
                                    ACT.Copy, scale=MLA_SCALE), tile=f"qnope{j}")
            act.wait_ge(full("proj3_3"), use("proj3_3") + 1)
            for h in range(H):
                b = take(act, f"knope{h}")
                step(act.activation(knT[:, h, :], b[:], ACT.Copy), tile=f"knope{h}")

            for what, u in attention_order(len(UNITS)):
                kind, h, t = UNITS[u]
                if what == "score":
                    for c in range(2 if kind == "d" else 1):
                        b = take(act, f"s{u}_{c}")
                        act.wait_ge(sem("neg_max"), max_no(u, c))
                        if u >= 2 and c == 0:
                            act.wait_ge(full(f"pT{u - 2}"), use(f"pT{u - 2}") + 1)
                        step(act.activation(prob[:, u % 2, c, :], b[:], ACT.Exp, bias=psum_sum[:, u, c:c + 1],
                                            accum_out=psum_sum[:, u, 2 + c:3 + c]), tile=f"s{u}_{c}")
                elif what == "turn":
                    b = take(act, f"pT{u}")
                    if u >= 2:
                        act.wait_ge(full(f"av{u - 2}"), use(f"av{u - 2}") + 1)
                    step(act.activation(probT[:, u % 2, :], b[:], ACT.Copy), tile=f"pT{u}")
            act.wait_ge(sem("sub_ms"), 1)
            step(act.activation(stat[:, 48:56], stat[:, 40:48], ACT.Sqrt), "sub_root")
            for j in (2, 3):
                b = take(act, f"mixT{j}")
                step(act.activation(mixT[:, 2 * j:2 * j + 2, :], b[:].rearrange("p (k t) -> p k t", k=2), ACT.Copy),
                     tile=f"mixT{j}")
            for t in range(NT):
                act.wait_ge(sem("x1_done"), 2 * t + 2)
                step(act.activation(xn[:, 0, :], xc[:, 2 + t, :], ACT.Square, accum_out=stat[:, t:t + 1]), "ss2_done")
            act.wait_ge(sem("ms2_done"), 1)
            step(act.activation(stat[:, 4:6], stat[:, 2:4], ACT.Sqrt), "root2_done")
            for j in range(4):
                b = take(act, f"hfT{j}")
                step(act.activation(hfT[:, 2 * j:2 * j + 2, :], b[:].rearrange("p (k t) -> p k t", k=2), ACT.Copy),
                     tile=f"hfT{j}")
            for t in range(NT):
                act.wait_ge(sem("top_done"), t + 1)
                step(act.activation(topx[:, t, 4:8], top[:, t, 0:TOP_K], ACT.Exp, bias=topx[:, t, 0:1],
                                    accum_out=topx[:, t, 1:2]), "topx_done")

            gather_out(act, 0, MAIN)
            with act.Fori(0, PAIRS) as pair:
                load_b1(act, pair, pair, MAIN)
                sigmoids(act, pair, MAIN)
                gather_out(act, pair + 1, MAIN)
                act_rest(act, pair, MAIN)
            most_act = load_most(act)
            with act.Fori(1, ROUNDS) as r:
                with act.If(most_act > r * CAP):
                    with act.Fori(0, PAIRS) as pair:
                        n = (r - 1) * PAIRS + pair
                        load_b1(act, n, pair, OVER)
                        gather_out(act, n, OVER)
                        sigmoids(act, n, OVER)
                        act_rest(act, n, OVER)

            for t in range(NT):
                act.wait_ge(sem("x_moe"), t + 1)
                if t == 0:
                    act.wait_ge(sem("moe_used"), 1)
                step(act.activation(xn[:, 0, :], x2[:, t, :], ACT.Square, accum_out=stat[:, t:t + 1]), "ss3_done")
            act.wait_ge(sem("ms3_done"), 1)
            step(act.activation(stat[:, 4:6], stat[:, 2:4], ACT.Sqrt), "root3_done")

            def transposed(name, dst, k, scale=1.0):
                b = take(act, name)
                step(act.activation(dst, b[:].rearrange("p (k t) -> p k t", k=k), ACT.Copy, scale=scale), tile=name)

            for j in range(4):
                transposed(f"xT{j}", x2T[:, 2 * j:2 * j + 2, :], 2)
            for t in range(NT):
                b = take(act, f"in{t}_0")
                step(act.activation(u_tok[:, t, :], b[:], ACT.Copy), tile=f"in{t}_0")
                b = take(act, f"in{t}_1")
                step(act.activation(q_tok[:, t, :], b[:], ACT.Copy), tile=f"in{t}_1")
            transposed("kT", k2T, 2)
            transposed("qT0", q2T[:, 0:2, :], 2, HD ** -0.5)
            transposed("qT1", q2T[:, 2:4, :], 2, HD ** -0.5)
            transposed("pd0", pool_dT[:, 0:2, :], 2)
            transposed("pd1", pool_dT[:, 2:4, :], 2)
            for what, u in attention_order(len(UNITS2)):
                h, blk = UNITS2[u]
                w = (blk + 1) * P
                if what == "score":
                    act.wait_ge(sem("masked"), u + 1)
                    step(act.activation(prob2[:, u % 2, 0:w], prob2[:, u % 2, 0:w], ACT.Exp, bias=soft[:, u, 1:2],
                                        accum_out=soft[:, u, 2:3]))
                    step(act.activation(soft[:, u, 3:4], sinks[:, h:h + 1], ACT.Exp, bias=soft[:, u, 1:2]), "exp2_done")
                elif what == "turn":
                    b = take(act, f"tw{u}")
                    step(act.activation(prob2T[:, u % 2, 0:w], b[:, 0:w], ACT.Copy), tile=f"tw{u}")
            transposed("oT0", mix2T[:, 4:6, :], 2)
            transposed("oT1", mix2T[:, 6:8, :], 2)
            transposed("plT", pT, 2)
            for t in range(NT):
                act.wait_ge(sem("var1"), t + 1)
                step(act.activation(stat[:, 16 + t:17 + t], stat[:, 12 + t:13 + t], ACT.Sqrt), "root4_done")
            for j in range(4):
                transposed(f"h1T{j}", x2T[:, 2 * j:2 * j + 2, :], 2)
            for j in range(16):
                b = take(act, f"part{j}")
                if j >= 4:
                    act.wait_ge(sem("wide_used"), j - 3)
                step(act.activation(wide[:, j % 4, :], b[:], ACT.Relu), tile=f"part{j}")
            for t in range(NT):
                act.wait_ge(sem("var2"), t + 1)
                step(act.activation(stat[:, 26 + t:27 + t], stat[:, 22 + t:23 + t], ACT.Sqrt), "root5_done")
            for j in range(4):
                transposed(f"h2T{j}", x2T[:, 2 * j:2 * j + 2, :], 2)
            for n in range(4):
                act.wait_ge(sem("gate_in"), n + 1)
                step(act.activation(gate_z[:, n, :], gate_z[:, n, :], ACT.Sigmoid), "gate_done")

        @block.vector
        def _(dve):
            step = stepper(dve, "dve_link")
            V = nc.vector

            dve.wait_ge(sem("csig_done"), 1)
            step(V.tensor_tensor(small[0:16, :], small[0:16, :], csig[:], ALU.mult), "silu_done")
            b = take(dve, "smallT")
            dve.wait_ge(sem("consts"), 3)
            step(V.tensor_copy(cT[:, :, 0:2], b[:, 0:16].rearrange("p (i k) -> p k i", i=2)))
            step(V.tensor_copy(vecT[:], b[:, 16:32]), tile="smallT")

            dve.wait_ge(sem("ss_done"), 4)
            step(V.tensor_scalar(stat[:, 4:8], stat[:, 0:4], 1.0 / D, EPS, ALU.mult, ALU.add), "ms_done")
            dve.wait_ge(sem("lam_in"), 64)
            for n in range(2):
                step(V.tensor_tensor_reduce(lamv[:, 2 * n, :], lamv[:, 2 * n, :], lamv[:, 2 * n + 1, :], 1.0, 0.0,
                                            ALU.mult, ALU.add, lam[:, n:n + 1]), "lam_sums" if n else None)
            dve.wait_ge(sem("root_done"), 1)
            step(V.reciprocal(stat[:, 12:16], stat[:, 8:12]))
            for t in range(4):
                step(V.tensor_scalar(xn[:, t, :], xc[:, t, :], stat[:, 12 + t:13 + t], None, ALU.mult), "xn_done",
                     wait=t == 3)
            dve.wait_ge(sem("lam_exp"), 1)
            step(V.tensor_tensor(lam[:, 4:5], lam[:, 3:4], lam[:, 2:3], ALU.subtract))
            step(V.tensor_scalar(lam[:, 5:6], lam[:, 4:5], -LAM_INIT, None, ALU.add))

            b = take(dve, "ada0")
            dve.wait_ge(sem("bada_in"), 96)
            step(V.tensor_tensor(mrows[:, 0, :], b[:], mrows[:, 0, :], ALU.add), tile="ada0")
            b = take(dve, "modT")[:].rearrange("p (b q r) -> p r q b", b=4, q=4)
            for i in range(2):
                step(V.tensor_copy(modT[:, i, :].rearrange("p (q b) -> p q b", q=4), b[:, i]),
                     tile="modT" if i else None)
            for i in range(2):
                step(V.scalar_tensor_tensor(out=scol[:, i, :], in0=modT[:, i, 8:16], scalar=1.0, in1=vecT[:, 0:8],
                                            op0=ALU.add, op1=ALU.mult))
            for k in range(KD):
                b = take(dve, f"hT{k}")
                step(V.tensor_scalar(hT[:, k, 0:T], b[:, 0:T], scol[:, 1, k:k + 1], modT[:, 1, k:k + 1],
                                     ALU.mult, ALU.add), "hT_done", wait=False)
                step(V.tensor_scalar(hT[:, k, T:KEYS], b[:, T:KEYS], scol[:, 0, k:k + 1], modT[:, 0, k:k + 1],
                                     ALU.mult, ALU.add), tile=f"hT{k}")

            def rotate(dst, src, t, n, last):
                w = n * 64
                cos = rope_cos[:, t, :].unsqueeze(1).broadcast_to([P, n, 64])
                step(V.tensor_tensor(ropet[:, 0, 0:w].rearrange("p (n c) -> p n c", n=n),
                                     src.rearrange("p (n c) -> p n c", n=n), cos, ALU.mult))
                s = src.rearrange("p (n f c) -> p n f c", f=2, c=16)
                r = ropet[:, 1, 0:w].rearrange("p (n f c) -> p n f c", f=2, c=16)
                for half in range(2):
                    for axis in range(2):
                        sin = rope_sin[:, t, axis * 16:axis * 16 + 16].unsqueeze(1).broadcast_to([P, n, 16])
                        step(V.tensor_tensor(r[:, axis::2, half, :], s[:, axis::2, 1 - half, :], sin, ALU.mult),
                             wait=half == 1 and axis == 1)
                o0 = ropet[:, 0, 0:w].rearrange("p (n f c) -> p n f c", f=2, c=16)
                d = dst.rearrange("p (n f c) -> p n f c", f=2, c=16)
                step(V.tensor_tensor(d[:, :, 0, :], o0[:, :, 0, :], r[:, :, 0, :], ALU.subtract))
                step(V.tensor_tensor(d[:, :, 1, :], o0[:, :, 1, :], r[:, :, 1, :], ALU.add), **last)

            dve.wait_ge(sem("rope_in"), 32)
            for t in range(4):
                for c in ((1, 3) if t < 2 else (0, 1, 3)):
                    name = f"proj{t}_{c}"
                    b = take(dve, name)
                    if c == 3:
                        at = 0 if t < 2 else Q_RANK
                        if t >= 2:
                            step(V.tensor_copy(cq[:, t - 2, :], b[:, 0:Q_RANK]))
                        step(V.tensor_copy(ckv[:, t, :], b[:, at:at + KV_RANK]))
                        krs = b[:, at + KV_RANK:at + KV_RANK + ROPE]
                        if t < 2:
                            step(V.tensor_copy(kr[:, t, 0, :], krs), tile=name)
                        else:
                            rotate(kr[:, t, 0, :], krs, t - 2, 1, {"tile": name})
                        step(V.tensor_copy(kr[:, t, 1, :], kr[:, t, 0, :]), "kr_done")
                    elif t >= 2:
                        rotate((dq[:, t - 2, :] if c == 0 else dk[:, t, :]), b[:], t - 2, 8, {"tile": name})
            for t in range(4):
                step(V.tensor_tensor_reduce(sq[:, 0:KV_RANK], ckv[:, t, :], ckv[:, t, :], 1.0, 0.0, ALU.mult, ALU.add,
                                            stat[:, 12 + t:13 + t]))
            for t in range(2):
                step(V.tensor_tensor_reduce(sq[:, 0:Q_RANK], cq[:, t, :], cq[:, t, :], 1.0, 0.0, ALU.mult, ALU.add,
                                            stat[:, 16 + t:17 + t]))
            step(V.tensor_scalar(stat[:, 18:22], stat[:, 12:16], 1.0 / KV_RANK, EPS, ALU.mult, ALU.add))
            step(V.tensor_scalar(stat[:, 22:24], stat[:, 16:18], 1.0 / Q_RANK, EPS, ALU.mult, ALU.add), "lat_ms")
            dve.wait_ge(sem("lat_root"), 1)
            step(V.reciprocal(stat[:, 30:36], stat[:, 24:30]))
            for t in range(4):
                step(V.tensor_scalar(ckv[:, t, :], ckv[:, t, :], stat[:, 30 + t:31 + t], None, ALU.mult), "lat_done")
            for t in range(2):
                step(V.tensor_scalar(cq[:, t, :], cq[:, t, :], stat[:, 34 + t:35 + t], None, ALU.mult), "lat_done")
            b = take(dve, "ckvT")
            step(V.tensor_scalar(ckvT, b[:], vecT[:, 10:11], None, ALU.mult), tile="ckvT")
            b = take(dve, "krT")
            step(V.tensor_copy(krT, b[:]), tile="krT")
            b = take(dve, "cqT")
            for k in range(2):
                step(V.tensor_scalar(cqT[:, k, :], b[:, k * T:(k + 1) * T], vecT[:, 8 + k:9 + k], None, ALU.mult),
                     tile="cqT" if k else None)
            b = take(dve, "qrope")
            for t in range(NT):
                rotate(qr[:, t, :], b[:, t * 256:(t + 1) * 256], t, H, {"tile": "qrope"} if t else {})
            for t in range(4):
                b = take(dve, f"mv{t}")
                step(V.tensor_copy(mv[:, t, :], b[:]), tile=f"mv{t}")
            b = take(dve, "qrT")
            step(V.tensor_scalar(qrT, b[:].rearrange("p (j t) -> p j t", j=2), MLA_SCALE, None, ALU.mult), tile="qrT")

            for what, u in attention_order(len(UNITS)):
                kind, h, t = UNITS[u]
                if what == "score":
                    for c in range(2 if kind == "d" else 1):
                        b = take(dve, f"s{u}_{c}")
                        step(V.tensor_reduce(psum_sum[:, u, c:c + 1], b[:], AX, ALU.max, negate=True), "neg_max")
                elif what == "turn":
                    continue
                else:
                    b = take(dve, f"av{u}")
                    at = h * P + (0 if kind == "d" else 512)
                    step(V.tensor_scalar(o[:, t, at:at + P], b[:, 0:P], psum_sum[:, u, 4:5], None, ALU.mult),
                         tile=f"av{u}")
                if what == "score":
                    last = f"s{u}_1" if kind == "d" else f"s{u}_0"
                    wait_read(dve, f"s{u}_0")
                    wait_read(dve, last)
                    step(V.reciprocal(psum_sum[:, u, 4:6] if kind == "d" else psum_sum[:, u, 4:5],
                                      psum_sum[:, u, 2:4] if kind == "d" else psum_sum[:, u, 2:3]),
                         "pmix_done" if kind == "m" else None)
                    if kind == "d":
                        step(V.scalar_tensor_tensor(out=psum_sum[:, u, 6:7], in0=psum_sum[:, u, 5:6],
                                                    scalar=psum_sum[:, u, 2:3], in1=lam[:, 5:6],
                                                    op0=ALU.mult, op1=ALU.mult))
                        step(V.scalar_tensor_tensor(out=prob[:, u % 2, 0, :], in0=prob[:, u % 2, 1, :],
                                                    scalar=psum_sum[:, u, 6:7], in1=prob[:, u % 2, 0, :],
                                                    op0=ALU.mult, op1=ALU.add), "pmix_done")
                if what == "value" and u == 3:
                    for i in (1, 2):
                        b = take(dve, f"ada{i}")
                        step(V.tensor_tensor(mrows[:, i, :], b[:], mrows[:, i, :], ALU.add), tile=f"ada{i}")
                    for n in range(8):
                        b = take(dve, f"bc{n}")
                        dst = bc[:, n // 2, (n % 2) * 512:(n % 2) * 512 + 512]
                        if n // 2 == 2:
                            dve.wait_ge(sem("ffnw_in"), 16)
                            step(V.scalar_tensor_tensor(out=dst, in0=b[:], scalar=1.0,
                                                        in1=dst,
                                                        op0=ALU.add, op1=ALU.mult), tile=f"bc{n}")
                        else:
                            step(V.tensor_copy(dst, b[:]), tile=f"bc{n}")

            for t in range(NT):
                for h in range(H):
                    n = t * H + h
                    step(V.tensor_tensor_reduce(sq[:, 0:P], o[:, t, h * P:(h + 1) * P], o[:, t, h * P:(h + 1) * P],
                                                1.0, 0.0, ALU.mult, ALU.add, stat[:, 32 + n:33 + n]))
            step(V.tensor_scalar(stat[:, 40:48], stat[:, 32:40], 1.0 / P, EPS, ALU.mult, ALU.add), "sub_ms")
            dve.wait_ge(sem("sub_root"), 1)
            step(V.reciprocal(stat[:, 56:64], stat[:, 48:56]))
            for t in range(NT):
                for h in range(H):
                    n = t * H + h
                    step(V.tensor_scalar(o[:, t, h * P:(h + 1) * P], o[:, t, h * P:(h + 1) * P],
                                         stat[:, 56 + n:57 + n], None, ALU.mult), "sub_done")
            step(V.tensor_scalar(vecT[:, 11:12], vecT[:, 11:12], 1.0 - LAM_INIT, None, ALU.mult))
            for j in range(2):
                b = take(dve, f"mixT{j}")
                step(V.tensor_scalar(mixT[:, 2 * j:2 * j + 2, :], b[:].rearrange("p (k t) -> p k t", k=2),
                                     vecT[:, 11:12], None, ALU.mult), tile=f"mixT{j}")
            for t in range(NT):
                for n in range(2):
                    cols = slice(n * 512, n * 512 + 512)
                    b = take(dve, f"wo{t}_{n}")
                    step(V.tensor_tensor(sq[:, 0:512], b[:], bc[:, 0, cols], ALU.mult), tile=f"wo{t}_{n}")
                    step(V.tensor_tensor(xc[:, 2 + t, cols], xc[:, 2 + t, cols], sq[:, 0:512], ALU.add), "x1_done")

            dve.wait_ge(sem("ss2_done"), 2)
            step(V.tensor_scalar(stat[:, 2:4], stat[:, 0:2], 1.0 / D, EPS, ALU.mult, ALU.add), "ms2_done")
            dve.wait_ge(sem("root2_done"), 1)
            step(V.reciprocal(stat[:, 6:8], stat[:, 4:6]))
            for t in range(NT):
                step(V.scalar_tensor_tensor(out=hf[:, t, :], in0=xc[:, 2 + t, :], scalar=stat[:, 6 + t:7 + t],
                                            in1=bc[:, 2, :], op0=ALU.mult, op1=ALU.mult))
                step(V.tensor_tensor(hf[:, t, :], hf[:, t, :], bc[:, 1, :], ALU.add), "hf_done")

            dve.wait_ge(sem("iota_done"), 1)
            step(V.tensor_copy(iota_s, iota_i))
            step(V.tensor_copy(iota_e[:], iota_i[:, 0:E]))
            step(V.memset(gates[:], 0.0))
            step(V.memset(slots[:], -1.0))
            b = take(dve, "logits")
            step(V.tensor_copy(logit[:], b[:, 0:NT * E].rearrange("p (t e) -> p t e", t=NT)), tile="logits")
            for t in range(NT):
                step(V.max(top[:, t, :], logit[:, t, :]))
                step(V.tensor_scalar(topx[:, t, 0:1], top[:, t, 0:1], -1.0, None, ALU.mult), "top_done")
                step(V.max_index(top_at[:, t, :], top[:, t, :], logit[:, t, :]))
            step(V.tensor_copy(top_atf[:], top_at[:]))
            for t in range(NT):
                dve.wait_ge(sem("topx_done"), t + 1)
                step(V.reciprocal(topx[:, t, 2:3], topx[:, t, 1:2]))
                step(V.tensor_scalar(gate4[:, t, :], topx[:, t, 4:8], topx[:, t, 2:3], None, ALU.mult))
                for k in range(TOP_K):
                    step(V.tensor_scalar(hot[:, t, k, :], iota_e[:], top_atf[:, t, k:k + 1], gate4[:, t, k:k + 1],
                                         ALU.is_equal, ALU.mult))
                step(V.tensor_reduce(gates[:, t, 0:E], hot[:, t].rearrange("p k e -> p e k"), AX, ALU.add))
                for k in range(TOP_K):
                    step(V.tensor_scalar(hot[:, t, k, :], iota_e[:], top_atf[:, t, k:k + 1], None, ALU.is_equal))
                step(V.tensor_reduce(chosen[:, t, :], hot[:, t].rearrange("p k e -> p e k"), AX, ALU.add), "chosen_done")
            b = take(dve, "rank")
            for t in range(NT):
                step(V.scalar_tensor_tensor(out=slots[:, t, 0:E], in0=b[:, t * E:(t + 1) * E], scalar=1.0,
                                            in1=chosen[:, t, :], op0=ALU.add, op1=ALU.mult))
                step(V.tensor_scalar(slots[:, t, 0:E], slots[:, t, 0:E], -1.0, None, ALU.add))
            step(V.tensor_reduce(most[:, 0:1], b[:, 2 * E:3 * E], AX, ALU.max))
            step(V.tensor_copy(most_i[:], most[:, 0:1]), tile="rank")
            b = take(dve, "gatesT")
            step(V.tensor_copy(gatesT, b[0:E, 0:T]), tile="gatesT")
            for t in range(NT):
                for n in range(2):
                    b = take(dve, f"yb{t}_{n}")
                    step(V.tensor_copy(y[:, t, n * 512:n * 512 + 512], b[:]), tile=f"yb{t}_{n}")

            dve.sem_inc(moe("y_added", MAIN), 1)
            dve.sem_inc(moe("y_added", OVER), 1)
            select(dve, 0, 0, MAIN)
            with dve.Fori(0, PAIRS) as pair:
                dve.wait_ge(moe("xt_full", MAIN), pair + 1)
                select(dve, pair + 1, pair + 1, MAIN)
                dve_pair(dve, pair, pair, MAIN)
            most_dve = load_most(dve)
            with dve.Fori(1, ROUNDS) as r:
                with dve.If(most_dve > r * CAP):
                    V.tensor_scalar(iota_s, iota_s, float(CAP), None, ALU.add).then_inc(moe("next_round", OVER), 1)
                    with dve.Fori(0, PAIRS) as pair:
                        n = (r - 1) * PAIRS + pair
                        dve.wait_ge(moe("next_round", OVER), r)
                        select(dve, n, pair, OVER)
                        dve_pair(dve, n, pair, OVER)

            for t in range(NT):
                step(V.tensor_tensor(y[:, t, :], y[:, t, :], gf, ALU.mult))
                step(V.tensor_tensor(x2[:, t, :], x2[:, t, :], y[:, t, :], ALU.add), "x_moe")
            dve.wait_ge(sem("ss3_done"), 2)
            step(V.tensor_scalar(stat[:, 2:4], stat[:, 0:2], 1.0 / D, EPS, ALU.mult, ALU.add), "ms3_done")
            dve.wait_ge(sem("root3_done"), 1)
            step(V.reciprocal(stat[:, 6:8], stat[:, 4:6]))
            dve.wait_ge(sem("norm_in"), 48)
            for t in range(NT):
                step(V.scalar_tensor_tensor(out=x2[:, t, :], in0=x2[:, t, :], scalar=stat[:, 6 + t:7 + t],
                                            in1=final_w, op0=ALU.mult, op1=ALU.mult), "x2_done")
            for t in range(NT):
                b = take(dve, f"in{t}_2")
                for i in range(2):
                    step(V.tensor_copy(k_tok[:, t, :, i, :], b[:, 0:P].rearrange("p (h c) -> p h c", h=KVH)))
                step(V.tensor_copy(v_tok[:, t, :], b[:, P:2 * P]), tile=f"in{t}_2")
            dve.wait_ge(sem("mix_in"), 80)
            for j in range(2):
                b = take(dve, f"py{j}")
                for i in range(2):
                    g = 2 * j + i
                    step(V.tensor_scalar(mix2T[:, g, :], b[:, i * T:(i + 1) * T], vecT[:, 12 + g:13 + g], None, ALU.mult),
                         tile=f"py{j}" if i else None)
            for what, u in attention_order(len(UNITS2)):
                h, blk = UNITS2[u]
                w = (blk + 1) * P
                if what == "score":
                    b = take(dve, f"sw{u}")
                    if u >= 2:
                        dve.wait_ge(full(f"tw{u - 2}"), use(f"tw{u - 2}") + 1)
                    step(V.scalar_tensor_tensor(out=prob2[:, u % 2, 0:w], in0=neg_dist[:, 2 * P - w:2 * P],
                                                scalar=SLOPES[h], in1=b[:, 0:w], op0=ALU.mult, op1=ALU.add),
                         tile=f"sw{u}")
                    step(V.tensor_reduce(soft[:, u, 0:1], prob2[:, u % 2, 0:w], AX, ALU.max))
                    step(V.tensor_scalar(soft[:, u, 1:2], soft[:, u, 0:1], sinks[:, h:h + 1], -1.0, ALU.max, ALU.mult),
                         "masked")
                elif what == "value":
                    step(V.tensor_tensor(soft[:, u, 4:5], soft[:, u, 2:3], soft[:, u, 3:4], ALU.add))
                    step(V.reciprocal(soft[:, u, 5:6], soft[:, u, 4:5]))
                    b = take(dve, f"vw{u}")
                    step(V.tensor_scalar(o2[:, blk, h * HD:(h + 1) * HD], b[:, 0:HD], soft[:, u, 5:6], None, ALU.mult),
                         tile=f"vw{u}")

            def layer_norm(tiles, at, var, root, g, b_, done):
                for t in range(NT):
                    for c in range(2):
                        cols = slice(c * 512, c * 512 + 512)
                        bk = take(dve, f"{tiles}{t}_{c}")
                        step(V.scalar_tensor_tensor(out=x2[:, t, cols], in0=x2[:, t, cols], scalar=DEEPNORM, in1=bk[:],
                                                    op0=ALU.mult, op1=ALU.add), tile=f"{tiles}{t}_{c}")
                        step(V.bn_stats(bn[:, t, c, :], x2[:, t, cols]))
                    step(V.bn_aggr(stat[:, 40 + 2 * t:42 + 2 * t], bn[:, t, :, :].rearrange("p c s -> p (c s)")))
                    step(V.tensor_scalar(stat[:, at + t:at + t + 1], stat[:, 41 + 2 * t:42 + 2 * t], LN_EPS, None, ALU.add),
                         var)
                for t in range(NT):
                    dve.wait_ge(sem(root), t + 1)
                    step(V.reciprocal(stat[:, at + 8 + t:at + 9 + t], stat[:, at + 4 + t:at + 5 + t]))
                    step(V.tensor_scalar(x2[:, t, :], x2[:, t, :], stat[:, 40 + 2 * t:41 + 2 * t],
                                         stat[:, at + 8 + t:at + 9 + t], ALU.subtract, ALU.mult))
                    step(V.tensor_tensor(x2[:, t, :], x2[:, t, :], g, ALU.mult))
                    step(V.tensor_tensor(x2[:, t, :], x2[:, t, :], b_, ALU.add), done)

            layer_norm("wo2", 12, "var1", "root4_done", ln1g, ln1b, "h1_done")
            for j in range(16):
                wait_read(dve, f"part{j}")
                step(V.tensor_tensor(wide[:, j % 4, :], wide[:, j % 4, :], wide[:, j % 4, :], ALU.mult), "wide_done")
            dve.wait_ge(sem("norm2_in"), 32)
            layer_norm("wide", 22, "var2", "root5_done", ln2g, ln2b, "h2_done")
            dve.wait_ge(sem("b_gate_in"), 16)
            for n in range(4):
                t, c = divmod(n, 2)
                b = take(dve, f"gate{t}_{c}")
                step(V.tensor_tensor(gate_z[:, n, :], b[:], b_gate[:, c * 512:(c + 1) * 512], ALU.add), "gate_in", wait=n == 3)
            for n in range(4):
                t, c = divmod(n, 2)
                cols = slice(c * 512, c * 512 + 512)
                dve.wait_ge(sem("gate_done"), n + 1)
                b = take(dve, f"ple{t}_{c}")
                step(V.tensor_tensor(gate_z[:, n, :], gate_z[:, n, :], b[:], ALU.mult))
                step(V.tensor_tensor(x2[:, t, cols], x2[:, t, cols], gate_z[:, n, :], ALU.add), "out_done")

        @block.tensor
        def _(pe):
            def mm(out_, lhsT, rhs, first, last):
                return pe.matmul(out_, lhsT, rhs, start=first, stop=last, skip_group_check=True)

            freed = sem("ring_freed")

            pe.wait_ge(sem("consts"), 4)
            pe.wait_ge(sem("silu_done"), 1)
            b = claim(pe, "smallT")
            pe.transpose(b[:, 0:32], small[:], ident[0:32, 0:32]).then_inc(full("smallT"), 1)

            def ada(t):
                name = f"ada{t}"
                b = claim(pe, name)
                for k in range(KD):
                    n = CHUNK[(name, k)]
                    ring_wait(pe, n)
                    for q in range(4):
                        m = mm(b[32 * q:32 * q + 32, :], cT[:, k, :], slot(n)[:, q * 512:(q + 1) * 512],
                               k == 0, k == KD - 1)
                    if k < KD - 1:
                        m.then_inc(freed, 1)
                m.then_inc(full(name), 1)
                pe.wait_ge(full(name), use(name) + 1)
                pe.sem_inc(freed, 1)

            wait_read(pe, "smallT")
            ada(0)
            wait_read(pe, "ada0")
            b = claim(pe, "modT")
            for blk in range(4):
                m = pe.transpose(b[:, blk * P:(blk + 1) * P], mrows[:, 0, blk * P:(blk + 1) * P], ident[:])
            m.then_inc(full("modT"), 1)
            pe.wait_ge(sem("xn_done"), 4)
            for k in range(KD):
                b = claim(pe, f"hT{k}")
                for t in range(4):
                    m = pe.transpose(b[:, t * P:(t + 1) * P], xn[:, t, k * P:(k + 1) * P], ident[:])
                m.then_inc(full(f"hT{k}"), 1)

            wait_read(pe, "hT7")
            pe.wait_ge(sem("hT_done"), KD)
            for t in range(4):
                for c in ((1, 2, 3) if t < 2 else (0, 1, 2, 3)):
                    lo = 512 * c if c < 3 else (CKV if t < 2 else CQ)
                    hi = 512 * (c + 1) if c < 3 else IN_COLS
                    b = claim(pe, f"proj{t}_{c}")
                    for k in range(KD):
                        n = CHUNK[("w_in", k)]
                        if t == 0 and c == 1:
                            ring_wait(pe, n)
                        m = mm(b[:, 0:hi - lo], hT[:, k, t * P:(t + 1) * P], slot(n)[:, lo:hi], k == 0, k == KD - 1)
                    m.then_inc(full(f"proj{t}_{c}"), 1)
            pe.wait_ge(full("proj3_3"), use("proj3_3") + 1)
            pe.sem_inc(freed, KD)

            pe.wait_ge(sem("lat_done"), 6)
            b = claim(pe, "ckvT")
            for t in range(4):
                m = pe.transpose(b[:, t * P:(t + 1) * P], ckv[:, t, :], ident[:])
            m.then_inc(full("ckvT"), 1)
            pe.wait_ge(sem("kr_done"), 4)
            b = claim(pe, "krT")
            for t in range(4):
                m = pe.transpose(b[:, t * P:(t + 1) * P], kr[:, t, :, :].rearrange("p a c -> p (a c)"), ident[:])
            m.then_inc(full("krT"), 1)
            b = claim(pe, "cqT")
            for k in range(2):
                for t in range(NT):
                    m = pe.transpose(b[:, k * T + t * P:k * T + (t + 1) * P], cq[:, t, k * P:(k + 1) * P], ident[:])
            m.then_inc(full("cqT"), 1)
            wait_read(pe, "proj0_1")
            wait_read(pe, "proj1_1")
            wait_read(pe, "proj2_1")
            wait_read(pe, "proj3_1")
            for h in range(H):
                b = claim(pe, f"dkT{h}")
                for t in range(4):
                    m = pe.transpose(b[:, t * P:(t + 1) * P], dk[:, t, h * P:(h + 1) * P], ident[:])
                m.then_inc(full(f"dkT{h}"), 1)
            wait_read(pe, "proj2_0")
            wait_read(pe, "proj3_0")
            for j in range(2):
                b = claim(pe, f"dqT{j}")
                for hh in range(2):
                    for t in range(NT):
                        h = 2 * j + hh
                        m = pe.transpose(b[:, hh * T + t * P:hh * T + (t + 1) * P], dq[:, t, h * P:(h + 1) * P], ident[:])
                m.then_inc(full(f"dqT{j}"), 1)

            nq = CHUNK[("w_uq", 0)]
            ring_wait(pe, nq)
            wq = slot(nq)[:, 0:2 * 768].rearrange("p (k h c) -> p k h c", k=2, h=H)
            wait_read(pe, "cqT")
            b = claim(pe, "qrope")
            for t in range(NT):
                for k in range(2):
                    m = mm(b[:, t * 256:(t + 1) * 256], cqT[:, k, t * P:(t + 1) * P], wq[:, k, :, NOPE:NOPE + ROPE],
                           k == 0, k == 1)
            m.then_inc(full("qrope"), 1)
            for j in range(2):
                b = claim(pe, f"qnope{j}")
                for hh in range(2):
                    for k in range(2):
                        m = mm(b[:, hh * T:(hh + 1) * T], wq[:, k, 2 * j + hh, 0:NOPE], cqT[:, k, :], k == 0, k == 1)
                m.then_inc(full(f"qnope{j}"), 1)
            pe.wait_ge(full("qnope1"), use("qnope1") + 1)
            pe.sem_inc(freed, 1)
            nk = CHUNK[("w_ukv", 0)]
            ring_wait(pe, nk)
            wkv = slot(nk)[:, 0:1024].rearrange("p (h c) -> p h c", h=H)
            wait_read(pe, "ckvT")
            for h in range(H):
                b = claim(pe, f"knope{h}")
                mm(b[:], wkv[:, h, 0:NOPE], ckvT, True, True).then_inc(full(f"knope{h}"), 1)
            for t in range(4):
                b = claim(pe, f"mv{t}")
                m = mm(b[:], ckvT[:, t * P:(t + 1) * P], wkv[:, :, NOPE:2 * NOPE], True, True)
                m.then_inc(full(f"mv{t}"), 1)
            pe.wait_ge(full("mv3"), use("mv3") + 1)
            pe.sem_inc(freed, 1)
            wait_read(pe, "qrope")
            b = claim(pe, "qrT")
            for j in range(2):
                for t in range(NT):
                    m = pe.transpose(b[:, j * T + t * P:j * T + (t + 1) * P], qr[:, t, j * P:(j + 1) * P], ident[:])
            m.then_inc(full("qrT"), 1)

            for what, u in attention_order(len(UNITS)):
                kind, h, t = UNITS[u]
                if what == "score" and kind == "d":
                    if u == 0:
                        for x in ("dkT3", "dqT1", "proj3_2", "proj2_2", "proj1_2", "proj0_2"):
                            wait_read(pe, x)
                    for c in range(2):
                        b = claim(pe, f"s{u}_{c}")
                        rows = slice(64 * c, 64 * c + 64)
                        mm(b[:], dqT[rows, h, t * P:(t + 1) * P], dkT[rows, h, :], True, True)\
                            .then_inc(full(f"s{u}_{c}"), 1)
                elif what == "score":
                    if UNITS[u - 1][0] == "d":
                        for x in ("knope3", "qnope1", "krT", "qrT", "mv3"):
                            wait_read(pe, x)
                    b = claim(pe, f"s{u}_0")
                    rows = slice(64 * (h % 2), 64 * (h % 2) + 64)
                    mm(b[:], qnT[:, h, t * P:(t + 1) * P], knT[:, h, :], True, False)
                    mm(b[:], qrT[rows, h // 2, t * P:(t + 1) * P], krT[rows, :], False, True)\
                        .then_inc(full(f"s{u}_0"), 1)
                elif what == "turn":
                    pe.wait_ge(sem("pmix_done"), u + 1)
                    b = claim(pe, f"pT{u}")
                    for n in range(4):
                        m = pe.transpose(b[:, n * P:(n + 1) * P], prob[:, u % 2, 0, n * P:(n + 1) * P], ident[:])
                    m.then_inc(full(f"pT{u}"), 1)
                else:
                    wait_read(pe, f"pT{u}")
                    b = claim(pe, f"av{u}")
                    vals = dv if kind == "d" else mv
                    for n in range(4):
                        m = mm(b[:, 0:P], probT[:, u % 2, n * P:(n + 1) * P], vals[:, n, h * P:(h + 1) * P],
                               n == 0, n == 3)
                    m.then_inc(full(f"av{u}"), 1)
                if what == "value" and u == 3:
                    ada(1)
                    ada(2)
                    wait_read(pe, "ada1")
                    wait_read(pe, "ada2")
                    for n, (third, q) in enumerate(((1, 0), (1, 1), (1, 2), (1, 3), (2, 0), (2, 1), (2, 2), (2, 3))):
                        b = claim(pe, f"bc{n}")
                        mm(b[:], ones[32 * q:32 * q + 1, :], mrows[32 * q:32 * q + 1, third, :], True, True)\
                            .then_inc(full(f"bc{n}"), 1)

            for j in range(4):
                if j == 0:
                    pe.wait_ge(sem("sub_done"), 8)
                b = claim(pe, f"mixT{j}")
                for kk in range(2):
                    for t in range(NT):
                        k = 2 * j + kk
                        m = pe.transpose(b[:, kk * T + t * P:kk * T + (t + 1) * P], o[:, t, k * P:(k + 1) * P], ident[:])
                m.then_inc(full(f"mixT{j}"), 1)
            bw = {(t, n): claim(pe, f"wo{t}_{n}") for t in range(NT) for n in range(2)}
            for j in range(4):
                n_ = CHUNK[("w_out", j)]
                ring_wait(pe, n_)
                wait_read(pe, f"mixT{j}")
                w = slot(n_).rearrange("p (k n) -> p k n", k=2)
                for t in range(NT):
                    for n in range(2):
                        for kk in range(2):
                            k = 2 * j + kk
                            m = mm(bw[t, n][:], mixT[:, k, t * P:(t + 1) * P], w[:, kk, n * 512:(n + 1) * 512],
                                   k == 0, k == KD - 1)
                        if j == 3:
                            m.then_inc(full(f"wo{t}_{n}"), 1)
                        elif t == 1 and n == 1:
                            m.then_inc(freed, 1)

            pe.wait_ge(sem("hf_done"), NT)
            for j in range(4):
                b = claim(pe, f"hfT{j}")
                for kk in range(2):
                    for t in range(NT):
                        k = 2 * j + kk
                        m = pe.transpose(b[:, kk * T + t * P:kk * T + (t + 1) * P], hf[:, t, k * P:(k + 1) * P], ident[:])
                m.then_inc(full(f"hfT{j}"), 1)
            pe.wait_ge(full("wo1_1"), use("wo1_1") + 1)
            pe.sem_inc(freed, 1)
            pe.wait_ge(sem("router_in"), 32)
            b = claim(pe, "logits")
            for j in range(4):
                wait_read(pe, f"hfT{j}")
            for t in range(NT):
                for k in range(KD):
                    mm(b[:, t * E:(t + 1) * E], hfT[:, k, t * P:(t + 1) * P], rw[:, k, :], k == 0, False)
                m = mm(b[:, t * E:(t + 1) * E], ones[0:1, :], rb[:], False, True)
            m.then_inc(full("logits"), 1)
            pe.wait_ge(sem("chosen_done"), NT)
            pe.wait_ge(sem("below_done"), 1)
            b = claim(pe, "rank")
            mm(b[:, 0:E], below, chosen[:, 0, :], True, True)
            mm(b[:, E:2 * E], ones[:], chosen[:, 0, :], True, False)
            mm(b[:, E:2 * E], below, chosen[:, 1, :], False, True)
            mm(b[:, 2 * E:3 * E], ones[:], chosen[:, 0, :], True, False)
            mm(b[:, 2 * E:3 * E], ones[:], chosen[:, 1, :], False, True).then_inc(full("rank"), 1)
            b = claim(pe, "gatesT")
            for t in range(NT):
                m = pe.transpose(b[0:E, t * P:(t + 1) * P], gates[:, t, 0:E], ident[:])
            m.then_inc(full("gatesT"), 1)
            wait_read(pe, "gatesT")
            pe.wait_ge(sem("b2_in"), 16)
            for t in range(NT):
                for n in range(2):
                    b = claim(pe, f"yb{t}_{n}")
                    mm(b[:], gatesT[:, t * P:(t + 1) * P], b2[:, n * 512:(n + 1) * 512], True, True)\
                        .then_inc(full(f"yb{t}_{n}"), 1)
            for name in FRONT_TILES[-8:]:
                wait_read(pe, name)

            pe.wait_ge(sem("pick_done"), 1)
            gather(pe, 0, MAIN, None)
            with pe.Fori(0, PAIRS) as pair:
                hidden(pe, pair, MAIN)
                gather(pe, pair + 1, MAIN, pair * 4 + 1)
                pe_rest(pe, pair, MAIN, 1)
            pe.wait_ge(moe("y_added", MAIN), 4 * PAIRS + 1)
            most_pe = load_most(pe)
            pe.sem_inc(moe("ring_freed", OVER), SLOTS)
            with pe.Fori(1, ROUNDS) as r:
                with pe.If(most_pe > r * CAP):
                    with pe.Fori(0, PAIRS) as pair:
                        n = (r - 1) * PAIRS + pair
                        gather(pe, n, OVER, n * 4 + 1)
                        hidden(pe, n, OVER)
                        pe_rest(pe, n, OVER, 0)
                        pe.wait_ge(moe("y_added", OVER), 4 * n + 5)

            pe.wait_ge(moe("mixed", MAIN), 4 * PAIRS)
            pe.sem_inc(sem("moe_used"), 1)
            pe.sem_inc(sem("moe_done"), 1)

            def turn_tokens(name, src, ready):
                pe.wait_ge(sem(ready), NT)
                for j in range(4):
                    b = claim(pe, f"{name}{j}")
                    for kk in range(2):
                        for t in range(NT):
                            k = 2 * j + kk
                            m = pe.transpose(b[:, kk * T + t * P:kk * T + (t + 1) * P], src[:, t, k * P:(k + 1) * P], ident[:])
                    m.then_inc(full(f"{name}{j}"), 1)

            turn_tokens("xT", x2, "x2_done")
            parts = [(0, 512), (512, 1024), (1024, 1280)]
            bi = {(t, n): claim(pe, f"in{t}_{n}") for t in range(NT) for n in range(3)}
            for k in range(KD):
                ring_wait(pe, CHUNK[("w_in2", k)])
                wait_read(pe, f"xT{k // 2}")
                for t in range(NT):
                    for n, (lo, hi) in enumerate(parts):
                        m = mm(bi[t, n][:, 0:hi - lo], x2T[:, k, t * P:(t + 1) * P], slot(CHUNK[("w_in2", k)])[:, lo:hi],
                               k == 0, k == KD - 1)
                        if k == KD - 1:
                            m.then_inc(full(f"in{t}_{n}"), 1)
                if k < KD - 1:
                    m.then_inc(freed, 1)
            wait_read(pe, "in1_2")
            pe.sem_inc(freed, 1)
            wait_read(pe, "in0_2")
            b = claim(pe, "kT")
            for h in range(KVH):
                for t in range(NT):
                    m = pe.transpose(b[:, h * T + t * P:h * T + (t + 1) * P],
                                     k_tok[:, t, h].rearrange("p a c -> p (a c)"), ident[:])
            m.then_inc(full("kT"), 1)
            wait_read(pe, "in0_1")
            wait_read(pe, "in1_1")
            for j in range(2):
                b = claim(pe, f"qT{j}")
                for i in range(2):
                    for t in range(NT):
                        k = 2 * j + i
                        m = pe.transpose(b[:, i * T + t * P:i * T + (t + 1) * P], q_tok[:, t, k * P:(k + 1) * P], ident[:])
                m.then_inc(full(f"qT{j}"), 1)
            wait_read(pe, "in0_0")
            wait_read(pe, "in1_0")
            pe.wait_ge(sem("mix_in"), 80)
            for j in range(2):
                b = claim(pe, f"pd{j}")
                for i in range(2):
                    g = 2 * j + i
                    for t in range(NT):
                        m = mm(b[:, i * T:(i + 1) * T], u_tok[:, t, g * P:(g + 1) * P], bands[:, g, t, :], t == 0, t == 1)
                m.then_inc(full(f"pd{j}"), 1)
            for j in range(2):
                wait_read(pe, f"pd{j}")
                b = claim(pe, f"py{j}")
                for i in range(2):
                    g = 2 * j + i
                    m = mm(b[:, i * T:(i + 1) * T], w_pool[:, g, :], pool_dT[:, g, :], True, True)
                m.then_inc(full(f"py{j}"), 1)
            wait_read(pe, "kT")
            wait_read(pe, "qT1")
            for what, u in attention_order(len(UNITS2)):
                h, blk = UNITS2[u]
                w = (blk + 1) * P
                rows = slice(64 * (h % 2), 64 * (h % 2) + 64)
                if what == "score":
                    b = claim(pe, f"sw{u}")
                    mm(b[:, 0:w], q2T[rows, h // 2, blk * P:(blk + 1) * P], k2T[rows, h // 4, 0:w], True, True)\
                        .then_inc(full(f"sw{u}"), 1)
                elif what == "turn":
                    pe.wait_ge(sem("exp2_done"), u + 1)
                    b = claim(pe, f"tw{u}")
                    for n in range(blk + 1):
                        m = pe.transpose(b[:, n * P:(n + 1) * P], prob2[:, u % 2, n * P:(n + 1) * P], ident[:])
                    m.then_inc(full(f"tw{u}"), 1)
                else:
                    wait_read(pe, f"tw{u}")
                    b = claim(pe, f"vw{u}")
                    kv = (h // 4) * HD
                    for n in range(blk + 1):
                        m = mm(b[:, 0:HD], prob2T[:, u % 2, n * P:(n + 1) * P], v_tok[:, n, kv:kv + HD], n == 0, n == blk)
                    m.then_inc(full(f"vw{u}"), 1)
            for j in range(2):
                for u in ((2 * (4 * j + 3) + 1, 2 * (4 * j + 3))):
                    wait_read(pe, f"vw{u}")
                b = claim(pe, f"oT{j}")
                for i in range(2):
                    for t in range(NT):
                        k = 2 * j + i
                        m = pe.transpose(b[:, i * T + t * P:i * T + (t + 1) * P], o2[:, t, k * P:(k + 1) * P], ident[:])
                m.then_inc(full(f"oT{j}"), 1)

            def by_pairs(kind, tiles, src, ready, last=True):
                bw = {(t, n): claim(pe, f"{tiles}{t}_{n}") for t in range(NT) for n in range(2)}
                for j in range(4):
                    n_ = CHUNK[(kind, j)]
                    ring_wait(pe, n_)
                    for name in ready(j):
                        wait_read(pe, name)
                    w = slot(n_).rearrange("p (k n) -> p k n", k=2)
                    for t in range(NT):
                        for n in range(2):
                            for kk in range(2):
                                k = 2 * j + kk
                                m = mm(bw[t, n][:], src[:, k, t * P:(t + 1) * P], w[:, kk, n * 512:(n + 1) * 512],
                                       k == 0, k == KD - 1)
                            if j == 3:
                                m.then_inc(full(f"{tiles}{t}_{n}"), 1)
                            elif t == 1 and n == 1:
                                m.then_inc(freed, 1)

            by_pairs("w_out2", "wo2", mix2T, lambda j: [["py0"], ["py1"], ["oT0"], ["oT1"]][j])
            b = claim(pe, "plT")
            for k in range(2):
                for t in range(NT):
                    m = pe.transpose(b[:, k * T + t * P:k * T + (t + 1) * P], p_tok[:, t, k * P:(k + 1) * P], ident[:])
            m.then_inc(full("plT"), 1)
            wait_read(pe, "wo21_1")
            pe.sem_inc(freed, 1)
            turn_tokens("h1T", x2, "h1_done")
            sums = {(t, c): claim(pe, f"wide{t}_{c}") for t in range(NT) for c in range(2)}

            def wide_part(j):
                n_ = CHUNK[("ff1", j)]
                ring_wait(pe, n_)
                if j == 0:
                    for i in range(4):
                        wait_read(pe, f"h1T{i}")
                w = slot(n_).rearrange("p (k n) -> p k n", k=KD)
                b = claim(pe, f"part{j}")
                for i in range(2):
                    for k in range(KD):
                        m = mm(b[:, i * T:(i + 1) * T], w[:, k, i * P:(i + 1) * P], x2T[:, k, :], k == 0, k == KD - 1)
                m.then_inc(full(f"part{j}"), 1)

            def wide_sum(j):
                n_ = CHUNK[("ff2", j)]
                ring_wait(pe, n_)
                pe.wait_ge(sem("wide_done"), j + 1)
                w = slot(n_).rearrange("p (k n) -> p k n", k=2)
                for t in range(NT):
                    for c in range(2):
                        for kk in range(2):
                            m = mm(sums[t, c][:], wide[:, j % 4, kk * T + t * P:kk * T + (t + 1) * P],
                                   w[:, kk, c * 512:(c + 1) * 512], j == 0 and kk == 0, j == 15 and kk == 1)
                        if j == 15:
                            m.then_inc(full(f"wide{t}_{c}"), 1)
                        elif t == 0 and c == 0:
                            m.then_inc(freed, 1)
                        elif t == 1 and c == 0:
                            m.then_inc(sem("wide_last"), 1)
                        elif t == 1 and c == 1:
                            m.then_inc(sem("wide_used"), 1)

            wide_part(0)
            for j in range(16):
                if j < 15:
                    wide_part(j + 1)
                wide_sum(j)
                if j < 15:
                    pe.wait_ge(sem("wide_used"), j + 1)
                    pe.sem_inc(freed, 1)
            pe.wait_ge(full("wide1_1"), use("wide1_1") + 1)
            pe.sem_inc(freed, 2)

            ring_wait(pe, CHUNK[("w_ple", 0)])
            wait_read(pe, "plT")
            turn_tokens("h2T", x2, "h2_done")
            w = slot(CHUNK[("w_ple", 0)]).rearrange("p (k n) -> p k n", k=2)
            for t in range(NT):
                for c in range(2):
                    b = claim(pe, f"ple{t}_{c}")
                    for k in range(2):
                        m = mm(b[:], pT[:, k, t * P:(t + 1) * P], w[:, k, c * 512:(c + 1) * 512], k == 0, k == 1)
                    m.then_inc(full(f"ple{t}_{c}"), 1)
            by_pairs("gate", "gate", x2T, lambda j: [f"h2T{j}"])


INPUTS = [
    "x", "c", "ctx", "c_ctx", "w_ada", "b_ada", "attn_norm_w", "w_in", "q_norm_w", "kv_norm_w", "w_uq", "w_ukv",
    "lambda_q1", "lambda_k1", "lambda_q2", "lambda_k2", "subln_w", "w_out", "ffn_norm_w", "router_w", "router_b",
    "w1", "b1", "w2", "b2", "final_norm_w", "p_2", "w_in_2", "w_pool_2", "pool_scale_2", "attn_sinks_2", "w_out_2",
    "ln1_g_2", "ln1_b_2", "w_ff1_2", "w_ff2_2", "ln2_g_2", "ln2_b_2", "w_ple_2", "w_ple_gate_2", "b_ple_gate_2",
]


def shape_tables():
    import numpy as np

    pairs, grid_w = 16, 64
    row = np.repeat(np.arange(T // grid_w, dtype=np.float32), grid_w)
    col = np.tile(np.arange(grid_w, dtype=np.float32), T // grid_w)
    inv = (np.float32(10000.0) ** (-np.arange(pairs, dtype=np.float32) / np.float32(pairs))).astype(np.float32)
    ang = np.stack([row[:, None] * inv, col[:, None] * inv], axis=1).astype(np.float32)
    cos = np.cos(ang).astype(np.float32)
    sin = np.sin(ang).astype(np.float32)
    dist = np.arange(P)[:, None] + P - np.arange(2 * P)[None, :]
    neg_dist = np.where((dist >= 0) & (dist < P), -dist, -1e32).astype(np.float32)
    pool_bands = np.zeros((4, T, T), np.float32)
    for g, w in enumerate((2, 4, 8, 16)):
        for t in range(T):
            lo = max(t + 1 - w, 0)
            pool_bands[g, lo:t + 1, t] = np.float32(1.0) / np.float32(t + 1 - lo)
            pool_bands[g, t, t] -= np.float32(1.0)
    return {
        "rope_cos": np.ascontiguousarray(np.concatenate([cos, cos], axis=2).reshape(T, 64)),
        "rope_sin": np.ascontiguousarray(sin.reshape(T, 32)),
        "neg_dist": neg_dist,
        "pool_bands": pool_bands,
    }


def kernel(**inputs):
    import numpy as np
    import concourse.bacc as bacc
    from concourse.bass_utils import run_bass_kernel_spmd as run

    nc = bacc.Bacc("TRN2", target_bir_lowering=False, num_devices=1)
    arrays, args = {}, {}
    tables = shape_tables()
    for name in INPUTS + list(tables):
        v = np.ascontiguousarray(inputs[name] if name in inputs else tables[name])
        arrays[f"in_{name}"] = v
        args[name] = nc.dram_tensor(f"in_{name}", v.shape, mybir.dt.from_np(v.dtype), kind="ExternalInput").ap()
    out = nc.dram_tensor("out", (1, T, D), F32, kind="ExternalOutput").ap()
    build(nc, args, out)
    return run(nc, [arrays], core_ids=[0]).results[0]["out"]
```

```python
from contextlib import ExitStack

import concourse.bass as bass
from concourse import mybir

F32 = mybir.dt.float32
F32R = mybir.dt.float32r
I32 = mybir.dt.int32
U32 = mybir.dt.uint32
ALU = mybir.AluOpType
ACT = mybir.ActivationFunctionType
AX = mybir.AxisListType.X

P = 128
D = 1024
KD = D // P
T = 256
NT = T // P
EPS = 1e-6

H = 4
DQ, DK, DV, CQ, CKV, KR = 0, 512, 1024, 1536, 1792, 1920
IN_COLS = 1984
Q_RANK, KV_RANK, NOPE, ROPE = 256, 128, 128, 64
DIFF_SCALE = 64 ** -0.5
MLA_SCALE = (NOPE + ROPE) ** -0.5
LAM_INIT = 0.8 - 0.6
KEYS = 2 * T

E = 32
TOP_K = 4
FF = 1024
CAP = 64
ROUNDS = T // CAP
LIMIT = 7.0
ALPHA = 1.702

IN2 = 1280
LN_EPS = 1e-5
DEEPNORM = 2.0 ** 0.25
FF2 = 4096
QH, KVH, HD = 8, 2, 64
SLOPES = [2.0 ** (-8.0 * (h + 1) / QH) for h in range(QH)]

SLOTS = 12
SLOT = 2048

ADA0 = [("ada0", k) for k in range(KD)]
W_IN = [("w_in", k) for k in range(KD)]
MLA = [("w_uq", 0), ("w_ukv", 0)]
ADA12 = [(f"ada{t}", k) for t in (1, 2) for k in range(KD)]
W_OUT = [("w_out", j) for j in range(4)]
FRONT = ADA0 + W_IN + MLA + ADA12 + W_OUT
PAIRS = E // 2
PAIR = [("w1", k, i) for k in range(KD) for i in range(2)] + [("w2", j, i) for j in range(4) for i in range(2)]
N_FRONT = len(FRONT)
N_MOE = PAIRS * len(PAIR)
assert len(PAIR) == 2 * SLOTS
BACK = ([("w_in2", k) for k in range(KD)] + [("w_out2", j) for j in range(4)]
        + [("ff1", 0)] + [c for j in range(15) for c in (("ff1", j + 1), ("ff2", j))] + [("ff2", 15)]
        + [("w_ple", 0)] + [("gate", j) for j in range(4)])
CHUNK = {c: n for n, c in enumerate(FRONT)}
CHUNK.update({c: N_FRONT + N_MOE + n for n, c in enumerate(BACK)})

ROUNDED = 4
BACK_SLOTS = SLOTS - ROUNDED
SPLIT = [c for c in BACK if c[0] != "w_ple"]
N_BEFORE = N_FRONT + N_MOE
FREED_BY_PAIR = [(n % SLOTS, n) for n in range(N_BEFORE - SLOTS, N_BEFORE) if n % SLOTS < BACK_SLOTS]
SLOT_OF, USE_OF, AFTER = {}, {}, {}
for _c, _n in CHUNK.items():
    if _n < N_BEFORE:
        SLOT_OF[_c], USE_OF[_c], AFTER[_c] = _n % SLOTS, _n // SLOTS + 1, _n - SLOTS + 1
    else:
        _m = _n - N_BEFORE
        _s, _last = FREED_BY_PAIR[_m % BACK_SLOTS]
        SLOT_OF[_c], USE_OF[_c] = _s, _last // SLOTS + 1 + _m // BACK_SLOTS + 1
        AFTER[_c] = _last + 1 if _m < BACK_SLOTS else _n - BACK_SLOTS + 1

FRONT_TILES = (
    ["smallT", "ada0", "modT"] + [f"hT{k}" for k in range(KD)]
    + [f"proj{t}_{c}" for t in range(4) for c in ((1, 2, 3) if t < 2 else (0, 1, 2, 3))]
    + ["ckvT", "krT", "cqT"] + [f"dkT{h}" for h in range(H)] + ["dqT0", "dqT1"]
    + ["qrope", "qnope0", "qnope1"] + [f"knope{h}" for h in range(H)] + [f"mv{t}" for t in range(4)] + ["qrT"]
)
UNITS = [("d", h, t) for h in range(H) for t in range(NT)] + [("m", h, t) for h in range(H) for t in range(NT)]


def attention_order(n_units):
    order = []
    for i in range(n_units + 2):
        if i < n_units:
            order.append(("score", i))
        if 1 <= i <= n_units:
            order.append(("turn", i - 1))
        if i >= 2:
            order.append(("value", i - 2))
    return order


for _what, _u in attention_order(len(UNITS)):
    if _what == "score":
        FRONT_TILES += [f"s{_u}_{c}" for c in range(2 if UNITS[_u][0] == "d" else 1)]
    else:
        FRONT_TILES.append(f"{'pT' if _what == 'turn' else 'av'}{_u}")
    if _what == "value" and _u == 3:
        FRONT_TILES += ["ada1", "ada2"] + [f"bc{n}" for n in range(8)]
FRONT_TILES += [f"mixT{j}" for j in range(4)] + [f"wo{t}_{n}" for t in range(NT) for n in range(2)]
FRONT_TILES += [f"hfT{j}" for j in range(4)] + ["logits", "rank"]

UNITS2 = [(h, b) for h in range(QH) for b in range(NT)]

BACK_TILES = [f"xT{j}" for j in range(4)] + [f"in{t}_{n}" for t in range(NT) for n in range(3)]
BACK_TILES += ["kT", "qT0", "qT1", "pd0", "pd1", "py0", "py1"]
BACK_TILES += [{"score": "sw", "turn": "tw", "value": "vw"}[w] + str(u) for w, u in attention_order(len(UNITS2))]
BACK_TILES += ["oT0", "oT1"] + [f"wo2{t}_{n}" for t in range(NT) for n in range(2)] + ["plT"]
BACK_TILES += [f"h1T{j}" for j in range(4)]


def place_tiles():
    held, at = [0] * 8, {}

    def put(name, bank):
        at[name] = (bank, held[bank])
        held[bank] += 1

    for part in (FRONT_TILES, BACK_TILES):
        for n, name in enumerate(part):
            put(name, n % 8)
    for n, name in enumerate([f"wide{t}_{c}" for t in range(NT) for c in range(2)]):
        put(name, n)
    for j in range(16):
        put(f"part{j}", 4 + j % 4)
    for n, name in enumerate([f"ple{t}_{c}" for t in range(NT) for c in range(2)] + [f"h2T{j}" for j in range(4)]):
        put(name, (n + 4) % 8)
    for n, name in enumerate([f"gate{t}_{c}" for t in range(NT) for c in range(2)]):
        put(name, n)
    return at


GATE_BANKS, UP_BANKS, GATHER_BANKS, OUT_BANKS = (0, 1), (2, 3), (4, 5), (6, 7)
TURN_BANKS, SHARE_BANK, MIX_BANKS = GATE_BANKS, UP_BANKS[0], GATHER_BANKS


def build(nc, a, out):
    with ExitStack() as ctx:
        address = {}

        def sb(name, shape, dt=F32):
            t = ctx.enter_context(nc.sbuf_tensor(name, shape, dt))
            size = 4
            for n in shape[1:]:
                size *= n
            address[name] = nc.sbuf_base - size
            return t

        def over(name, shape, place, skip=0):
            return nc.alloc_sbuf_tensor_at(name, shape, F32, offset=address[place] + 4 * skip)

        sems, count = {}, {}

        def sem(name):
            if name not in sems:
                sems[name] = ctx.enter_context(nc.semaphore(name))
                count[name] = 0
            return sems[name]

        banks = [ctx.enter_context(nc.psum_tensor(f"bank{i}", [P, 512], F32)) for i in range(8)]

        ring = sb("ring", [P, SLOTS, SLOT])
        ident = sb("ident", [P, P])
        ones = sb("ones", [P, P])
        xc = sb("xc", [P, 4, D])
        xn = sb("xn", [P, 4, D])
        hT = sb("hT", [P, KD, KEYS])
        small = sb("small", [32, P])
        csig = sb("csig", [16, P])
        cT = sb("cT", [P, KD, 32])
        vecT = sb("vecT", [P, 16])
        mrows = sb("mrows", [P, 3, 512])
        modT = sb("modT", [P, 2, 16])
        scol = sb("scol", [P, 2, KD])
        lamv = sb("lamv", [P, 4, 64])
        lam = sb("lam", [P, 8])
        rope_cos = sb("rope_cos", [P, NT, 64])
        rope_sin = sb("rope_sin", [P, NT, 32])
        stat = sb("stat", [P, 64])
        sq = sb("sq", [P, D])
        ropet = sq[:].rearrange("p (a c) -> p a c", a=2)
        dq = sb("dq", [P, NT, 512])
        dk = sb("dk", [P, 4, 512])
        dv = sb("dv", [P, 4, 512])
        cq = sb("cq", [P, NT, Q_RANK])
        ckv = sb("ckv", [P, 4, KV_RANK])
        kr = sb("kr", [P, 4, 2, ROPE])
        dkT = xc[:, 0:2, :].rearrange("p a (h k) -> p (a h) k", h=2)
        dqT = sb("dqT", [P, H, T])
        cqT = cq[:]
        ckvT = ckv[:].rearrange("p t c -> p (t c)")
        krT = kr[:].rearrange("p t a c -> p (t a c)")
        qnT = xn[:, 0, :].rearrange("p (h t) -> p h t", h=H)
        qrT = xn[:, 1, 0:512].rearrange("p (j t) -> p j t", j=2)
        qr = xn[:, 1, 512:1024].rearrange("p (t c) -> p t c", t=NT)
        knT = hT[:, 0:4, :]
        mv = hT[:, 4:8, :]
        prob = xn[:, 2:4, :].rearrange("p a (c k) -> p a c k", c=2)
        probT = dq[:]
        psum_sum = sb("psum_sum", [P, len(UNITS), 8])
        o = dk[:].rearrange("p (t a) c -> p t (a c)", t=NT)
        mixT = hT[:, 0:4, :].rearrange("p k (a t) -> p (k a) t", a=2)
        bc = sb("bc", [P, 4, D])

        hf = xn[:, 2:4, :]
        hfT = hT[:, 4:8, :].rearrange("p k (a t) -> p (k a) t", a=2)
        rw = xc[:, 1, 0:KD * E].rearrange("p (k e) -> p k e", k=KD)
        rb = sb("rb", [1, E])
        b2rows = xc[0:2, 0, :]
        logit = sb("logit", [P, NT, E])
        top = sb("top", [P, NT, 8])
        top_at = sb("top_at", [P, NT, 8], U32)
        top_atf = sb("top_atf", [P, NT, 8])
        topx = sb("topx", [P, NT, 8])
        gate4 = sb("gate4", [P, NT, TOP_K])
        hot = sq[:, 0:NT * TOP_K * E].rearrange("p (t k e) -> p t k e", t=NT, k=TOP_K)
        gates = sb("gates", [P, NT, E + 2])
        chosen = sb("chosen", [P, NT, E])
        slots = sb("slots", [P, NT, E + 2])
        iota_i = ropet[:, 1, 256:256 + CAP].bitcast(I32)
        iota_e = sb("iota_e", [P, E])
        iota_s = mrows[:, 0, P:P + CAP]
        below = mrows[:, 0, 0:P]
        most = sb("most", [P, 2])
        most_i = sb("most_i", [P, 1], I32)
        sel = xn[:, 0, 768:1024].rearrange("p (t s) -> p t s", t=NT)
        selg = xn[:, 0, 0:256].rearrange("p (t s) -> p t s", t=NT)
        gathered = xn[:, 1, :].rearrange("p (k s) -> p k s", k=KD)
        selgT = xn[:, 0, 512:768]
        b1rows = dv[0:2, :, :].rearrange("p t c -> p (t c)")
        pick = small[0:2, :]
        out2 = o[:, 0, :]
        gs = mrows[:, 1:3, :].rearrange("p a n -> p (a n)")
        us = o[:, 1, :]
        sg = sq[:]
        actT = dq[:].rearrange("p a (j s) -> p (a j) s", j=4)

        final_w, ln1g, ln1b, gf = (bc[:, n, :] for n in range(4))
        ln2g, ln2b = xc[:, 0, :], xc[:, 1, :]
        bands = hT[:, 4:8, :].rearrange("p g (k t) -> p g k t", k=NT)
        w_pool = cq[:].rearrange("p t (g c) -> p (t g) c", g=2)
        p_tok = ckv[:].rearrange("p (t a) c -> p t (a c)", t=NT)
        neg_dist = kr[:, 0:2, :, :].rearrange("p t a c -> p (t a c)")
        sinks = kr[:, 2, 0, 0:QH]
        b_gate = dv[:, 0:2, :].rearrange("p t c -> p (t c)")
        x2 = xc[:, 2:4, :]
        u_tok, q_tok = dk[:, 0:2, :], dk[:, 2:4, :]
        k_tok = dq[:, 0, :].rearrange("p (t h a c) -> p t h a c", t=NT, h=KVH, a=2)
        v_tok = dq[:, 1, 0:2 * KVH * HD].rearrange("p (t c) -> p t c", t=NT)
        pool_dT = xn[:, 0, :].rearrange("p (g t) -> p g t", g=4)
        q2T = xn[:, 1, :].rearrange("p (j t) -> p j t", j=4)
        k2T = sq[:, 0:KVH * T].rearrange("p (h t) -> p h t", h=KVH)
        prob2 = dv[:, 2, :].rearrange("p (a k) -> p a k", a=2)
        prob2T = dv[:, 3, :].rearrange("p (a k) -> p a k", a=2)
        soft = psum_sum
        o2 = u_tok
        wide = dk[:, 0:2, :]
        pT = sq[:, 512:1024].rearrange("p (k t) -> p k t", k=2)
        bn = sb("bn", [P, NT, 2, 6])
        w_hi = over("w_hi", [P, ROUNDED, SLOT], "ring", BACK_SLOTS * SLOT)
        w_lo = over("w_lo", [P, BACK_SLOTS, SLOT], "ring")
        x_hi = over("x_hi", [P, KD, T], "xn", 2 * D)
        x_lo = over("x_lo", [P, KD, T], "hT")
        h_lo = over("h_lo", [P, KD, T], "hT", 4 * KEYS)
        wide_hi = over("wide_hi", [P, 2, 512], "hT")
        wide_lo = over("wide_lo", [P, 2, 512], "hT", 2 * 512)
        gate_z = hT[:, 0:4, :]

        tile_at = place_tiles()

        def full(name):
            return sem(f"bank_full{tile_at[name][0]}")

        def drained(name):
            return sem(f"bank_drained{tile_at[name][0]}")

        def use(name):
            return tile_at[name][1]

        def bank(name):
            return banks[tile_at[name][0]]

        def claim(pe, name):
            if use(name):
                pe.wait_ge(drained(name), use(name))
            return bank(name)

        def take(eng, name):
            eng.wait_ge(full(name), use(name) + 1)
            return bank(name)

        def wait_read(eng, name):
            eng.wait_ge(drained(name), use(name) + 1)

        def stepper(eng, link):
            def step(ins, name=None, tile=None, wait=True):
                if tile is not None:
                    s, v = drained(tile), use(tile) + 1
                else:
                    s = sem(name or link)
                    count[name or link] += 1
                    v = count[name or link]
                ins.then_inc(s, 1)
                if wait:
                    eng.wait_ge(s, v)
            return step

        def ring_wait(eng, chunk):
            eng.wait_ge(sem(f"landed{SLOT_OF[chunk]}"), 16 * USE_OF[chunk])

        def slot(chunk):
            return ring[:, SLOT_OF[chunk], :]

        def used_wait(eng, chunk):
            kind, k = chunk
            if kind == "ff1":
                eng.wait_ge(full(f"part{k}"), use(f"part{k}") + 1)
            elif kind == "ff2" and k < 15:
                eng.wait_ge(sem("wide_used"), k + 1)
            elif chunk == ("ff2", 15):
                eng.wait_ge(full("wide1_1"), use("wide1_1") + 1)
            elif chunk == ("w_out2", 3):
                eng.wait_ge(full("wo21_1"), use("wo21_1") + 1)
            elif chunk == ("w_in2", 7):
                eng.wait_ge(full("in1_2"), use("in1_2") + 1)
            else:
                eng.wait_ge(sem("ring_freed"), CHUNK[chunk] + 1)

        def splits_at(j):
            return [SPLIT.index(c) for c in (("ff1", j + 2), ("ff2", j + 1)) if c in SPLIT]

        def width(kind):
            return IN2 if kind == "w_in2" else SLOT

        def round_weights(act, n):
            chunk = SPLIT[n]
            if n >= ROUNDED:
                used_wait(act, SPLIT[n - ROUNDED])
            ring_wait(act, chunk)
            w = width(chunk[0])
            act.activation(w_hi[:, n % ROUNDED, 0:w].bitcast(F32R), slot(chunk)[:, 0:w], ACT.Copy)\
                .then_inc(sem("w_rounded"), 1)

        def rest_of_weights(dve, n):
            chunk = SPLIT[n]
            w = width(chunk[0])
            dve.wait_ge(sem("w_rounded"), n + 1)
            dve.tensor_tensor(w_lo[:, SLOT_OF[chunk], 0:w].bitcast(F32R), slot(chunk)[:, 0:w],
                              w_hi[:, n % ROUNDED, 0:w], ALU.subtract).then_inc(sem("w_split"), 1)

        def split_weights(pe, chunk):
            n = SPLIT.index(chunk)
            pe.wait_ge(sem("w_split"), n + 1)
            return (w_hi[:, n % ROUNDED, :].bitcast(F32R), w_lo[:, SLOT_OF[chunk], :].bitcast(F32R))

        def source(kind, k, expert=None):
            if kind[:3] == "ada":
                t = int(kind[3])
                return a["w_ada"][0, k * P:(k + 1) * P, t * SLOT:(t + 1) * SLOT], slice(0, SLOT), None
            if kind == "w_in":
                return a["w_in"][0, k * P:(k + 1) * P, :], slice(0, IN_COLS), None
            if kind == "w_uq":
                return a["w_uq"][0].rearrange("(k p) n -> p k n", p=P), slice(0, 2 * 768), 2
            if kind == "w_ukv":
                return a["w_ukv"][0], slice(0, 1024), None
            if kind == "w1":
                return a["w1"][0, expert, k * P:(k + 1) * P, :], slice(0, SLOT), None
            if kind == "w2":
                return (a["w2"][0, expert, k * 2 * P:(k + 1) * 2 * P, :].rearrange("(k p) n -> p k n", p=P),
                        slice(0, SLOT), 2)
            if kind == "w_in2":
                return a["w_in_2"][0, k * P:(k + 1) * P, :], slice(0, IN2), None
            if kind == "ff1":
                return a["w_ff1_2"][0, :, k * 256:(k + 1) * 256].rearrange("(k p) n -> p k n", p=P), slice(0, SLOT), KD
            pairs = {"w_out2": "w_out_2", "ff2": "w_ff2_2", "w_ple": "w_ple_2", "gate": "w_ple_gate_2"}
            if kind in pairs:
                return (a[pairs[kind]][0, k * 2 * P:(k + 1) * 2 * P, :].rearrange("(k p) n -> p k n", p=P),
                        slice(0, SLOT), 2)
            if kind == "w_out":
                return a["w_out"][0, k * 2 * P:(k + 1) * 2 * P, :].rearrange("(k p) n -> p k n", p=P), slice(0, SLOT), 2

        def load_chunk(sp, chunk):
            src, cols, parts = source(*chunk)
            dst = slot(chunk)[:, cols]
            if parts:
                dst = dst.rearrange("p (k n) -> p k n", k=parts)
            if AFTER[chunk] > 0:
                sp.wait_ge(sem("ring_freed"), AFTER[chunk])
            sp.dma_start(dst, src).then_inc(sem(f"landed{SLOT_OF[chunk]}"), 16)

        def max_no(u, c):
            return sum(2 if k == "d" else 1 for k, _, _ in UNITS[:u]) + c + 1

        MAIN, OVER = "", "over_"

        def moe(name, which):
            return sem(which + name)

        def mine(i):
            return slice(CAP * i, CAP * i + CAP)

        def freed_by(n, i, which):
            return n * len(PAIR) + ((N_FRONT if which == MAIN else SLOTS) + i + 1)

        def pair_slot(i):
            return (N_FRONT + i) % SLOTS

        def load_most(eng):
            wait_read(eng, "rank")
            return eng.value_load(most_i[0:1, 0:1], min_val=0, max_val=T)

        def pair_loads(sp, n, pair, which):
            for i, (kind, k, second) in enumerate(PAIR):
                src, cols, parts = source(kind, k, pair * 2 + second)
                s = pair_slot(i)
                dst = ring[:, s, cols]
                if parts:
                    dst = dst.rearrange("p (k n) -> p k n", k=parts)
                sp.wait_ge(moe("ring_freed", which),
                           n * len(PAIR) + ((N_FRONT if which == MAIN else SLOTS) + i + 1 - SLOTS))
                sp.dma_start(dst, src).then_inc(moe(f"landed{s}", which), 16)

        def sp_overflow(sp):
            count_ = load_most(sp)
            for r in range(1, ROUNDS):
                with sp.If(count_ > r * CAP):
                    sp.wait_ge(sem("ring_freed"), N_FRONT + N_MOE)
                    with sp.Fori(0, PAIRS) as pair:
                        pair_loads(sp, pair + (r - 1) * PAIRS, pair, OVER)
                    sp.wait_ge(moe("ring_freed", OVER), SLOTS + r * N_MOE)
            return count_

        def pair_landed(pe, n, i, which):
            before = (N_FRONT + i) // SLOTS if which == MAIN else i // SLOTS
            pe.wait_ge(moe(f"landed{pair_slot(i)}", which), (n * 2 + (before + 1)) * 16)

        def gather(pe, n, which, y_read):
            pe.wait_ge(moe("sel_ready", which), n + 1)
            if y_read is not None:
                pe.wait_ge(moe("y_added", which), y_read)
            for k in range(KD):
                for t in range(NT):
                    m = pe.matmul(banks[GATHER_BANKS[k // 4]][:, k % 4 * P:(k % 4 + 1) * P], hf[:, t, k * P:(k + 1) * P],
                                  sel[:, t, :], start=t == 0, stop=t == 1, skip_group_check=True)
            m.then_inc(moe("xt_full", which), 1)

        def hidden(pe, n, which):
            pe.wait_ge(moe("xt_read", which), n + 1)
            for k in range(KD):
                for i in range(2):
                    pair_landed(pe, n, 2 * k + i, which)
                for q, bank_no in enumerate(GATE_BANKS + UP_BANKS):
                    for i in range(2):
                        m = pe.matmul(banks[bank_no][mine(i), :], gathered[:, k, mine(i)],
                                      ring[:, pair_slot(2 * k + i), q * 512:(q + 1) * 512],
                                      start=k == 0, stop=k == KD - 1, skip_group_check=True)
                    if k == KD - 1 and q == 1:
                        m.then_inc(moe("gate_full", which), 1)
                m.then_inc(moe("ring_freed", which), 2)
                if k == 5:
                    pe.wait_ge(moe("b1_in", which), (n + 1) * 16)
                    for q, bank_no in enumerate(GATE_BANKS + UP_BANKS):
                        m = pe.matmul(banks[bank_no][:], pick, b1rows[:, q * 512:(q + 1) * 512],
                                      start=False, stop=False, skip_group_check=True)

        def pe_rest(pe, n, which, ahead):
            for half in range(2):
                pe.wait_ge(moe("gated", which), n * 2 + (half + 1))
                for j in range(4):
                    m = pe.transpose(banks[TURN_BANKS[half]][:, j * P:(j + 1) * P],
                                     us[:, half * 512 + j * P:half * 512 + (j + 1) * P], ident[:])
                m.then_inc(moe("turned", which), 1)
                if half == 0:
                    pe.wait_ge(moe("selg_ready", which), n + 1)
                    for t in range(NT):
                        m = pe.transpose(banks[SHARE_BANK][:, t * P:(t + 1) * P], selg[:, t, :], ident[:])
                    m.then_inc(moe("share_full", which), 1)
            for j in range(4):
                if j % 2 == 0:
                    pe.wait_ge(moe("act_read", which), n * 2 + (j // 2 + 1))
                for i in range(2):
                    pair_landed(pe, n, 2 * KD + 2 * j + i, which)
                for c in range(2):
                    for kk in range(2):
                        for i in range(2):
                            w = ring[:, pair_slot(2 * KD + 2 * j + i), :].rearrange("p (k n) -> p k n", k=2)
                            k = 2 * j + kk
                            m = pe.matmul(banks[OUT_BANKS[c]][mine(i), :], actT[:, k, mine(i)],
                                          w[:, kk, c * 512:(c + 1) * 512],
                                          start=k == 0, stop=k == KD - 1, skip_group_check=True)
                    if j == 3 and c == 0:
                        m.then_inc(moe("out_half", which), 1)
                m.then_inc(moe("ring_freed", which), 2)
                if j == 2:
                    pe.wait_ge(moe("b2_in", which), (n + 1) * 16)
                    for c in range(2):
                        pe.matmul(banks[OUT_BANKS[c]][:], pick, b2rows[:, c * 512:(c + 1) * 512],
                                  start=False, stop=False, skip_group_check=True)
            pe.wait_ge(moe("share_read", which), n + 1)
            pe.wait_ge(moe("xt_read", which), n + (1 + ahead))
            for q in range(4):
                t, c = divmod(q, 2)
                if q < 2:
                    pe.wait_ge(moe("out_read", which), n * 2 + (c + 1))
                else:
                    pe.wait_ge(moe("y_added", which), n * 4 + q)
                pe.matmul(banks[MIX_BANKS[c]][:], selgT[:, t * P:(t + 1) * P], out2[:, c * 512:(c + 1) * 512],
                          start=True, stop=True, skip_group_check=True).then_inc(moe("mixed", which), 1)

        def load_b1(act, n, pair, which):
            act.dma_start(b1rows, a["b1"][0, bass.ds(pair * 2, 2), :]).then_inc(moe("b1_in", which), 16)

        def load_b2(act, n, pair, which):
            act.dma_start(b2rows, a["b2"][0, bass.ds(pair * 2, 2), :]).then_inc(moe("b2_in", which), 16)

        def gather_out(act, n, which):
            act.wait_ge(moe("xt_full", which), n + 1)
            for j in range(2):
                m = act.activation(gathered[:, 4 * j:4 * j + 4, :],
                                   banks[GATHER_BANKS[j]][:].rearrange("p (k s) -> p k s", k=4), ACT.Copy)
            m.then_inc(moe("xt_read", which), 1)

        def sigmoids(act, n, which):
            for half in range(2):
                cols = slice(half * 512, half * 512 + 512)
                act.wait_ge(moe("gate_clipped", which), n * 2 + (half + 1))
                act.activation(sg[:, cols], gs[:, cols], ACT.Sigmoid, scale=ALPHA).then_inc(moe("sigmoid", which), 1)

        def act_rest(act, n, which):
            for half in range(2):
                act.wait_ge(moe("turned", which), n * 2 + (half + 1))
                act.activation(actT[:, 4 * half:4 * half + 4, :],
                               banks[TURN_BANKS[half]][:].rearrange("p (j s) -> p j s", j=4), ACT.Copy)\
                    .then_inc(moe("act_read", which), 1)
            act.wait_ge(moe("share_full", which), n + 1)
            act.activation(selgT, banks[SHARE_BANK][:, 0:T], ACT.Copy).then_inc(moe("share_read", which), 1)

        def select(dve, n, pair, which):
            for t in range(NT):
                for i in range(2):
                    m = dve.tensor_scalar(sel[:, t, mine(i)], iota_s, slots[:, t, bass.ds(pair * 2 + i, 1)], None,
                                          ALU.is_equal)
            m.then_inc(moe("sel_ready", which), 1)

        def dve_pair(dve, n, pair, which):
            for t in range(NT):
                for i in range(2):
                    m = dve.tensor_scalar(selg[:, t, mine(i)], iota_s, slots[:, t, bass.ds(pair * 2 + i, 1)],
                                          gates[:, t, bass.ds(pair * 2 + i, 1)], ALU.is_equal, ALU.mult)
            m.then_inc(moe("selg_ready", which), 1)
            dve.wait_ge(moe("gate_full", which), n + 1)
            for half in range(2):
                dve.tensor_scalar(gs[:, half * 512:half * 512 + 512], banks[GATE_BANKS[half]][:], LIMIT, None, ALU.min)\
                    .then_inc(moe("gate_clipped", which), 1)
            dve.wait_ge(moe("ring_freed", which), freed_by(n, 2 * KD - 1, which))
            for half in range(2):
                cols = slice(half * 512, half * 512 + 512)
                dve.tensor_scalar(us[:, cols], banks[UP_BANKS[half]][:], LIMIT, -LIMIT, ALU.min, ALU.max)\
                    .then_inc(moe("up_clipped", which), 1)
            for half in range(2):
                cols = slice(half * 512, half * 512 + 512)
                dve.wait_ge(moe("gate_clipped", which), n * 2 + (half + 1))
                dve.wait_ge(moe("up_clipped", which), n * 2 + (half + 1))
                dve.scalar_tensor_tensor(out=us[:, cols], in0=us[:, cols], scalar=1.0, in1=gs[:, cols],
                                         op0=ALU.add, op1=ALU.mult).then_inc(moe("up_gate", which), 1)
                dve.wait_ge(moe("up_gate", which), n * 2 + (half + 1))
                dve.wait_ge(moe("sigmoid", which), n * 2 + (half + 1))
                dve.tensor_tensor(us[:, cols], us[:, cols], sg[:, cols], ALU.mult).then_inc(moe("gated", which), 1)
            for c in range(2):
                if c == 0:
                    dve.wait_ge(moe("out_half", which), n + 1)
                else:
                    dve.wait_ge(moe("ring_freed", which), freed_by(n, len(PAIR) - 1, which))
                cols = slice(c * 512, c * 512 + 512)
                dve.tensor_tensor(out2[:, cols], banks[OUT_BANKS[c]][:], gf[:, cols], ALU.mult)\
                    .then_inc(moe("out_read", which), 1)
            for q in range(4):
                t, c = divmod(q, 2)
                dve.wait_ge(moe("mixed", which), n * 4 + (q + 1))
                cols = slice(c * 512, c * 512 + 512)
                dve.tensor_tensor(x2[:, t, cols], x2[:, t, cols], banks[MIX_BANKS[c]][:], ALU.add)\
                    .then_inc(moe("y_added", which), 1)

        block = ctx.enter_context(nc.Block())

        @block.sync
        def _(sp):
            for chunk in FRONT:
                load_chunk(sp, chunk)
            with sp.Fori(0, PAIRS) as pair:
                pair_loads(sp, pair, pair, MAIN)
            sp_overflow(sp)
            for chunk in BACK:
                load_chunk(sp, chunk)
            for t in range(NT):
                for c in range(2):
                    sp.wait_ge(sem("out_done"), 2 * t + c + 1)
                    sp.dma_start(out[0, t * P:(t + 1) * P, c * 512:(c + 1) * 512], x2[:, t, c * 512:(c + 1) * 512])\
                        .then_inc(sem("stored"), 16)
            sp.wait_ge(sem("stored"), 64)

        @block.gpsimd
        def _(pool):
            step = stepper(pool, "pool_link")
            step(pool.memset(ident[:], 0.0))
            step(pool.affine_select(out=ident[:], in_=ident[:], compare_op=ALU.not_equal, fill=1.0, base=0,
                                    pattern=[[-1, P]], channel_multiplier=1), "consts")
            step(pool.memset(ones[:], 1.0), "consts")
            step(pool.memset(cT[:], 0.0), "consts")
            step(pool.memset(mrows[:], 0.0), "consts")
            for t in range(3):
                for i in range(2):
                    src = a["b_ada"][0, t * SLOT:(t + 1) * SLOT].rearrange("(q n) -> q n", q=4)
                    pool.dma_start(mrows[i:97 + i:32, t, :], src).then_inc(sem("bada_in"), 16)
            pool.dma_start(rb[:], a["router_b"]).then_inc(sem("router_in"), 16)
            pool.wait_ge(sem("x1_done"), 4)
            step(pool.memset(below, 1.0))
            step(pool.affine_select(out=below, in_=below, compare_op=ALU.is_gt, fill=0.0, base=0,
                                    pattern=[[1, P]], channel_multiplier=-1), "below_done")
            step(pool.iota(iota_i, pattern=[[1, CAP]], base=0, channel_multiplier=0), "iota_done")
            step(pool.memset(pick, 1.0))
            step(pool.affine_select(out=pick, in_=pick, compare_op=ALU.is_gt, fill=0.0, base=1,
                                    pattern=[[1, P]], channel_multiplier=-CAP))
            step(pool.affine_select(out=pick, in_=pick, compare_op=ALU.is_gt, fill=0.0, base=CAP,
                                    pattern=[[-1, P]], channel_multiplier=CAP), "pick_done")
            wait_read(pool, "mixT0")
            pool.dma_start(rw, a["router_w"][0].rearrange("(k p) e -> p k e", p=P)).then_inc(sem("router_in"), 16)
            pool.wait_ge(sem("hf_done"), NT)
            for dst, name in ((final_w, "final_norm_w"), (ln1g, "ln1_g_2"), (ln1b, "ln1_b_2")):
                src = a[name] if name != "final_norm_w" else a[name].rearrange("(a n) -> a n", a=1)
                pool.dma_start(dst, src.broadcast_to([P, D])).then_inc(sem("norm_in"), 16)
            pool.dma_start(w_pool, a["w_pool_2"][0].rearrange("g c d -> c g d")).then_inc(sem("mix_in"), 16)
            pool.dma_start(p_tok, a["p_2"][0, 0].rearrange("(t p) c -> p t c", p=P)).then_inc(sem("mix_in"), 16)
            pool.dma_start(neg_dist, a["neg_dist"]).then_inc(sem("mix_in"), 16)
            pool.dma_start(sinks, a["attn_sinks_2"].broadcast_to([P, QH])).then_inc(sem("mix_in"), 16)
            wait_read(pool, "logits")
            pool.dma_start(bands, a["pool_bands"].rearrange("g (k p) t -> p g k t", p=P)).then_inc(sem("mix_in"), 16)
            pool.wait_ge(sem("moe_done"), 1)
            pool.dma_start(ln2g, a["ln2_g_2"].broadcast_to([P, D])).then_inc(sem("norm2_in"), 16)
            pool.dma_start(ln2b, a["ln2_b_2"].broadcast_to([P, D])).then_inc(sem("norm2_in"), 16)
            pool.dma_start(b_gate, a["b_ple_gate_2"].broadcast_to([P, D])).then_inc(sem("b_gate_in"), 16)

        @block.scalar
        def _(act):
            step = stepper(act, "act_link")

            def load(dst, src, name, inc=16):
                act.dma_start(dst, src).then_inc(sem(name), 16)

            load(small[0:8, :], a["c"][0].rearrange("(r n) -> r n", n=P), "c_in")
            load(small[8:16, :], a["c_ctx"].rearrange("(r n) -> r n", n=P), "c_in")
            load(small[16:24, :], a["attn_norm_w"][0].rearrange("(r n) -> r n", n=P), "c_in")
            load(small[24:26, :], a["q_norm_w"][0].rearrange("(r n) -> r n", n=P), "c_in")
            load(small[26:27, :], a["kv_norm_w"][0].rearrange("(r n) -> r n", n=P), "c_in")
            load(small[27:28, :], a["subln_w"][0].rearrange("(r n) -> r n", n=P), "c_in")
            load(small[28:32, :], a["pool_scale_2"][0].rearrange("(r n) -> r n", n=P), "c_in")
            load(xc[:, 0:2, :], a["ctx"][0].rearrange("(t p) d -> p t d", p=P), "ctx_in")
            load(xc[:, 2:4, :], a["x"][0].rearrange("(t p) d -> p t d", p=P), "x_in")
            for n, name in enumerate(("lambda_q1", "lambda_k1", "lambda_q2", "lambda_k2")):
                load(lamv[:, n, :], a[name].broadcast_to([P, 64]), "lam_in")
            load(rope_cos[:], a["rope_cos"].rearrange("(t p) c -> p t c", p=P), "rope_in")
            load(rope_sin[:], a["rope_sin"].rearrange("(t p) c -> p t c", p=P), "rope_in")
            load(bc[:, 2, :], a["ffn_norm_w"].broadcast_to([P, D]), "ffnw_in")

            act.wait_ge(sem("c_in"), 16 * 7)
            step(act.activation(csig[:], small[0:16, :], ACT.Sigmoid), "csig_done")
            act.wait_ge(sem("ctx_in"), 16)
            for t in range(4):
                if t == 2:
                    act.wait_ge(sem("x_in"), 16)
                step(act.activation(sq[:], xc[:, t, :], ACT.Square, accum_out=stat[:, t:t + 1]), "ss_done")
            act.wait_ge(sem("ms_done"), 1)
            step(act.activation(stat[:, 8:12], stat[:, 4:8], ACT.Sqrt), "root_done")
            act.wait_ge(sem("lam_sums"), 1)
            step(act.activation(lam[:, 2:4], lam[:, 0:2], ACT.Exp), "lam_exp")

            for t in range(4):
                for c in ((1, 2, 3) if t < 2 else (0, 1, 2, 3)):
                    if c == 2:
                        step(act.activation(dv[:, t, :], take(act, f"proj{t}_2")[:], ACT.Copy), tile=f"proj{t}_2")
                    elif c == 1 and t < 2:
                        step(act.activation(dk[:, t, :], take(act, f"proj{t}_1")[:], ACT.Copy), tile=f"proj{t}_1")
            act.wait_ge(sem("lat_ms"), 1)
            step(act.activation(stat[:, 24:30], stat[:, 18:24], ACT.Sqrt), "lat_root")
            for h in range(H):
                b = take(act, f"dkT{h}")
                step(act.activation(dkT[:, h, :], b[:], ACT.Copy), tile=f"dkT{h}")
            for j in range(2):
                b = take(act, f"dqT{j}")
                step(act.activation(dqT[:, 2 * j:2 * j + 2, :], b[:].rearrange("p (h t) -> p h t", h=2),
                                    ACT.Copy, scale=DIFF_SCALE), tile=f"dqT{j}")
            for j in range(2):
                b = take(act, f"qnope{j}")
                if j == 0:
                    act.wait_ge(sem("hT_done"), KD)
                    act.wait_ge(full("hT7"), use("hT7") + 1)
                step(act.activation(qnT[:, 2 * j:2 * j + 2, :], b[:].rearrange("p (h t) -> p h t", h=2),
                                    ACT.Copy, scale=MLA_SCALE), tile=f"qnope{j}")
            act.wait_ge(full("proj3_3"), use("proj3_3") + 1)
            for h in range(H):
                b = take(act, f"knope{h}")
                step(act.activation(knT[:, h, :], b[:], ACT.Copy), tile=f"knope{h}")

            for what, u in attention_order(len(UNITS)):
                kind, h, t = UNITS[u]
                if what == "score":
                    for c in range(2 if kind == "d" else 1):
                        b = take(act, f"s{u}_{c}")
                        act.wait_ge(sem("neg_max"), max_no(u, c))
                        if u >= 2 and c == 0:
                            act.wait_ge(full(f"pT{u - 2}"), use(f"pT{u - 2}") + 1)
                        step(act.activation(prob[:, u % 2, c, :], b[:], ACT.Exp, bias=psum_sum[:, u, c:c + 1],
                                            accum_out=psum_sum[:, u, 2 + c:3 + c]), tile=f"s{u}_{c}")
                elif what == "turn":
                    b = take(act, f"pT{u}")
                    if u >= 2:
                        act.wait_ge(full(f"av{u - 2}"), use(f"av{u - 2}") + 1)
                    step(act.activation(probT[:, u % 2, :], b[:], ACT.Copy), tile=f"pT{u}")
            act.wait_ge(sem("sub_ms"), 1)
            step(act.activation(stat[:, 48:56], stat[:, 40:48], ACT.Sqrt), "sub_root")
            for j in (2, 3):
                b = take(act, f"mixT{j}")
                step(act.activation(mixT[:, 2 * j:2 * j + 2, :], b[:].rearrange("p (k t) -> p k t", k=2), ACT.Copy),
                     tile=f"mixT{j}")
            for t in range(NT):
                act.wait_ge(sem("x1_done"), 2 * t + 2)
                step(act.activation(xn[:, 0, :], xc[:, 2 + t, :], ACT.Square, accum_out=stat[:, t:t + 1]), "ss2_done")
            act.wait_ge(sem("ms2_done"), 1)
            step(act.activation(stat[:, 4:6], stat[:, 2:4], ACT.Sqrt), "root2_done")
            for j in range(4):
                b = take(act, f"hfT{j}")
                step(act.activation(hfT[:, 2 * j:2 * j + 2, :], b[:].rearrange("p (k t) -> p k t", k=2), ACT.Copy),
                     tile=f"hfT{j}")
            for t in range(NT):
                act.wait_ge(sem("top_done"), t + 1)
                step(act.activation(topx[:, t, 4:8], top[:, t, 0:TOP_K], ACT.Exp, bias=topx[:, t, 0:1],
                                    accum_out=topx[:, t, 1:2]), "topx_done")

            gather_out(act, 0, MAIN)
            with act.Fori(0, PAIRS) as pair:
                load_b1(act, pair, pair, MAIN)
                sigmoids(act, pair, MAIN)
                gather_out(act, pair + 1, MAIN)
                load_b2(act, pair, pair, MAIN)
                act_rest(act, pair, MAIN)
            most_act = load_most(act)
            with act.Fori(1, ROUNDS) as r:
                with act.If(most_act > r * CAP):
                    with act.Fori(0, PAIRS) as pair:
                        n = (r - 1) * PAIRS + pair
                        load_b1(act, n, pair, OVER)
                        gather_out(act, n, OVER)
                        sigmoids(act, n, OVER)
                        load_b2(act, n, pair, OVER)
                        act_rest(act, n, OVER)

            act.wait_ge(sem("moe_used"), 1)
            step(act.activation(xn[:, 0, :], x2[:, 0, :], ACT.Square, accum_out=stat[:, 0:1]), "ss3_done")
            act.wait_ge(sem("ms3_done"), 1)
            step(act.activation(stat[:, 4:6], stat[:, 2:4], ACT.Sqrt), "root3_done")

            def transposed(name, dst, k, scale=1.0):
                b = take(act, name)
                step(act.activation(dst, b[:].rearrange("p (k t) -> p k t", k=k), ACT.Copy, scale=scale), tile=name)

            def rounded(name, dst, k=2):
                b = take(act, name)
                step(act.activation(dst.bitcast(F32R), b[:].rearrange("p (k t) -> p k t", k=k), ACT.Copy), "tile_rounded",
                     wait=False)

            for n in range(ROUNDED - 1):
                round_weights(act, n)
            for j in range(4):
                rounded(f"xT{j}", x_hi[:, 2 * j:2 * j + 2, :])
            for n in range(ROUNDED - 1, 8):
                round_weights(act, n)
            for t in range(NT):
                b = take(act, f"in{t}_0")
                step(act.activation(u_tok[:, t, :], b[:], ACT.Copy), tile=f"in{t}_0")
                b = take(act, f"in{t}_1")
                step(act.activation(q_tok[:, t, :], b[:], ACT.Copy), tile=f"in{t}_1")
            transposed("kT", k2T, 2)
            transposed("qT0", q2T[:, 0:2, :], 2, HD ** -0.5)
            transposed("qT1", q2T[:, 2:4, :], 2, HD ** -0.5)
            transposed("pd0", pool_dT[:, 0:2, :], 2)
            transposed("pd1", pool_dT[:, 2:4, :], 2)
            for what, u in attention_order(len(UNITS2)):
                h, blk = UNITS2[u]
                w = (blk + 1) * P
                if what == "score":
                    act.wait_ge(sem("masked"), u + 1)
                    step(act.activation(prob2[:, u % 2, 0:w], prob2[:, u % 2, 0:w], ACT.Exp, bias=soft[:, u, 1:2],
                                        accum_out=soft[:, u, 2:3]))
                    step(act.activation(soft[:, u, 3:4], sinks[:, h:h + 1], ACT.Exp, bias=soft[:, u, 1:2]), "exp2_done")
                    if u in (3, 6, 9, 12):
                        round_weights(act, 7 + u // 3)
                elif what == "turn":
                    b = take(act, f"tw{u}")
                    step(act.activation(prob2T[:, u % 2, 0:w], b[:, 0:w], ACT.Copy), tile=f"tw{u}")
            rounded("oT0", x_hi[:, 4:6, :])
            rounded("oT1", x_hi[:, 6:8, :])
            for t in range(NT):
                act.wait_ge(sem("var1"), t + 1)
                step(act.activation(stat[:, 16 + t:17 + t], stat[:, 12 + t:13 + t], ACT.Sqrt), "root4_done")
                if t == 0:
                    for n in range(12, 15):
                        round_weights(act, n)
            transposed("plT", pT, 2)
            for j in range(4):
                rounded(f"h1T{j}", x_hi[:, 2 * j:2 * j + 2, :])
            for j in range(16):
                b = take(act, f"part{j}")
                if j >= 2:
                    act.wait_ge(sem("wide_done"), j - 1)
                step(act.activation(wide[:, j % 2, :], b[:], ACT.Relu), tile=f"part{j}")
                act.wait_ge(sem("squared"), j + 1)
                if j >= 2:
                    act.wait_ge(sem("wide_used"), j - 1)
                step(act.activation(wide_hi[:, j % 2, :].bitcast(F32R), wide[:, j % 2, :], ACT.Copy), "wide_rounded",
                     wait=False)
                for n in splits_at(j):
                    round_weights(act, n)
            for n in range(44, 47):
                round_weights(act, n)
            for t in range(NT):
                act.wait_ge(sem("var2"), t + 1)
                step(act.activation(stat[:, 26 + t:27 + t], stat[:, 22 + t:23 + t], ACT.Sqrt), "root5_done")
                if t == 0:
                    round_weights(act, 47)
            for j in range(4):
                rounded(f"h2T{j}", x_hi[:, 2 * j:2 * j + 2, :])
            for n in range(4):
                act.wait_ge(sem("gate_in"), n + 1)
                step(act.activation(gate_z[:, n, :], gate_z[:, n, :], ACT.Sigmoid), "gate_done")

        @block.vector
        def _(dve):
            step = stepper(dve, "dve_link")
            V = nc.vector

            dve.wait_ge(sem("csig_done"), 1)
            step(V.tensor_tensor(small[0:16, :], small[0:16, :], csig[:], ALU.mult), "silu_done")
            b = take(dve, "smallT")
            dve.wait_ge(sem("consts"), 3)
            step(V.tensor_copy(cT[:, :, 0:2], b[:, 0:16].rearrange("p (i k) -> p k i", i=2)))
            step(V.tensor_copy(vecT[:], b[:, 16:32]), tile="smallT")

            dve.wait_ge(sem("ss_done"), 4)
            step(V.tensor_scalar(stat[:, 4:8], stat[:, 0:4], 1.0 / D, EPS, ALU.mult, ALU.add), "ms_done")
            dve.wait_ge(sem("lam_in"), 64)
            for n in range(2):
                step(V.tensor_tensor_reduce(lamv[:, 2 * n, :], lamv[:, 2 * n, :], lamv[:, 2 * n + 1, :], 1.0, 0.0,
                                            ALU.mult, ALU.add, lam[:, n:n + 1]), "lam_sums" if n else None)
            dve.wait_ge(sem("root_done"), 1)
            step(V.reciprocal(stat[:, 12:16], stat[:, 8:12]))
            for t in range(4):
                step(V.tensor_scalar(xn[:, t, :], xc[:, t, :], stat[:, 12 + t:13 + t], None, ALU.mult), "xn_done",
                     wait=t == 3)
            dve.wait_ge(sem("lam_exp"), 1)
            step(V.tensor_tensor(lam[:, 4:5], lam[:, 3:4], lam[:, 2:3], ALU.subtract))
            step(V.tensor_scalar(lam[:, 5:6], lam[:, 4:5], -LAM_INIT, None, ALU.add))

            b = take(dve, "ada0")
            dve.wait_ge(sem("bada_in"), 96)
            step(V.tensor_tensor(mrows[:, 0, :], b[:], mrows[:, 0, :], ALU.add), tile="ada0")
            b = take(dve, "modT")[:].rearrange("p (b q r) -> p r q b", b=4, q=4)
            for i in range(2):
                step(V.tensor_copy(modT[:, i, :].rearrange("p (q b) -> p q b", q=4), b[:, i]),
                     tile="modT" if i else None)
            for i in range(2):
                step(V.scalar_tensor_tensor(out=scol[:, i, :], in0=modT[:, i, 8:16], scalar=1.0, in1=vecT[:, 0:8],
                                            op0=ALU.add, op1=ALU.mult))
            for k in range(KD):
                b = take(dve, f"hT{k}")
                step(V.tensor_scalar(hT[:, k, 0:T], b[:, 0:T], scol[:, 1, k:k + 1], modT[:, 1, k:k + 1],
                                     ALU.mult, ALU.add), "hT_done", wait=False)
                step(V.tensor_scalar(hT[:, k, T:KEYS], b[:, T:KEYS], scol[:, 0, k:k + 1], modT[:, 0, k:k + 1],
                                     ALU.mult, ALU.add), tile=f"hT{k}")

            def rotate(dst, src, t, n, last):
                w = n * 64
                cos = rope_cos[:, t, :].unsqueeze(1).broadcast_to([P, n, 64])
                step(V.tensor_tensor(ropet[:, 0, 0:w].rearrange("p (n c) -> p n c", n=n),
                                     src.rearrange("p (n c) -> p n c", n=n), cos, ALU.mult))
                s = src.rearrange("p (n f c) -> p n f c", f=2, c=16)
                r = ropet[:, 1, 0:w].rearrange("p (n f c) -> p n f c", f=2, c=16)
                for half in range(2):
                    for axis in range(2):
                        sin = rope_sin[:, t, axis * 16:axis * 16 + 16].unsqueeze(1).broadcast_to([P, n, 16])
                        step(V.tensor_tensor(r[:, axis::2, half, :], s[:, axis::2, 1 - half, :], sin, ALU.mult),
                             wait=half == 1 and axis == 1)
                o0 = ropet[:, 0, 0:w].rearrange("p (n f c) -> p n f c", f=2, c=16)
                d = dst.rearrange("p (n f c) -> p n f c", f=2, c=16)
                step(V.tensor_tensor(d[:, :, 0, :], o0[:, :, 0, :], r[:, :, 0, :], ALU.subtract))
                step(V.tensor_tensor(d[:, :, 1, :], o0[:, :, 1, :], r[:, :, 1, :], ALU.add), **last)

            dve.wait_ge(sem("rope_in"), 32)
            for t in range(4):
                for c in ((1, 3) if t < 2 else (0, 1, 3)):
                    name = f"proj{t}_{c}"
                    b = take(dve, name)
                    if c == 3:
                        at = 0 if t < 2 else Q_RANK
                        if t >= 2:
                            step(V.tensor_copy(cq[:, t - 2, :], b[:, 0:Q_RANK]))
                        step(V.tensor_copy(ckv[:, t, :], b[:, at:at + KV_RANK]))
                        krs = b[:, at + KV_RANK:at + KV_RANK + ROPE]
                        if t < 2:
                            step(V.tensor_copy(kr[:, t, 0, :], krs), tile=name)
                        else:
                            rotate(kr[:, t, 0, :], krs, t - 2, 1, {"tile": name})
                        step(V.tensor_copy(kr[:, t, 1, :], kr[:, t, 0, :]), "kr_done")
                    elif t >= 2:
                        rotate((dq[:, t - 2, :] if c == 0 else dk[:, t, :]), b[:], t - 2, 8, {"tile": name})
            for t in range(4):
                step(V.tensor_tensor_reduce(sq[:, 0:KV_RANK], ckv[:, t, :], ckv[:, t, :], 1.0, 0.0, ALU.mult, ALU.add,
                                            stat[:, 12 + t:13 + t]))
            for t in range(2):
                step(V.tensor_tensor_reduce(sq[:, 0:Q_RANK], cq[:, t, :], cq[:, t, :], 1.0, 0.0, ALU.mult, ALU.add,
                                            stat[:, 16 + t:17 + t]))
            step(V.tensor_scalar(stat[:, 18:22], stat[:, 12:16], 1.0 / KV_RANK, EPS, ALU.mult, ALU.add))
            step(V.tensor_scalar(stat[:, 22:24], stat[:, 16:18], 1.0 / Q_RANK, EPS, ALU.mult, ALU.add), "lat_ms")
            dve.wait_ge(sem("lat_root"), 1)
            step(V.reciprocal(stat[:, 30:36], stat[:, 24:30]))
            for t in range(4):
                step(V.tensor_scalar(ckv[:, t, :], ckv[:, t, :], stat[:, 30 + t:31 + t], None, ALU.mult), "lat_done")
            for t in range(2):
                step(V.tensor_scalar(cq[:, t, :], cq[:, t, :], stat[:, 34 + t:35 + t], None, ALU.mult), "lat_done")
            b = take(dve, "ckvT")
            step(V.tensor_scalar(ckvT, b[:], vecT[:, 10:11], None, ALU.mult), tile="ckvT")
            b = take(dve, "krT")
            step(V.tensor_copy(krT, b[:]), tile="krT")
            b = take(dve, "cqT")
            for k in range(2):
                step(V.tensor_scalar(cqT[:, k, :], b[:, k * T:(k + 1) * T], vecT[:, 8 + k:9 + k], None, ALU.mult),
                     tile="cqT" if k else None)
            b = take(dve, "qrope")
            for t in range(NT):
                rotate(qr[:, t, :], b[:, t * 256:(t + 1) * 256], t, H, {"tile": "qrope"} if t else {})
            for t in range(4):
                b = take(dve, f"mv{t}")
                step(V.tensor_copy(mv[:, t, :], b[:]), tile=f"mv{t}")
            b = take(dve, "qrT")
            step(V.tensor_scalar(qrT, b[:].rearrange("p (j t) -> p j t", j=2), MLA_SCALE, None, ALU.mult), tile="qrT")

            for what, u in attention_order(len(UNITS)):
                kind, h, t = UNITS[u]
                if what == "score":
                    for c in range(2 if kind == "d" else 1):
                        b = take(dve, f"s{u}_{c}")
                        step(V.tensor_reduce(psum_sum[:, u, c:c + 1], b[:], AX, ALU.max, negate=True), "neg_max")
                elif what == "turn":
                    continue
                else:
                    b = take(dve, f"av{u}")
                    at = h * P + (0 if kind == "d" else 512)
                    step(V.tensor_scalar(o[:, t, at:at + P], b[:, 0:P], psum_sum[:, u, 4:5], None, ALU.mult),
                         tile=f"av{u}")
                if what == "score":
                    last = f"s{u}_1" if kind == "d" else f"s{u}_0"
                    wait_read(dve, f"s{u}_0")
                    wait_read(dve, last)
                    step(V.reciprocal(psum_sum[:, u, 4:6] if kind == "d" else psum_sum[:, u, 4:5],
                                      psum_sum[:, u, 2:4] if kind == "d" else psum_sum[:, u, 2:3]),
                         "pmix_done" if kind == "m" else None)
                    if kind == "d":
                        step(V.scalar_tensor_tensor(out=psum_sum[:, u, 6:7], in0=psum_sum[:, u, 5:6],
                                                    scalar=psum_sum[:, u, 2:3], in1=lam[:, 5:6],
                                                    op0=ALU.mult, op1=ALU.mult))
                        step(V.scalar_tensor_tensor(out=prob[:, u % 2, 0, :], in0=prob[:, u % 2, 1, :],
                                                    scalar=psum_sum[:, u, 6:7], in1=prob[:, u % 2, 0, :],
                                                    op0=ALU.mult, op1=ALU.add), "pmix_done")
                if what == "value" and u == 3:
                    for i in (1, 2):
                        b = take(dve, f"ada{i}")
                        step(V.tensor_tensor(mrows[:, i, :], b[:], mrows[:, i, :], ALU.add), tile=f"ada{i}")
                    for n in range(8):
                        b = take(dve, f"bc{n}")
                        dst = bc[:, n // 2, (n % 2) * 512:(n % 2) * 512 + 512]
                        if n // 2 == 2:
                            dve.wait_ge(sem("ffnw_in"), 16)
                            step(V.scalar_tensor_tensor(out=dst, in0=b[:], scalar=1.0,
                                                        in1=dst,
                                                        op0=ALU.add, op1=ALU.mult), tile=f"bc{n}")
                        else:
                            step(V.tensor_copy(dst, b[:]), tile=f"bc{n}")

            for t in range(NT):
                for h in range(H):
                    n = t * H + h
                    step(V.tensor_tensor_reduce(sq[:, 0:P], o[:, t, h * P:(h + 1) * P], o[:, t, h * P:(h + 1) * P],
                                                1.0, 0.0, ALU.mult, ALU.add, stat[:, 32 + n:33 + n]))
            step(V.tensor_scalar(stat[:, 40:48], stat[:, 32:40], 1.0 / P, EPS, ALU.mult, ALU.add), "sub_ms")
            dve.wait_ge(sem("sub_root"), 1)
            step(V.reciprocal(stat[:, 56:64], stat[:, 48:56]))
            for t in range(NT):
                for h in range(H):
                    n = t * H + h
                    step(V.tensor_scalar(o[:, t, h * P:(h + 1) * P], o[:, t, h * P:(h + 1) * P],
                                         stat[:, 56 + n:57 + n], None, ALU.mult), "sub_done")
            step(V.tensor_scalar(vecT[:, 11:12], vecT[:, 11:12], 1.0 - LAM_INIT, None, ALU.mult))
            for j in range(2):
                b = take(dve, f"mixT{j}")
                step(V.tensor_scalar(mixT[:, 2 * j:2 * j + 2, :], b[:].rearrange("p (k t) -> p k t", k=2),
                                     vecT[:, 11:12], None, ALU.mult), tile=f"mixT{j}")
            for t in range(NT):
                for n in range(2):
                    cols = slice(n * 512, n * 512 + 512)
                    b = take(dve, f"wo{t}_{n}")
                    step(V.tensor_tensor(sq[:, 0:512], b[:], bc[:, 0, cols], ALU.mult), tile=f"wo{t}_{n}")
                    step(V.tensor_tensor(xc[:, 2 + t, cols], xc[:, 2 + t, cols], sq[:, 0:512], ALU.add), "x1_done")

            dve.wait_ge(sem("ss2_done"), 2)
            step(V.tensor_scalar(stat[:, 2:4], stat[:, 0:2], 1.0 / D, EPS, ALU.mult, ALU.add), "ms2_done")
            dve.wait_ge(sem("root2_done"), 1)
            step(V.reciprocal(stat[:, 6:8], stat[:, 4:6]))
            for t in range(NT):
                step(V.scalar_tensor_tensor(out=hf[:, t, :], in0=xc[:, 2 + t, :], scalar=stat[:, 6 + t:7 + t],
                                            in1=bc[:, 2, :], op0=ALU.mult, op1=ALU.mult))
                step(V.tensor_tensor(hf[:, t, :], hf[:, t, :], bc[:, 1, :], ALU.add), "hf_done")

            dve.wait_ge(sem("iota_done"), 1)
            step(V.tensor_copy(iota_s, iota_i))
            step(V.tensor_copy(iota_e[:], iota_i[:, 0:E]))
            step(V.memset(gates[:], 0.0))
            step(V.memset(slots[:], -1.0))
            b = take(dve, "logits")
            step(V.tensor_copy(logit[:], b[:, 0:NT * E].rearrange("p (t e) -> p t e", t=NT)), tile="logits")
            for t in range(NT):
                step(V.max(top[:, t, :], logit[:, t, :]))
                step(V.tensor_scalar(topx[:, t, 0:1], top[:, t, 0:1], -1.0, None, ALU.mult), "top_done")
                step(V.max_index(top_at[:, t, :], top[:, t, :], logit[:, t, :]))
            step(V.tensor_copy(top_atf[:], top_at[:]))
            for t in range(NT):
                dve.wait_ge(sem("topx_done"), t + 1)
                step(V.reciprocal(topx[:, t, 2:3], topx[:, t, 1:2]))
                step(V.tensor_scalar(gate4[:, t, :], topx[:, t, 4:8], topx[:, t, 2:3], None, ALU.mult))
                for k in range(TOP_K):
                    step(V.tensor_scalar(hot[:, t, k, :], iota_e[:], top_atf[:, t, k:k + 1], gate4[:, t, k:k + 1],
                                         ALU.is_equal, ALU.mult))
                step(V.tensor_reduce(gates[:, t, 0:E], hot[:, t].rearrange("p k e -> p e k"), AX, ALU.add))
                for k in range(TOP_K):
                    step(V.tensor_scalar(hot[:, t, k, :], iota_e[:], top_atf[:, t, k:k + 1], None, ALU.is_equal))
                step(V.tensor_reduce(chosen[:, t, :], hot[:, t].rearrange("p k e -> p e k"), AX, ALU.add), "chosen_done")
            b = take(dve, "rank")
            for t in range(NT):
                step(V.scalar_tensor_tensor(out=slots[:, t, 0:E], in0=b[:, t * E:(t + 1) * E], scalar=1.0,
                                            in1=chosen[:, t, :], op0=ALU.add, op1=ALU.mult))
                step(V.tensor_scalar(slots[:, t, 0:E], slots[:, t, 0:E], -1.0, None, ALU.add))
            step(V.tensor_reduce(most[:, 0:1], b[:, 2 * E:3 * E], AX, ALU.max))
            step(V.tensor_copy(most_i[:], most[:, 0:1]), tile="rank")
            dve.sem_inc(moe("y_added", MAIN), 1)
            dve.sem_inc(moe("y_added", OVER), 1)
            select(dve, 0, 0, MAIN)
            with dve.Fori(0, PAIRS) as pair:
                dve.wait_ge(moe("xt_full", MAIN), pair + 1)
                select(dve, pair + 1, pair + 1, MAIN)
                dve_pair(dve, pair, pair, MAIN)
            most_dve = load_most(dve)
            with dve.Fori(1, ROUNDS) as r:
                with dve.If(most_dve > r * CAP):
                    V.tensor_scalar(iota_s, iota_s, float(CAP), None, ALU.add).then_inc(moe("next_round", OVER), 1)
                    with dve.Fori(0, PAIRS) as pair:
                        n = (r - 1) * PAIRS + pair
                        dve.wait_ge(moe("next_round", OVER), r)
                        select(dve, n, pair, OVER)
                        dve_pair(dve, n, pair, OVER)

            dve.wait_ge(sem("moe_used"), 1)
            step(V.tensor_tensor_reduce(xn[:, 1, :], x2[:, 1, :], x2[:, 1, :], 1.0, 0.0, ALU.mult, ALU.add, stat[:, 1:2]))
            dve.wait_ge(sem("ss3_done"), 1)
            step(V.tensor_scalar(stat[:, 2:4], stat[:, 0:2], 1.0 / D, EPS, ALU.mult, ALU.add), "ms3_done")
            dve.wait_ge(sem("root3_done"), 1)
            step(V.reciprocal(stat[:, 6:8], stat[:, 4:6]))
            dve.wait_ge(sem("norm_in"), 48)
            for half in range(2):
                for t in range(NT):
                    cols = slice(half * 512, half * 512 + 512)
                    step(V.scalar_tensor_tensor(out=x2[:, t, cols], in0=x2[:, t, cols], scalar=stat[:, 6 + t:7 + t],
                                                in1=final_w[:, cols], op0=ALU.mult, op1=ALU.mult), "x2_done", wait=False)
            def rest_of(name, dst, hi, k=2):
                b = take(dve, name)
                count["rests"] = count.get("rests", 0) + 1
                dve.wait_ge(sem("tile_rounded"), count["rests"])
                step(V.tensor_tensor(dst.bitcast(F32R), b[:].rearrange("p (k t) -> p k t", k=k), hi, ALU.subtract),
                     tile=name)

            rest_of_weights(dve, 0)
            rest_of_weights(dve, 1)
            rest_of_weights(dve, 2)
            for j in range(4):
                rest_of(f"xT{j}", x_lo[:, 2 * j:2 * j + 2, :], x_hi[:, 2 * j:2 * j + 2, :])
            for n in range(ROUNDED - 1, 8):
                rest_of_weights(dve, n)
            for t in range(NT):
                b = take(dve, f"in{t}_2")
                for i in range(2):
                    step(V.tensor_copy(k_tok[:, t, :, i, :], b[:, 0:P].rearrange("p (h c) -> p h c", h=KVH)))
                step(V.tensor_copy(v_tok[:, t, :], b[:, P:2 * P]), tile=f"in{t}_2")
            dve.wait_ge(sem("mix_in"), 80)
            for j in range(2):
                b = take(dve, f"py{j}")
                for i in range(2):
                    g = 2 * j + i
                    src = b[:, i * T:(i + 1) * T]
                    step(V.tensor_scalar(x_hi[:, g, :].bitcast(F32R), src, vecT[:, 12 + g:13 + g], None, ALU.mult))
                    step(V.scalar_tensor_tensor(out=x_lo[:, g, :].bitcast(F32R), in0=src, scalar=vecT[:, 12 + g:13 + g],
                                                in1=x_hi[:, g, :], op0=ALU.mult, op1=ALU.subtract),
                         tile=f"py{j}" if i else None)
            for what, u in attention_order(len(UNITS2)):
                h, blk = UNITS2[u]
                w = (blk + 1) * P
                if what == "score":
                    b = take(dve, f"sw{u}")
                    if u >= 2:
                        dve.wait_ge(full(f"tw{u - 2}"), use(f"tw{u - 2}") + 1)
                    step(V.scalar_tensor_tensor(out=prob2[:, u % 2, 0:w], in0=neg_dist[:, 2 * P - w:2 * P],
                                                scalar=SLOPES[h], in1=b[:, 0:w], op0=ALU.mult, op1=ALU.add),
                         tile=f"sw{u}")
                    step(V.tensor_reduce(soft[:, u, 0:1], prob2[:, u % 2, 0:w], AX, ALU.max))
                    step(V.tensor_scalar(soft[:, u, 1:2], soft[:, u, 0:1], sinks[:, h:h + 1], -1.0, ALU.max, ALU.mult),
                         "masked")
                    if u in (4, 7, 10, 13):
                        rest_of_weights(dve, 7 + u // 3)
                elif what == "value":
                    step(V.tensor_tensor(soft[:, u, 4:5], soft[:, u, 2:3], soft[:, u, 3:4], ALU.add))
                    step(V.reciprocal(soft[:, u, 5:6], soft[:, u, 4:5]))
                    b = take(dve, f"vw{u}")
                    step(V.tensor_scalar(o2[:, blk, h * HD:(h + 1) * HD], b[:, 0:HD], soft[:, u, 5:6], None, ALU.mult),
                         tile=f"vw{u}")

            for j in range(2):
                rest_of(f"oT{j}", x_lo[:, 4 + 2 * j:6 + 2 * j, :], x_hi[:, 4 + 2 * j:6 + 2 * j, :])

            def layer_norm(t, tiles, at, var, root, g, b_, done):
                for c in range(2):
                    cols = slice(c * 512, c * 512 + 512)
                    bk = take(dve, f"{tiles}{t}_{c}")
                    step(V.scalar_tensor_tensor(out=x2[:, t, cols], in0=x2[:, t, cols], scalar=DEEPNORM, in1=bk[:],
                                                op0=ALU.mult, op1=ALU.add), tile=f"{tiles}{t}_{c}")
                    step(V.bn_stats(bn[:, t, c, :], x2[:, t, cols]))
                step(V.bn_aggr(stat[:, 40 + 2 * t:42 + 2 * t], bn[:, t, :, :].rearrange("p c s -> p (c s)")))
                step(V.tensor_scalar(stat[:, at + t:at + t + 1], stat[:, 41 + 2 * t:42 + 2 * t], LN_EPS, None, ALU.add),
                     var)
                for c in range(2):
                    cols = slice(c * 512, c * 512 + 512)
                    step(V.scalar_tensor_tensor(out=x2[:, t, cols], in0=x2[:, t, cols], scalar=stat[:, 40 + 2 * t:41 + 2 * t],
                                                in1=g[:, cols], op0=ALU.subtract, op1=ALU.mult))
                    if c == 0:
                        dve.wait_ge(sem(root), t + 1)
                        step(V.reciprocal(stat[:, at + 8 + t:at + 9 + t], stat[:, at + 4 + t:at + 5 + t]))
                    step(V.scalar_tensor_tensor(out=x2[:, t, cols], in0=x2[:, t, cols], scalar=stat[:, at + 8 + t:at + 9 + t],
                                                in1=b_[:, cols], op0=ALU.mult, op1=ALU.add), done)

            layer_norm(0, "wo2", 12, "var1", "root4_done", ln1g, ln1b, "h1_done")
            rest_of_weights(dve, 12)
            rest_of_weights(dve, 13)
            layer_norm(1, "wo2", 12, "var1", "root4_done", ln1g, ln1b, "h1_done")
            for j in range(4):
                rest_of(f"h1T{j}", h_lo[:, 2 * j:2 * j + 2, :], x_hi[:, 2 * j:2 * j + 2, :])
            rest_of_weights(dve, 14)
            for j in range(16):
                wait_read(dve, f"part{j}")
                step(V.tensor_tensor(wide[:, j % 2, :], wide[:, j % 2, :], wide[:, j % 2, :], ALU.mult), "squared")
                dve.wait_ge(sem("wide_rounded"), j + 1)
                step(V.tensor_tensor(wide_lo[:, j % 2, :].bitcast(F32R), wide[:, j % 2, :], wide_hi[:, j % 2, :],
                                     ALU.subtract), "wide_done")
                for n in splits_at(j):
                    rest_of_weights(dve, n)
            for n in range(44, 47):
                rest_of_weights(dve, n)
            dve.wait_ge(sem("norm2_in"), 32)
            for t in range(NT):
                layer_norm(t, "wide", 22, "var2", "root5_done", ln2g, ln2b, "h2_done")
            for j in range(4):
                rest_of(f"h2T{j}", h_lo[:, 2 * j:2 * j + 2, :], x_hi[:, 2 * j:2 * j + 2, :])
            rest_of_weights(dve, 47)
            dve.wait_ge(sem("b_gate_in"), 16)
            for n in range(5):
                if n < 4:
                    t, c = divmod(n, 2)
                    b = take(dve, f"gate{t}_{c}")
                    step(V.tensor_tensor(gate_z[:, n, :], b[:], b_gate[:, c * 512:(c + 1) * 512], ALU.add), "gate_in",
                         wait=False)
                if n >= 1:
                    t, c = divmod(n - 1, 2)
                    cols = slice(c * 512, c * 512 + 512)
                    dve.wait_ge(sem("gate_done"), n)
                    b = take(dve, f"ple{t}_{c}")
                    step(V.tensor_tensor(gate_z[:, n - 1, :], gate_z[:, n - 1, :], b[:], ALU.mult))
                    step(V.tensor_tensor(x2[:, t, cols], x2[:, t, cols], gate_z[:, n - 1, :], ALU.add), "out_done")

        @block.tensor
        def _(pe):
            def mm(out_, lhsT, rhs, first, last):
                return pe.matmul(out_, lhsT, rhs, start=first, stop=last, skip_group_check=True)

            def mm3(out_, lhsT, rhs, first, last):
                (ah, al), (bh, bl) = lhsT, rhs
                mm(out_, ah, bh, first, False)
                mm(out_, ah, bl, False, False)
                return mm(out_, al, bh, False, last)

            freed = sem("ring_freed")

            pe.wait_ge(sem("consts"), 4)
            pe.wait_ge(sem("silu_done"), 1)
            b = claim(pe, "smallT")
            pe.transpose(b[:, 0:32], small[:], ident[0:32, 0:32]).then_inc(full("smallT"), 1)

            def ada(t):
                name = f"ada{t}"
                b = claim(pe, name)
                for k in range(KD):
                    n = (name, k)
                    ring_wait(pe, n)
                    for q in range(4):
                        m = mm(b[32 * q:32 * q + 32, :], cT[:, k, :], slot(n)[:, q * 512:(q + 1) * 512],
                               k == 0, k == KD - 1)
                    if k < KD - 1:
                        m.then_inc(freed, 1)
                m.then_inc(full(name), 1)
                pe.wait_ge(full(name), use(name) + 1)
                pe.sem_inc(freed, 1)

            wait_read(pe, "smallT")
            ada(0)
            wait_read(pe, "ada0")
            b = claim(pe, "modT")
            for blk in range(4):
                m = pe.transpose(b[:, blk * P:(blk + 1) * P], mrows[:, 0, blk * P:(blk + 1) * P], ident[:])
            m.then_inc(full("modT"), 1)
            pe.wait_ge(sem("xn_done"), 4)
            for k in range(KD):
                b = claim(pe, f"hT{k}")
                for t in range(4):
                    m = pe.transpose(b[:, t * P:(t + 1) * P], xn[:, t, k * P:(k + 1) * P], ident[:])
                m.then_inc(full(f"hT{k}"), 1)

            wait_read(pe, "hT7")
            pe.wait_ge(sem("hT_done"), KD)
            for t in range(4):
                for c in ((1, 2, 3) if t < 2 else (0, 1, 2, 3)):
                    lo = 512 * c if c < 3 else (CKV if t < 2 else CQ)
                    hi = 512 * (c + 1) if c < 3 else IN_COLS
                    b = claim(pe, f"proj{t}_{c}")
                    for k in range(KD):
                        n = ("w_in", k)
                        if t == 0 and c == 1:
                            ring_wait(pe, n)
                        m = mm(b[:, 0:hi - lo], hT[:, k, t * P:(t + 1) * P], slot(n)[:, lo:hi], k == 0, k == KD - 1)
                    m.then_inc(full(f"proj{t}_{c}"), 1)
            pe.wait_ge(full("proj3_3"), use("proj3_3") + 1)
            pe.sem_inc(freed, KD)

            pe.wait_ge(sem("lat_done"), 6)
            b = claim(pe, "ckvT")
            for t in range(4):
                m = pe.transpose(b[:, t * P:(t + 1) * P], ckv[:, t, :], ident[:])
            m.then_inc(full("ckvT"), 1)
            pe.wait_ge(sem("kr_done"), 4)
            b = claim(pe, "krT")
            for t in range(4):
                m = pe.transpose(b[:, t * P:(t + 1) * P], kr[:, t, :, :].rearrange("p a c -> p (a c)"), ident[:])
            m.then_inc(full("krT"), 1)
            b = claim(pe, "cqT")
            for k in range(2):
                for t in range(NT):
                    m = pe.transpose(b[:, k * T + t * P:k * T + (t + 1) * P], cq[:, t, k * P:(k + 1) * P], ident[:])
            m.then_inc(full("cqT"), 1)
            wait_read(pe, "proj0_1")
            wait_read(pe, "proj1_1")
            wait_read(pe, "proj2_1")
            wait_read(pe, "proj3_1")
            for h in range(H):
                b = claim(pe, f"dkT{h}")
                for t in range(4):
                    m = pe.transpose(b[:, t * P:(t + 1) * P], dk[:, t, h * P:(h + 1) * P], ident[:])
                m.then_inc(full(f"dkT{h}"), 1)
            wait_read(pe, "proj2_0")
            wait_read(pe, "proj3_0")
            for j in range(2):
                b = claim(pe, f"dqT{j}")
                for hh in range(2):
                    for t in range(NT):
                        h = 2 * j + hh
                        m = pe.transpose(b[:, hh * T + t * P:hh * T + (t + 1) * P], dq[:, t, h * P:(h + 1) * P], ident[:])
                m.then_inc(full(f"dqT{j}"), 1)

            nq = ("w_uq", 0)
            ring_wait(pe, nq)
            wq = slot(nq)[:, 0:2 * 768].rearrange("p (k h c) -> p k h c", k=2, h=H)
            wait_read(pe, "cqT")
            b = claim(pe, "qrope")
            for t in range(NT):
                for k in range(2):
                    m = mm(b[:, t * 256:(t + 1) * 256], cqT[:, k, t * P:(t + 1) * P], wq[:, k, :, NOPE:NOPE + ROPE],
                           k == 0, k == 1)
            m.then_inc(full("qrope"), 1)
            for j in range(2):
                b = claim(pe, f"qnope{j}")
                for hh in range(2):
                    for k in range(2):
                        m = mm(b[:, hh * T:(hh + 1) * T], wq[:, k, 2 * j + hh, 0:NOPE], cqT[:, k, :], k == 0, k == 1)
                m.then_inc(full(f"qnope{j}"), 1)
            pe.wait_ge(full("qnope1"), use("qnope1") + 1)
            pe.sem_inc(freed, 1)
            nk = ("w_ukv", 0)
            ring_wait(pe, nk)
            wkv = slot(nk)[:, 0:1024].rearrange("p (h c) -> p h c", h=H)
            wait_read(pe, "ckvT")
            for h in range(H):
                b = claim(pe, f"knope{h}")
                mm(b[:], wkv[:, h, 0:NOPE], ckvT, True, True).then_inc(full(f"knope{h}"), 1)
            for t in range(4):
                b = claim(pe, f"mv{t}")
                m = mm(b[:], ckvT[:, t * P:(t + 1) * P], wkv[:, :, NOPE:2 * NOPE], True, True)
                m.then_inc(full(f"mv{t}"), 1)
            pe.wait_ge(full("mv3"), use("mv3") + 1)
            pe.sem_inc(freed, 1)
            wait_read(pe, "qrope")
            b = claim(pe, "qrT")
            for j in range(2):
                for t in range(NT):
                    m = pe.transpose(b[:, j * T + t * P:j * T + (t + 1) * P], qr[:, t, j * P:(j + 1) * P], ident[:])
            m.then_inc(full("qrT"), 1)

            for what, u in attention_order(len(UNITS)):
                kind, h, t = UNITS[u]
                if what == "score" and kind == "d":
                    if u == 0:
                        for x in ("dkT3", "dqT1", "proj3_2", "proj2_2", "proj1_2", "proj0_2"):
                            wait_read(pe, x)
                    for c in range(2):
                        b = claim(pe, f"s{u}_{c}")
                        rows = slice(64 * c, 64 * c + 64)
                        mm(b[:], dqT[rows, h, t * P:(t + 1) * P], dkT[rows, h, :], True, True)\
                            .then_inc(full(f"s{u}_{c}"), 1)
                elif what == "score":
                    if UNITS[u - 1][0] == "d":
                        for x in ("knope3", "qnope1", "krT", "qrT", "mv3"):
                            wait_read(pe, x)
                    b = claim(pe, f"s{u}_0")
                    rows = slice(64 * (h % 2), 64 * (h % 2) + 64)
                    mm(b[:], qnT[:, h, t * P:(t + 1) * P], knT[:, h, :], True, False)
                    mm(b[:], qrT[rows, h // 2, t * P:(t + 1) * P], krT[rows, :], False, True)\
                        .then_inc(full(f"s{u}_0"), 1)
                elif what == "turn":
                    pe.wait_ge(sem("pmix_done"), u + 1)
                    b = claim(pe, f"pT{u}")
                    for n in range(4):
                        m = pe.transpose(b[:, n * P:(n + 1) * P], prob[:, u % 2, 0, n * P:(n + 1) * P], ident[:])
                    m.then_inc(full(f"pT{u}"), 1)
                else:
                    wait_read(pe, f"pT{u}")
                    b = claim(pe, f"av{u}")
                    vals = dv if kind == "d" else mv
                    for n in range(4):
                        m = mm(b[:, 0:P], probT[:, u % 2, n * P:(n + 1) * P], vals[:, n, h * P:(h + 1) * P],
                               n == 0, n == 3)
                    m.then_inc(full(f"av{u}"), 1)
                if what == "value" and u == 3:
                    ada(1)
                    ada(2)
                    wait_read(pe, "ada1")
                    wait_read(pe, "ada2")
                    for n, (third, q) in enumerate(((1, 0), (1, 1), (1, 2), (1, 3), (2, 0), (2, 1), (2, 2), (2, 3))):
                        b = claim(pe, f"bc{n}")
                        mm(b[:], ones[32 * q:32 * q + 1, :], mrows[32 * q:32 * q + 1, third, :], True, True)\
                            .then_inc(full(f"bc{n}"), 1)

            for j in range(4):
                if j == 0:
                    pe.wait_ge(sem("sub_done"), 8)
                b = claim(pe, f"mixT{j}")
                for kk in range(2):
                    for t in range(NT):
                        k = 2 * j + kk
                        m = pe.transpose(b[:, kk * T + t * P:kk * T + (t + 1) * P], o[:, t, k * P:(k + 1) * P], ident[:])
                m.then_inc(full(f"mixT{j}"), 1)
            bw = {(t, n): claim(pe, f"wo{t}_{n}") for t in range(NT) for n in range(2)}
            for j in range(4):
                n_ = ("w_out", j)
                ring_wait(pe, n_)
                wait_read(pe, f"mixT{j}")
                w = slot(n_).rearrange("p (k n) -> p k n", k=2)
                for t in range(NT):
                    for n in range(2):
                        for kk in range(2):
                            k = 2 * j + kk
                            m = mm(bw[t, n][:], mixT[:, k, t * P:(t + 1) * P], w[:, kk, n * 512:(n + 1) * 512],
                                   k == 0, k == KD - 1)
                        if j == 3:
                            m.then_inc(full(f"wo{t}_{n}"), 1)
                        elif t == 1 and n == 1:
                            m.then_inc(freed, 1)

            pe.wait_ge(sem("hf_done"), NT)
            for j in range(4):
                b = claim(pe, f"hfT{j}")
                for kk in range(2):
                    for t in range(NT):
                        k = 2 * j + kk
                        m = pe.transpose(b[:, kk * T + t * P:kk * T + (t + 1) * P], hf[:, t, k * P:(k + 1) * P], ident[:])
                m.then_inc(full(f"hfT{j}"), 1)
            pe.wait_ge(full("wo1_1"), use("wo1_1") + 1)
            pe.sem_inc(freed, 1)
            pe.wait_ge(sem("router_in"), 32)
            b = claim(pe, "logits")
            for j in range(4):
                wait_read(pe, f"hfT{j}")
            for t in range(NT):
                for k in range(KD):
                    mm(b[:, t * E:(t + 1) * E], hfT[:, k, t * P:(t + 1) * P], rw[:, k, :], k == 0, False)
                m = mm(b[:, t * E:(t + 1) * E], ones[0:1, :], rb[:], False, True)
            m.then_inc(full("logits"), 1)
            pe.wait_ge(sem("chosen_done"), NT)
            pe.wait_ge(sem("below_done"), 1)
            b = claim(pe, "rank")
            mm(b[:, 0:E], below, chosen[:, 0, :], True, True)
            mm(b[:, E:2 * E], ones[:], chosen[:, 0, :], True, False)
            mm(b[:, E:2 * E], below, chosen[:, 1, :], False, True)
            mm(b[:, 2 * E:3 * E], ones[:], chosen[:, 0, :], True, False)
            mm(b[:, 2 * E:3 * E], ones[:], chosen[:, 1, :], False, True).then_inc(full("rank"), 1)
            for name in FRONT_TILES[-8:]:
                wait_read(pe, name)

            pe.wait_ge(sem("pick_done"), 1)
            gather(pe, 0, MAIN, None)
            with pe.Fori(0, PAIRS) as pair:
                hidden(pe, pair, MAIN)
                gather(pe, pair + 1, MAIN, pair * 4 + 1)
                pe_rest(pe, pair, MAIN, 1)
            pe.wait_ge(moe("y_added", MAIN), 4 * PAIRS + 1)
            most_pe = load_most(pe)
            pe.sem_inc(moe("ring_freed", OVER), SLOTS)
            with pe.Fori(1, ROUNDS) as r:
                with pe.If(most_pe > r * CAP):
                    with pe.Fori(0, PAIRS) as pair:
                        n = (r - 1) * PAIRS + pair
                        gather(pe, n, OVER, n * 4 + 1)
                        hidden(pe, n, OVER)
                        pe_rest(pe, n, OVER, 0)
                        pe.wait_ge(moe("y_added", OVER), 4 * n + 5)

            pe.wait_ge(moe("mixed", MAIN), 4 * PAIRS)
            pe.sem_inc(sem("moe_used"), 1)
            pe.sem_inc(sem("moe_done"), 1)

            def turn_tokens(name, src, ready, by_tile=True):
                for j in range(4):
                    pe.wait_ge(sem(ready), NT + 1 + j // 2 if by_tile else NT * (1 + j // 2))
                    b = claim(pe, f"{name}{j}")
                    for kk in range(2):
                        for t in range(NT):
                            k = 2 * j + kk
                            m = pe.transpose(b[:, kk * T + t * P:kk * T + (t + 1) * P], src[:, t, k * P:(k + 1) * P], ident[:])
                    m.then_inc(full(f"{name}{j}"), 1)

            turn_tokens("xT", x2, "x2_done", False)
            parts = [(0, 512), (512, 1024), (1024, 1280)]
            bi = {(t, n): claim(pe, f"in{t}_{n}") for t in range(NT) for n in range(3)}
            for k in range(KD):
                w = split_weights(pe, ("w_in2", k))
                wait_read(pe, f"xT{k // 2}")
                for t in range(NT):
                    for n, (lo, hi) in enumerate(parts):
                        m = mm3(bi[t, n][:, 0:hi - lo], [v[:, k, t * P:(t + 1) * P].bitcast(F32R) for v in (x_hi, x_lo)],
                                [v[:, lo:hi] for v in w], k == 0, k == KD - 1)
                        if k == KD - 1:
                            m.then_inc(full(f"in{t}_{n}"), 1)
                if k < KD - 1:
                    m.then_inc(freed, 1)
            wait_read(pe, "in1_2")
            pe.sem_inc(freed, 1)
            wait_read(pe, "in0_2")
            b = claim(pe, "kT")
            for h in range(KVH):
                for t in range(NT):
                    m = pe.transpose(b[:, h * T + t * P:h * T + (t + 1) * P],
                                     k_tok[:, t, h].rearrange("p a c -> p (a c)"), ident[:])
            m.then_inc(full("kT"), 1)
            wait_read(pe, "in0_1")
            wait_read(pe, "in1_1")
            for j in range(2):
                b = claim(pe, f"qT{j}")
                for i in range(2):
                    for t in range(NT):
                        k = 2 * j + i
                        m = pe.transpose(b[:, i * T + t * P:i * T + (t + 1) * P], q_tok[:, t, k * P:(k + 1) * P], ident[:])
                m.then_inc(full(f"qT{j}"), 1)
            wait_read(pe, "in0_0")
            wait_read(pe, "in1_0")
            pe.wait_ge(sem("mix_in"), 80)
            for j in range(2):
                b = claim(pe, f"pd{j}")
                for i in range(2):
                    g = 2 * j + i
                    for t in range(NT):
                        m = mm(b[:, i * T:(i + 1) * T], u_tok[:, t, g * P:(g + 1) * P], bands[:, g, t, :], t == 0, t == 1)
                m.then_inc(full(f"pd{j}"), 1)
            for j in range(2):
                wait_read(pe, f"pd{j}")
                b = claim(pe, f"py{j}")
                for i in range(2):
                    g = 2 * j + i
                    m = mm(b[:, i * T:(i + 1) * T], w_pool[:, g, :], pool_dT[:, g, :], True, True)
                m.then_inc(full(f"py{j}"), 1)
            wait_read(pe, "kT")
            wait_read(pe, "qT1")
            for what, u in attention_order(len(UNITS2)):
                h, blk = UNITS2[u]
                w = (blk + 1) * P
                rows = slice(64 * (h % 2), 64 * (h % 2) + 64)
                if what == "score":
                    b = claim(pe, f"sw{u}")
                    mm(b[:, 0:w], q2T[rows, h // 2, blk * P:(blk + 1) * P], k2T[rows, h // 4, 0:w], True, True)\
                        .then_inc(full(f"sw{u}"), 1)
                elif what == "turn":
                    pe.wait_ge(sem("exp2_done"), u + 1)
                    b = claim(pe, f"tw{u}")
                    for n in range(blk + 1):
                        m = pe.transpose(b[:, n * P:(n + 1) * P], prob2[:, u % 2, n * P:(n + 1) * P], ident[:])
                    m.then_inc(full(f"tw{u}"), 1)
                else:
                    wait_read(pe, f"tw{u}")
                    b = claim(pe, f"vw{u}")
                    kv = (h // 4) * HD
                    for n in range(blk + 1):
                        m = mm(b[:, 0:HD], prob2T[:, u % 2, n * P:(n + 1) * P], v_tok[:, n, kv:kv + HD], n == 0, n == blk)
                    m.then_inc(full(f"vw{u}"), 1)
            for j in range(2):
                for u in ((2 * (4 * j + 3) + 1, 2 * (4 * j + 3))):
                    wait_read(pe, f"vw{u}")
                b = claim(pe, f"oT{j}")
                for i in range(2):
                    for t in range(NT):
                        k = 2 * j + i
                        m = pe.transpose(b[:, i * T + t * P:i * T + (t + 1) * P], o2[:, t, k * P:(k + 1) * P], ident[:])
                m.then_inc(full(f"oT{j}"), 1)

            def by_pairs(kind, tiles, src, ready, by_tile=False):
                bw = {(t, n): claim(pe, f"{tiles}{t}_{n}") for t in range(NT) for n in range(2)}
                order = ([(t, n, j) for t in range(NT) for n in range(2) for j in range(4)] if by_tile else
                         [(t, n, j) for t in range(NT) for j in range(4) for n in range(2)])
                for t, n, j in order:
                    if t == 0 and n == 0:
                        for name in ready(j):
                            wait_read(pe, name)
                    w = [v.rearrange("p (k n) -> p k n", k=2) for v in split_weights(pe, (kind, j))]
                    for kk in range(2):
                        k = 2 * j + kk
                        m = mm3(bw[t, n][:], [v[:, k, t * P:(t + 1) * P].bitcast(F32R) for v in src],
                                [v[:, kk, n * 512:(n + 1) * 512] for v in w], k == 0, k == KD - 1)
                    if j == 3:
                        m.then_inc(full(f"{tiles}{t}_{n}"), 1)
                    elif t == 1 and n == 1:
                        m.then_inc(freed, 1)

            by_pairs("w_out2", "wo2", (x_hi, x_lo), lambda j: [["py0"], ["py1"], ["oT0"], ["oT1"]][j])
            b = claim(pe, "plT")
            for k in range(2):
                for t in range(NT):
                    m = pe.transpose(b[:, k * T + t * P:k * T + (t + 1) * P], p_tok[:, t, k * P:(k + 1) * P], ident[:])
            m.then_inc(full("plT"), 1)
            wait_read(pe, "wo21_1")
            pe.sem_inc(freed, 1)
            turn_tokens("h1T", x2, "h1_done")
            sums = {(t, c): claim(pe, f"wide{t}_{c}") for t in range(NT) for c in range(2)}

            def wide_part(j):
                if j == 0:
                    for i in range(4):
                        wait_read(pe, f"h1T{i}")
                w = [v.rearrange("p (k n) -> p k n", k=KD) for v in split_weights(pe, ("ff1", j))]
                b = claim(pe, f"part{j}")
                for i in range(2):
                    for k in range(KD):
                        m = mm3(b[:, i * T:(i + 1) * T], [v[:, k, i * P:(i + 1) * P] for v in w],
                                [v[:, k, :].bitcast(F32R) for v in (x_hi, h_lo)], k == 0, k == KD - 1)
                m.then_inc(full(f"part{j}"), 1)

            def wide_sum(j):
                pe.wait_ge(sem("wide_done"), j + 1)
                w = [v.rearrange("p (k n) -> p k n", k=2) for v in split_weights(pe, ("ff2", j))]
                for t in range(NT):
                    for c in range(2):
                        for kk in range(2):
                            at = kk * T + t * P
                            m = mm3(sums[t, c][:], [v[:, j % 2, at:at + P].bitcast(F32R) for v in (wide_hi, wide_lo)],
                                    [v[:, kk, c * 512:(c + 1) * 512] for v in w], j == 0 and kk == 0, j == 15 and kk == 1)
                        if j == 15:
                            m.then_inc(full(f"wide{t}_{c}"), 1)
                        elif t == 0 and c == 0:
                            m.then_inc(freed, 1)
                        elif t == 1 and c == 0:
                            m.then_inc(sem("wide_last"), 1)
                        elif t == 1 and c == 1:
                            m.then_inc(sem("wide_used"), 1)

            wide_part(0)
            for j in range(16):
                if j < 15:
                    wide_part(j + 1)
                wide_sum(j)
                if j < 15:
                    pe.wait_ge(sem("wide_used"), j + 1)
                    pe.sem_inc(freed, 1)
            pe.wait_ge(full("wide1_1"), use("wide1_1") + 1)
            pe.sem_inc(freed, 2)

            ring_wait(pe, ("w_ple", 0))
            wait_read(pe, "plT")
            w = slot(("w_ple", 0)).rearrange("p (k n) -> p k n", k=2)
            for t in range(NT):
                for c in range(2):
                    b = claim(pe, f"ple{t}_{c}")
                    for k in range(2):
                        m = mm(b[:], pT[:, k, t * P:(t + 1) * P], w[:, k, c * 512:(c + 1) * 512], k == 0, k == 1)
                    m.then_inc(full(f"ple{t}_{c}"), 1)
            turn_tokens("h2T", x2, "h2_done")
            by_pairs("gate", "gate", (x_hi, h_lo), lambda j: [f"h2T{j}"], by_tile=True)


INPUTS = [
    "x", "c", "ctx", "c_ctx", "w_ada", "b_ada", "attn_norm_w", "w_in", "q_norm_w", "kv_norm_w", "w_uq", "w_ukv",
    "lambda_q1", "lambda_k1", "lambda_q2", "lambda_k2", "subln_w", "w_out", "ffn_norm_w", "router_w", "router_b",
    "w1", "b1", "w2", "b2", "final_norm_w", "p_2", "w_in_2", "w_pool_2", "pool_scale_2", "attn_sinks_2", "w_out_2",
    "ln1_g_2", "ln1_b_2", "w_ff1_2", "w_ff2_2", "ln2_g_2", "ln2_b_2", "w_ple_2", "w_ple_gate_2", "b_ple_gate_2",
]


def shape_tables():
    import numpy as np

    pairs, grid_w = 16, 64
    row = np.repeat(np.arange(T // grid_w, dtype=np.float32), grid_w)
    col = np.tile(np.arange(grid_w, dtype=np.float32), T // grid_w)
    inv = (np.float32(10000.0) ** (-np.arange(pairs, dtype=np.float32) / np.float32(pairs))).astype(np.float32)
    ang = np.stack([row[:, None] * inv, col[:, None] * inv], axis=1).astype(np.float32)
    cos = np.cos(ang).astype(np.float32)
    sin = np.sin(ang).astype(np.float32)
    dist = np.arange(P)[:, None] + P - np.arange(2 * P)[None, :]
    neg_dist = np.where((dist >= 0) & (dist < P), -dist, -1e32).astype(np.float32)
    pool_bands = np.zeros((4, T, T), np.float32)
    for g, w in enumerate((2, 4, 8, 16)):
        for t in range(T):
            lo = max(t + 1 - w, 0)
            pool_bands[g, lo:t + 1, t] = np.float32(1.0) / np.float32(t + 1 - lo)
            pool_bands[g, t, t] -= np.float32(1.0)
    return {
        "rope_cos": np.ascontiguousarray(np.concatenate([cos, cos], axis=2).reshape(T, 64)),
        "rope_sin": np.ascontiguousarray(sin.reshape(T, 32)),
        "neg_dist": neg_dist,
        "pool_bands": pool_bands,
    }


def kernel(**inputs):
    import numpy as np
    import concourse.bacc as bacc
    from concourse.bass_utils import run_bass_kernel_spmd as run

    nc = bacc.Bacc("TRN2", target_bir_lowering=False, num_devices=1)
    arrays, args = {}, {}
    tables = shape_tables()
    for name in INPUTS + list(tables):
        v = np.ascontiguousarray(inputs[name] if name in inputs else tables[name])
        arrays[f"in_{name}"] = v
        args[name] = nc.dram_tensor(f"in_{name}", v.shape, mybir.dt.from_np(v.dtype), kind="ExternalInput").ap()
    out = nc.dram_tensor("out", (1, T, D), F32, kind="ExternalOutput").ap()
    build(nc, args, out)
    return run(nc, [arrays], core_ids=[0]).results[0]["out"]
```

```python
from contextlib import ExitStack

import concourse.bass as bass
from concourse import mybir

F32 = mybir.dt.float32
F32R = mybir.dt.float32r
I32 = mybir.dt.int32
U32 = mybir.dt.uint32
ALU = mybir.AluOpType
ACT = mybir.ActivationFunctionType
AX = mybir.AxisListType.X

P = 128
D = 1024
KD = D // P
T = 256
NT = T // P
EPS = 1e-6

H = 4
DQ, DK, DV, CQ, CKV, KR = 0, 512, 1024, 1536, 1792, 1920
IN_COLS = 1984
Q_RANK, KV_RANK, NOPE, ROPE = 256, 128, 128, 64
DIFF_SCALE = 64 ** -0.5
MLA_SCALE = (NOPE + ROPE) ** -0.5
LAM_INIT = 0.8 - 0.6
KEYS = 2 * T

E = 32
TOP_K = 4
FF = 1024
CAP = 64
ROUNDS = T // CAP
LIMIT = 7.0
ALPHA = 1.702

IN2 = 1280
LN_EPS = 1e-5
DEEPNORM = 2.0 ** 0.25
FF2 = 4096
QH, KVH, HD = 8, 2, 64
SLOPES = [2.0 ** (-8.0 * (h + 1) / QH) for h in range(QH)]

SLOTS = 12
SLOT = 2048

ADA0 = [("ada0", k) for k in range(KD)]
W_IN = [("w_in", k) for k in range(KD)]
MLA = [("w_uq", 0), ("w_ukv", 0)]
ADA12 = [(f"ada{t}", k) for t in (1, 2) for k in range(KD)]
W_OUT = [("w_out", j) for j in range(4)]
FRONT = ADA0 + W_IN + MLA + ADA12 + W_OUT
PAIRS = E // 2
PAIR = [("w1", k, i) for k in range(KD) for i in range(2)] + [("w2", j, i) for j in range(4) for i in range(2)]
N_FRONT = len(FRONT)
N_MOE = PAIRS * len(PAIR)
assert len(PAIR) == 2 * SLOTS
BACK = ([("w_in2", k) for k in range(KD)] + [("w_out2", j) for j in range(4)]
        + [("ff1", 0)] + [c for j in range(15) for c in (("ff1", j + 1), ("ff2", j))] + [("ff2", 15)]
        + [("w_ple", 0)] + [("gate", j) for j in range(4)])
CHUNK = {c: n for n, c in enumerate(FRONT)}
CHUNK.update({c: N_FRONT + N_MOE + n for n, c in enumerate(BACK)})

ROUNDED = 4
BACK_SLOTS = SLOTS - ROUNDED
SPLIT = [c for c in BACK if c[0] != "w_ple"]
N_BEFORE = N_FRONT + N_MOE
FREED_BY_PAIR = [(n % SLOTS, n) for n in range(N_BEFORE - SLOTS, N_BEFORE) if n % SLOTS < BACK_SLOTS]
SLOT_OF, USE_OF, AFTER = {}, {}, {}
for _c, _n in CHUNK.items():
    if _n < N_BEFORE:
        SLOT_OF[_c], USE_OF[_c], AFTER[_c] = _n % SLOTS, _n // SLOTS + 1, _n - SLOTS + 1
    else:
        _m = _n - N_BEFORE
        _s, _last = FREED_BY_PAIR[_m % BACK_SLOTS]
        SLOT_OF[_c], USE_OF[_c] = _s, _last // SLOTS + 1 + _m // BACK_SLOTS + 1
        AFTER[_c] = _last + 1

SPLIT_FROM = 2
N_PROJ = CHUNK[("w_in", KD - 1)] + 1
for _c, _n in CHUNK.items():
    if N_PROJ <= _n < N_PROJ + SLOTS - KD:
        AFTER[_c] = N_PROJ

FRONT_TILES = (
    ["cT"] + [f"hT{k}" for k in range(KD)] + ["vecT", "ada0", "modT"]
    + [f"proj{t}_{c}" for t in range(2) for c in (1, 2, 3)]
    + ["proj2_3", "proj3_3"] + [f"proj{t}_{c}" for t in (2, 3) for c in (0, 1, 2)]
    + [f"dkT{h}" for h in range(H)] + ["dqT0", "dqT1"] + ["ckvT", "krT", "cqT"]
    + ["qrope", "qnope0", "qnope1"] + [f"knope{h}" for h in range(H)] + [f"mv{t}" for t in range(4)] + ["qrT"]
)
UNITS = [("d", h, t) for h in range(H) for t in range(NT)] + [("m", h, t) for h in range(H) for t in range(NT)]


def attention_order(n_units):
    order = []
    for i in range(n_units + 2):
        if i < n_units:
            order.append(("score", i))
        if 1 <= i <= n_units:
            order.append(("turn", i - 1))
        if i >= 2:
            order.append(("value", i - 2))
    return order


for _what, _u in attention_order(len(UNITS)):
    if _what == "score":
        FRONT_TILES += [f"s{_u}_{c}" for c in range(2 if UNITS[_u][0] == "d" else 1)]
    else:
        FRONT_TILES.append(f"{'pT' if _what == 'turn' else 'av'}{_u}")
    if _what == "value" and _u == 3:
        FRONT_TILES += ["ada1", "ada2"] + [f"bc{n}" for n in range(8)]
FRONT_TILES += [f"mixT{j}" for j in range(4)] + [f"wo{t}_{n}" for t in range(NT) for n in range(2)]
FRONT_TILES += [f"hfT0_{j}" for j in range(4)] + ["logits"] + [f"hfT1_{j}" for j in range(4)] + ["rank"]

UNITS2 = [(h, b) for h in range(QH // 2) for b in range(NT)]

BACK_TILES = [f"xT{j}" for j in range(4)] + [f"in{t}_{n}" for t in range(NT) for n in range(3)]
BACK_TILES += ["kT", "qT0", "qT1", "pd0", "pd1", "py0", "py1"]
for _what, _u in attention_order(len(UNITS2)):
    BACK_TILES += {"score": [f"sw{_u}_0", f"sw{_u}_1"], "turn": [f"tw{_u}"], "value": [f"vw{_u}"]}[_what]
BACK_TILES += ["oT0", "oT1"] + [f"wo2{t}_{n}" for t in range(NT) for n in range(2)] + ["plT"]
BACK_TILES += [f"h1T{j}" for j in range(4)]


def place_tiles():
    held, at = [0] * 8, {}

    def put(name, bank):
        at[name] = (bank, held[bank])
        held[bank] += 1

    for part in (FRONT_TILES, BACK_TILES):
        for n, name in enumerate(part):
            put(name, n % 8)
    for n, name in enumerate([f"wide{t}_{c}" for t in range(NT) for c in range(2)]):
        put(name, n)
    for j in range(16):
        put(f"part{j}", 4 + j % 4)
    for n, name in enumerate([f"ple{t}_{c}" for t in range(NT) for c in range(2)] + [f"h2T{j}" for j in range(4)]):
        put(name, (n + 4) % 8)
    for n, name in enumerate([f"gate{t}_{c}" for t in range(NT) for c in range(2)]):
        put(name, n)
    return at


GATE_BANKS, UP_BANKS, GATHER_BANKS, OUT_BANKS = (0, 1), (2, 3), (4, 5), (6, 7)
TURN_BANKS, SHARE_BANK, MIX_BANKS = GATE_BANKS, UP_BANKS[0], GATHER_BANKS


def build(nc, a, out):
    with ExitStack() as ctx:
        address = {}

        def sb(name, shape, dt=F32):
            t = ctx.enter_context(nc.sbuf_tensor(name, shape, dt))
            size = 4
            for n in shape[1:]:
                size *= n
            address[name] = nc.sbuf_base - size
            return t

        def over(name, shape, place, skip=0):
            return nc.alloc_sbuf_tensor_at(name, shape, F32, offset=address[place] + 4 * skip)

        sems, count = {}, {}

        def sem(name):
            if name not in sems:
                sems[name] = ctx.enter_context(nc.semaphore(name))
                count[name] = 0
            return sems[name]

        banks = [ctx.enter_context(nc.psum_tensor(f"bank{i}", [P, 512], F32)) for i in range(8)]

        ring = sb("ring", [P, SLOTS, SLOT])
        ident = sb("ident", [P, P])
        ones = sb("ones", [P, P])
        xc = sb("xc", [P, 4, D])
        xn = sb("xn", [P, 4, D])
        hT = sb("hT", [P, KD, KEYS])
        small = sb("small", [48, P])
        csig = sb("csig", [16, P])
        cT = sb("cT", [P, KD, 32])
        vecT = sb("vecT", [P, 16])
        mrows = sb("mrows", [P, 3, 512])
        modT = sb("modT", [P, 2, 16])
        scol = sb("scol", [P, 2, KD])
        lamv = sb("lamv", [P, 4, 64])
        lam = sb("lam", [P, 8])
        rope_cos = sb("rope_cos", [P, NT, 64])
        rope_sin = sb("rope_sin", [P, NT, 32])
        stat = sb("stat", [P, 64])
        sq = sb("sq", [P, D])
        ropet = sq[:].rearrange("p (a c) -> p a c", a=2)
        dq = sb("dq", [P, NT, 512])
        dk = sb("dk", [P, 4, 512])
        dv = sb("dv", [P, 4, 512])
        cq = sb("cq", [P, NT, Q_RANK])
        ckv = sb("ckv", [P, 4, KV_RANK])
        kr = sb("kr", [P, 4, 2, ROPE])
        dkT = xc[:, 0:2, :].rearrange("p a (h k) -> p (a h) k", h=2)
        dqT = sb("dqT", [P, H, T])
        cqT = cq[:]
        ckvT = ckv[:].rearrange("p t c -> p (t c)")
        krT = kr[:].rearrange("p t a c -> p (t a c)")
        qnT = xn[:, 0, :].rearrange("p (h t) -> p h t", h=H)
        qrT = xn[:, 1, 0:512].rearrange("p (j t) -> p j t", j=2)
        qr = xn[:, 1, 512:1024].rearrange("p (t c) -> p t c", t=NT)
        knT = hT[:, 0:4, :]
        mv = hT[:, 4:8, :]
        prob = xn[:, 2:4, :].rearrange("p a (c k) -> p a c k", c=2)
        probT = dq[:]
        psum_sum = sb("psum_sum", [P, len(UNITS), 8])
        o = dk[:].rearrange("p (t a) c -> p t (a c)", t=NT)
        mixT = hT[:, 0:4, :].rearrange("p k (a t) -> p (k a) t", a=2)
        bc = sb("bc", [P, 4, D])

        hf = xn[:, 2:4, :]
        hfT = hT[:, 4:8, :].rearrange("p k (a t) -> p (k a) t", a=2)
        rw = xc[:, 1, 0:KD * E].rearrange("p (k e) -> p k e", k=KD)
        rb = sb("rb", [1, E])
        b2rows = xc[0:2, 0, :]
        logit = sb("logit", [P, NT, E])
        top = sb("top", [P, NT, 8])
        top_at = sb("top_at", [P, NT, 8], U32)
        top_atf = sb("top_atf", [P, NT, 8])
        topx = sb("topx", [P, NT, 8])
        gate4 = sb("gate4", [P, NT, TOP_K])
        hot = sq[:, 0:NT * TOP_K * E].rearrange("p (t k e) -> p t k e", t=NT, k=TOP_K)
        gates = sb("gates", [P, NT, E + 2])
        chosen = sb("chosen", [P, NT, E])
        slots = sb("slots", [P, NT, E + 2])
        iota_i = ropet[:, 1, 256:256 + CAP].bitcast(I32)
        iota_e = sb("iota_e", [P, E])
        iota_s = mrows[:, 0, P:P + CAP]
        below = mrows[:, 0, 0:P]
        most = sb("most", [P, 2])
        most_i = sb("most_i", [P, 1], I32)
        sel = xn[:, 0, 768:1024].rearrange("p (t s) -> p t s", t=NT)
        selg = xn[:, 0, 0:256].rearrange("p (t s) -> p t s", t=NT)
        gathered = xn[:, 1, :].rearrange("p (k s) -> p k s", k=KD)
        selgT = xn[:, 0, 512:768]
        b1rows = dv[0:2, :, :].rearrange("p t c -> p (t c)")
        pick = small[0:2, :]
        out2 = o[:, 0, :]
        gs = mrows[:, 1:3, :].rearrange("p a n -> p (a n)")
        us = o[:, 1, :]
        sg = sq[:]
        actT = dq[:].rearrange("p a (j s) -> p (a j) s", j=4)

        final_w, ln1g, ln1b, gf = (bc[:, n, :] for n in range(4))
        ln2g, ln2b = xc[:, 0, :], xc[:, 1, :]
        bands = hT[:, 4:8, :].rearrange("p g (k t) -> p g k t", k=NT)
        w_pool = cq[:].rearrange("p t (g c) -> p (t g) c", g=2)
        p_tok = ckv[:].rearrange("p (t a) c -> p t (a c)", t=NT)
        neg_dist = kr[:, 0:2, :, :].rearrange("p t a c -> p (t a c)")
        sinks = kr[:, 2, 0, 0:QH]
        b_gate = dv[:, 0:2, :].rearrange("p t c -> p (t c)")
        x2 = xc[:, 2:4, :]
        u_tok, q_tok = dk[:, 0:2, :], dk[:, 2:4, :]
        k_tok = dq[:, 0, :].rearrange("p (t h a c) -> p t h a c", t=NT, h=KVH, a=2)
        v_tok = dq[:, 1, 0:2 * KVH * HD].rearrange("p (t c) -> p t c", t=NT)
        pool_dT = xn[:, 0, :].rearrange("p (g t) -> p g t", g=4)
        q2T = xn[:, 1, :].rearrange("p (j t) -> p j t", j=4)
        k2T = sq[:, 0:KVH * T].rearrange("p (h t) -> p h t", h=KVH)
        prob2 = dv[:, 2:4, :]
        prob2T = [dq[:, 0, :], sq[:, 512:1024]]
        soft = psum_sum[:].rearrange("p (u a) c -> p u (a c)", a=2)
        o2 = u_tok
        wide = dk[:, 0:2, :]
        pT = sq[:, 512:1024].rearrange("p (k t) -> p k t", k=2)
        bn = sb("bn", [P, NT, 2, 6])
        w_hi = over("w_hi", [P, ROUNDED, SLOT], "ring", BACK_SLOTS * SLOT)
        w_lo = over("w_lo", [P, BACK_SLOTS, SLOT], "ring")
        first_spare = N_PROJ % SLOTS
        in_hi_a = over("in_hi_a", [P, SLOTS - KD, SLOT], "ring", first_spare * SLOT)
        in_hi_b = over("in_hi_b", [P, 2, SLOT], "bc")
        in_lo = {k: over(f"in_lo{k}", [P, SLOT], "ring", SLOT_OF["w_in", k] * SLOT) for k in range(SPLIT_FROM, KD)}
        tok_hi = over("tok_hi", [P, KD, KEYS], "xn")
        tok_lo = over("tok_lo", [P, KD, KEYS], "hT")
        x_hi = over("x_hi", [P, KD, T], "xn", 2 * D)
        x_lo = over("x_lo", [P, KD, T], "hT")
        h_lo = over("h_lo", [P, KD, T], "hT", 4 * KEYS)
        wide_hi = over("wide_hi", [P, 2, 512], "hT")
        wide_lo = over("wide_lo", [P, 2, 512], "hT", 2 * 512)
        gate_z = hT[:, 0:4, :]

        tile_at = place_tiles()

        def full(name):
            return sem(f"bank_full{tile_at[name][0]}")

        def drained(name):
            return sem(f"bank_drained{tile_at[name][0]}")

        def use(name):
            return tile_at[name][1]

        def bank(name):
            return banks[tile_at[name][0]]

        def claim(pe, name):
            if use(name):
                pe.wait_ge(drained(name), use(name))
            return bank(name)

        def take(eng, name):
            eng.wait_ge(full(name), use(name) + 1)
            return bank(name)

        def wait_read(eng, name):
            eng.wait_ge(drained(name), use(name) + 1)

        def stepper(eng, link):
            def step(ins, name=None, tile=None, wait=True):
                if tile is not None:
                    s, v = drained(tile), use(tile) + 1
                else:
                    s = sem(name or link)
                    count[name or link] += 1
                    v = count[name or link]
                ins.then_inc(s, 1)
                if wait:
                    eng.wait_ge(s, v)
            return step

        def ring_wait(eng, chunk):
            eng.wait_ge(sem(f"landed{SLOT_OF[chunk]}"), 16 * USE_OF[chunk])

        def slot(chunk):
            return ring[:, SLOT_OF[chunk], :]

        def used_wait(eng, chunk):
            kind, k = chunk
            if kind == "ff1":
                eng.wait_ge(full(f"part{k}"), use(f"part{k}") + 1)
            elif kind == "ff2" and k < 15:
                eng.wait_ge(sem("wide_used"), k + 1)
            elif chunk == ("ff2", 15):
                eng.wait_ge(full("wide1_1"), use("wide1_1") + 1)
            elif chunk == ("w_out2", 3):
                eng.wait_ge(full("wo21_1"), use("wo21_1") + 1)
            elif chunk == ("w_in2", 7):
                eng.wait_ge(full("in1_2"), use("in1_2") + 1)
            else:
                eng.wait_ge(sem("ring_freed"), CHUNK[chunk] + 1)

        def in_hi(k):
            n = k - SPLIT_FROM
            return in_hi_a[:, n, 0:IN_COLS] if n < SLOTS - KD else in_hi_b[:, n - (SLOTS - KD), 0:IN_COLS]

        def splits_at(j):
            return [SPLIT.index(c) for c in (("ff1", j + 2), ("ff2", j + 1)) if c in SPLIT]

        def width(kind):
            return IN2 if kind == "w_in2" else SLOT

        def round_weights(act, n):
            chunk = SPLIT[n]
            if n >= ROUNDED:
                used_wait(act, SPLIT[n - ROUNDED])
            ring_wait(act, chunk)
            w = width(chunk[0])
            act.activation(w_hi[:, n % ROUNDED, 0:w].bitcast(F32R), slot(chunk)[:, 0:w], ACT.Copy)\
                .then_inc(sem("w_rounded"), 1)

        def rest_of_weights(dve, n):
            chunk = SPLIT[n]
            w = width(chunk[0])
            dve.wait_ge(sem("w_rounded"), n + 1)
            dve.tensor_tensor(w_lo[:, SLOT_OF[chunk], 0:w].bitcast(F32R), slot(chunk)[:, 0:w],
                              w_hi[:, n % ROUNDED, 0:w], ALU.subtract).then_inc(sem("w_split"), 1)

        def split_weights(pe, chunk):
            n = SPLIT.index(chunk)
            pe.wait_ge(sem("w_split"), n + 1)
            return (w_hi[:, n % ROUNDED, :].bitcast(F32R), w_lo[:, SLOT_OF[chunk], :].bitcast(F32R))

        def source(kind, k, expert=None):
            if kind[:3] == "ada":
                t = int(kind[3])
                return a["w_ada"][0, k * P:(k + 1) * P, t * SLOT:(t + 1) * SLOT], slice(0, SLOT), None
            if kind == "w_in":
                return a["w_in"][0, k * P:(k + 1) * P, :], slice(0, IN_COLS), None
            if kind == "w_uq":
                return a["w_uq"][0].rearrange("(k p) n -> p k n", p=P), slice(0, 2 * 768), 2
            if kind == "w_ukv":
                return a["w_ukv"][0], slice(0, 1024), None
            if kind == "w1":
                return a["w1"][0, expert, k * P:(k + 1) * P, :], slice(0, SLOT), None
            if kind == "w2":
                return (a["w2"][0, expert, k * 2 * P:(k + 1) * 2 * P, :].rearrange("(k p) n -> p k n", p=P),
                        slice(0, SLOT), 2)
            if kind == "w_in2":
                return a["w_in_2"][0, k * P:(k + 1) * P, :], slice(0, IN2), None
            if kind == "ff1":
                return a["w_ff1_2"][0, :, k * 256:(k + 1) * 256].rearrange("(k p) n -> p k n", p=P), slice(0, SLOT), KD
            pairs = {"w_out2": "w_out_2", "ff2": "w_ff2_2", "w_ple": "w_ple_2", "gate": "w_ple_gate_2"}
            if kind in pairs:
                return (a[pairs[kind]][0, k * 2 * P:(k + 1) * 2 * P, :].rearrange("(k p) n -> p k n", p=P),
                        slice(0, SLOT), 2)
            if kind == "w_out":
                return a["w_out"][0, k * 2 * P:(k + 1) * 2 * P, :].rearrange("(k p) n -> p k n", p=P), slice(0, SLOT), 2

        def load_chunk(sp, chunk):
            src, cols, parts = source(*chunk)
            dst = slot(chunk)[:, cols]
            if parts:
                dst = dst.rearrange("p (k n) -> p k n", k=parts)
            b = CHUNK[chunk] - N_BEFORE
            if b >= BACK_SLOTS:
                used_wait(sp, BACK[b - BACK_SLOTS])
            elif AFTER[chunk] > 0:
                sp.wait_ge(sem("ring_freed"), AFTER[chunk])
            sp.dma_start(dst, src).then_inc(sem(f"landed{SLOT_OF[chunk]}"), 16)

        def max_no(u, c):
            return sum(2 if k == "d" else 1 for k, _, _ in UNITS[:u]) + c + 1

        MAIN, OVER = "", "over_"

        def moe(name, which):
            return sem(which + name)

        def mine(i):
            return slice(CAP * i, CAP * i + CAP)

        def freed_by(n, i, which):
            return n * len(PAIR) + ((N_FRONT if which == MAIN else SLOTS) + i + 1)

        def pair_slot(i):
            return (N_FRONT + i) % SLOTS

        def load_most(eng):
            wait_read(eng, "rank")
            return eng.value_load(most_i[0:1, 0:1], min_val=0, max_val=T)

        def pair_loads(sp, n, pair, which):
            for i, (kind, k, second) in enumerate(PAIR):
                src, cols, parts = source(kind, k, pair * 2 + second)
                s = pair_slot(i)
                dst = ring[:, s, cols]
                if parts:
                    dst = dst.rearrange("p (k n) -> p k n", k=parts)
                sp.wait_ge(moe("ring_freed", which),
                           n * len(PAIR) + ((N_FRONT if which == MAIN else SLOTS) + i + 1 - SLOTS))
                sp.dma_start(dst, src).then_inc(moe(f"landed{s}", which), 16)

        def sp_overflow(sp):
            count_ = load_most(sp)
            with sp.If(count_ > CAP):
                sp.wait_ge(sem("ring_freed"), N_FRONT + N_MOE)
                for r in range(1, ROUNDS):
                    with sp.If(count_ > r * CAP):
                        with sp.Fori(0, PAIRS) as pair:
                            pair_loads(sp, pair + (r - 1) * PAIRS, pair, OVER)
                        sp.wait_ge(moe("ring_freed", OVER), SLOTS + r * N_MOE)

        def pair_landed(pe, n, i, which):
            before = (N_FRONT + i) // SLOTS if which == MAIN else i // SLOTS
            pe.wait_ge(moe(f"landed{pair_slot(i)}", which), (n * 2 + (before + 1)) * 16)

        def gather(pe, n, which, y_read):
            pe.wait_ge(moe("sel_ready", which), n + 1)
            if y_read is not None:
                pe.wait_ge(moe("y_added", which), y_read)
            for k in range(KD):
                for t in range(NT):
                    m = pe.matmul(banks[GATHER_BANKS[k // 4]][:, k % 4 * P:(k % 4 + 1) * P], hf[:, t, k * P:(k + 1) * P],
                                  sel[:, t, :], start=t == 0, stop=t == 1, skip_group_check=True)
            m.then_inc(moe("xt_full", which), 1)

        def hidden(pe, n, which):
            pe.wait_ge(moe("xt_read", which), n + 1)
            for k in range(KD):
                for i in range(2):
                    pair_landed(pe, n, 2 * k + i, which)
                for q, bank_no in enumerate(GATE_BANKS + UP_BANKS):
                    for i in range(2):
                        m = pe.matmul(banks[bank_no][mine(i), :], gathered[:, k, mine(i)],
                                      ring[:, pair_slot(2 * k + i), q * 512:(q + 1) * 512],
                                      start=k == 0, stop=k == KD - 1, skip_group_check=True)
                    if k == KD - 1 and q == 1:
                        m.then_inc(moe("gate_full", which), 1)
                m.then_inc(moe("ring_freed", which), 2)
                if k == 5:
                    pe.wait_ge(moe("b1_in", which), (n + 1) * 16)
                    for q, bank_no in enumerate(GATE_BANKS + UP_BANKS):
                        m = pe.matmul(banks[bank_no][:], pick, b1rows[:, q * 512:(q + 1) * 512],
                                      start=False, stop=False, skip_group_check=True)

        def pe_rest(pe, n, which, ahead):
            for half in range(2):
                pe.wait_ge(moe("gated", which), n * 2 + (half + 1))
                for j in range(4):
                    m = pe.transpose(banks[TURN_BANKS[half]][:, j * P:(j + 1) * P],
                                     us[:, half * 512 + j * P:half * 512 + (j + 1) * P], ident[:])
                m.then_inc(moe("turned", which), 1)
                if half == 0:
                    pe.wait_ge(moe("selg_ready", which), n + 1)
                    for t in range(NT):
                        m = pe.transpose(banks[SHARE_BANK][:, t * P:(t + 1) * P], selg[:, t, :], ident[:])
                    m.then_inc(moe("share_full", which), 1)
            for j in range(4):
                if j % 2 == 0:
                    pe.wait_ge(moe("act_read", which), n * 2 + (j // 2 + 1))
                for i in range(2):
                    pair_landed(pe, n, 2 * KD + 2 * j + i, which)
                for c in range(2):
                    for kk in range(2):
                        for i in range(2):
                            w = ring[:, pair_slot(2 * KD + 2 * j + i), :].rearrange("p (k n) -> p k n", k=2)
                            k = 2 * j + kk
                            m = pe.matmul(banks[OUT_BANKS[c]][mine(i), :], actT[:, k, mine(i)],
                                          w[:, kk, c * 512:(c + 1) * 512],
                                          start=k == 0, stop=k == KD - 1, skip_group_check=True)
                    if j == 3 and c == 0:
                        m.then_inc(moe("out_half", which), 1)
                m.then_inc(moe("ring_freed", which), 2)
                if j == 2:
                    pe.wait_ge(moe("b2_in", which), (n + 1) * 16)
                    for c in range(2):
                        pe.matmul(banks[OUT_BANKS[c]][:], pick, b2rows[:, c * 512:(c + 1) * 512],
                                  start=False, stop=False, skip_group_check=True)
            pe.wait_ge(moe("share_read", which), n + 1)
            pe.wait_ge(moe("xt_read", which), n + (1 + ahead))
            for q in range(4):
                t, c = divmod(q, 2)
                if q < 2:
                    pe.wait_ge(moe("out_read", which), n * 2 + (c + 1))
                else:
                    pe.wait_ge(moe("y_added", which), n * 4 + q)
                pe.matmul(banks[MIX_BANKS[c]][:], selgT[:, t * P:(t + 1) * P], out2[:, c * 512:(c + 1) * 512],
                          start=True, stop=True, skip_group_check=True).then_inc(moe("mixed", which), 1)

        def load_b1(act, n, pair, which):
            act.dma_start(b1rows, a["b1"][0, bass.ds(pair * 2, 2), :]).then_inc(moe("b1_in", which), 16)

        def load_b2(act, n, pair, which):
            act.dma_start(b2rows, a["b2"][0, bass.ds(pair * 2, 2), :]).then_inc(moe("b2_in", which), 16)

        def gather_out(act, n, which):
            act.wait_ge(moe("xt_full", which), n + 1)
            for j in range(2):
                m = act.activation(gathered[:, 4 * j:4 * j + 4, :],
                                   banks[GATHER_BANKS[j]][:].rearrange("p (k s) -> p k s", k=4), ACT.Copy)
            m.then_inc(moe("xt_read", which), 1)

        def sigmoids(act, n, which):
            for half in range(2):
                cols = slice(half * 512, half * 512 + 512)
                act.wait_ge(moe("gate_clipped", which), n * 2 + (half + 1))
                act.activation(sg[:, cols], gs[:, cols], ACT.Sigmoid, scale=ALPHA).then_inc(moe("sigmoid", which), 1)

        def act_rest(act, n, which):
            for half in range(2):
                act.wait_ge(moe("turned", which), n * 2 + (half + 1))
                act.activation(actT[:, 4 * half:4 * half + 4, :],
                               banks[TURN_BANKS[half]][:].rearrange("p (j s) -> p j s", j=4), ACT.Copy)\
                    .then_inc(moe("act_read", which), 1)
            act.wait_ge(moe("share_full", which), n + 1)
            act.activation(selgT, banks[SHARE_BANK][:, 0:T], ACT.Copy).then_inc(moe("share_read", which), 1)

        def select(dve, n, pair, which):
            for t in range(NT):
                for i in range(2):
                    m = dve.tensor_scalar(sel[:, t, mine(i)], iota_s, slots[:, t, bass.ds(pair * 2 + i, 1)], None,
                                          ALU.is_equal)
            m.then_inc(moe("sel_ready", which), 1)

        def dve_pair(dve, n, pair, which):
            for t in range(NT):
                for i in range(2):
                    m = dve.tensor_scalar(selg[:, t, mine(i)], iota_s, slots[:, t, bass.ds(pair * 2 + i, 1)],
                                          gates[:, t, bass.ds(pair * 2 + i, 1)], ALU.is_equal, ALU.mult)
            m.then_inc(moe("selg_ready", which), 1)
            dve.wait_ge(moe("gate_full", which), n + 1)
            for half in range(2):
                dve.tensor_scalar(gs[:, half * 512:half * 512 + 512], banks[GATE_BANKS[half]][:], LIMIT, None, ALU.min)\
                    .then_inc(moe("gate_clipped", which), 1)
            dve.wait_ge(moe("ring_freed", which), freed_by(n, 2 * KD - 1, which))
            for half in range(2):
                cols = slice(half * 512, half * 512 + 512)
                dve.tensor_scalar(us[:, cols], banks[UP_BANKS[half]][:], LIMIT, -LIMIT, ALU.min, ALU.max)\
                    .then_inc(moe("up_clipped", which), 1)
            for half in range(2):
                cols = slice(half * 512, half * 512 + 512)
                dve.wait_ge(moe("gate_clipped", which), n * 2 + (half + 1))
                dve.wait_ge(moe("up_clipped", which), n * 2 + (half + 1))
                dve.scalar_tensor_tensor(out=us[:, cols], in0=us[:, cols], scalar=1.0, in1=gs[:, cols],
                                         op0=ALU.add, op1=ALU.mult).then_inc(moe("up_gate", which), 1)
                dve.wait_ge(moe("up_gate", which), n * 2 + (half + 1))
                dve.wait_ge(moe("sigmoid", which), n * 2 + (half + 1))
                dve.tensor_tensor(us[:, cols], us[:, cols], sg[:, cols], ALU.mult).then_inc(moe("gated", which), 1)
            for c in range(2):
                if c == 0:
                    dve.wait_ge(moe("out_half", which), n + 1)
                else:
                    dve.wait_ge(moe("ring_freed", which), freed_by(n, len(PAIR) - 1, which))
                cols = slice(c * 512, c * 512 + 512)
                dve.tensor_tensor(out2[:, cols], banks[OUT_BANKS[c]][:], gf[:, cols], ALU.mult)\
                    .then_inc(moe("out_read", which), 1)
            for q in range(4):
                t, c = divmod(q, 2)
                dve.wait_ge(moe("mixed", which), n * 4 + (q + 1))
                cols = slice(c * 512, c * 512 + 512)
                dve.tensor_tensor(x2[:, t, cols], x2[:, t, cols], banks[MIX_BANKS[c]][:], ALU.add)\
                    .then_inc(moe("y_added", which), 1)

        block = ctx.enter_context(nc.Block())

        @block.sync
        def _(sp):
            sp.dma_start(xc[:, 0:2, :], a["ctx"][0].rearrange("(t p) d -> p t d", p=P)).then_inc(sem("ctx_in"), 16)
            sp.dma_start(xc[:, 2:4, :], a["x"][0].rearrange("(t p) d -> p t d", p=P)).then_inc(sem("x_in"), 16)
            for chunk in FRONT:
                load_chunk(sp, chunk)
            with sp.Fori(0, PAIRS) as pair:
                pair_loads(sp, pair, pair, MAIN)
            sp_overflow(sp)
            for chunk in BACK:
                load_chunk(sp, chunk)
            for t in range(NT):
                for c in range(2):
                    sp.wait_ge(sem("out_done"), 2 * t + c + 1)
                    sp.dma_start(out[0, t * P:(t + 1) * P, c * 512:(c + 1) * 512], x2[:, t, c * 512:(c + 1) * 512])\
                        .then_inc(sem("stored"), 16)
            sp.wait_ge(sem("stored"), 64)

        @block.gpsimd
        def _(pool):
            step = stepper(pool, "pool_link")
            step(pool.memset(ident[:], 0.0))
            step(pool.affine_select(out=ident[:], in_=ident[:], compare_op=ALU.not_equal, fill=1.0, base=0,
                                    pattern=[[-1, P]], channel_multiplier=1), "consts")
            step(pool.memset(ones[:], 1.0), "consts")
            step(pool.memset(cT[:], 0.0), "consts")
            step(pool.memset(mrows[:], 0.0), "consts")
            for t in range(3):
                for i in range(2):
                    src = a["b_ada"][0, t * SLOT:(t + 1) * SLOT].rearrange("(q n) -> q n", q=4)
                    pool.dma_start(mrows[i:97 + i:32, t, :], src).then_inc(sem("bada_in" if t else "bada0_in"), 16)
            pool.dma_start(rb[:], a["router_b"]).then_inc(sem("router_in"), 16)
            wait_read(pool, "mixT0")
            pool.dma_start(rw, a["router_w"][0].rearrange("(k p) e -> p k e", p=P)).then_inc(sem("router_in"), 16)
            pool.wait_ge(sem("x1_done"), 4)
            step(pool.memset(below, 1.0))
            step(pool.affine_select(out=below, in_=below, compare_op=ALU.is_gt, fill=0.0, base=0,
                                    pattern=[[1, P]], channel_multiplier=-1), "below_done")
            step(pool.iota(iota_i, pattern=[[1, CAP]], base=0, channel_multiplier=0), "iota_done")
            step(pool.memset(pick, 1.0))
            step(pool.affine_select(out=pick, in_=pick, compare_op=ALU.is_gt, fill=0.0, base=1,
                                    pattern=[[1, P]], channel_multiplier=-CAP))
            step(pool.affine_select(out=pick, in_=pick, compare_op=ALU.is_gt, fill=0.0, base=CAP,
                                    pattern=[[-1, P]], channel_multiplier=CAP), "pick_done")
            pool.wait_ge(sem("hf_done"), 2 * NT)
            for dst, name in ((final_w, "final_norm_w"), (ln1g, "ln1_g_2"), (ln1b, "ln1_b_2")):
                src = a[name] if name != "final_norm_w" else a[name].rearrange("(a n) -> a n", a=1)
                pool.dma_start(dst, src.broadcast_to([P, D])).then_inc(sem("norm_in"), 16)
            pool.dma_start(w_pool, a["w_pool_2"][0].rearrange("g c d -> c g d")).then_inc(sem("mix_in"), 16)
            pool.dma_start(p_tok, a["p_2"][0, 0].rearrange("(t p) c -> p t c", p=P)).then_inc(sem("mix_in"), 16)
            pool.dma_start(neg_dist, a["neg_dist"]).then_inc(sem("mix_in"), 16)
            pool.dma_start(sinks, a["attn_sinks_2"].broadcast_to([P, QH])).then_inc(sem("mix_in"), 16)
            wait_read(pool, "logits")
            pool.dma_start(bands, a["pool_bands"].rearrange("g (k p) t -> p g k t", p=P)).then_inc(sem("mix_in"), 16)
            pool.wait_ge(sem("moe_used"), 1)
            pool.dma_start(ln2g, a["ln2_g_2"].broadcast_to([P, D])).then_inc(sem("norm2_in"), 16)
            pool.dma_start(ln2b, a["ln2_b_2"].broadcast_to([P, D])).then_inc(sem("norm2_in"), 16)
            pool.dma_start(b_gate, a["b_ple_gate_2"].broadcast_to([P, D])).then_inc(sem("b_gate_in"), 16)

        @block.scalar
        def _(act):
            step = stepper(act, "act_link")

            def load(dst, src, name, inc=16):
                act.dma_start(dst, src).then_inc(sem(name), 16)

            load(small[0:8, :], a["c"][0].rearrange("(r n) -> r n", n=P), "c_in")
            load(small[8:16, :], a["c_ctx"].rearrange("(r n) -> r n", n=P), "c_in")
            load(small[32:40, :], a["attn_norm_w"][0].rearrange("(r n) -> r n", n=P), "vec_in")
            load(small[40:42, :], a["q_norm_w"][0].rearrange("(r n) -> r n", n=P), "vec_in")
            load(small[42:43, :], a["kv_norm_w"][0].rearrange("(r n) -> r n", n=P), "vec_in")
            load(small[43:44, :], a["subln_w"][0].rearrange("(r n) -> r n", n=P), "vec_in")
            load(small[44:48, :], a["pool_scale_2"][0].rearrange("(r n) -> r n", n=P), "vec_in")

            act.wait_ge(sem("c_in"), 16 * 2)
            step(act.activation(csig[:], small[0:16, :], ACT.Sigmoid), "csig_done")
            act.wait_ge(sem("ctx_in"), 16)
            for t in range(4):
                if t == 2:
                    act.wait_ge(sem("x_in"), 16)
                step(act.activation(sq[:], xc[:, t, :], ACT.Square, accum_out=stat[:, t:t + 1]), "ss_done")
            act.wait_ge(sem("ms_done"), 1)
            step(act.activation(stat[:, 8:12], stat[:, 4:8], ACT.Sqrt), "root_done")
            for n, name in enumerate(("lambda_q1", "lambda_k1", "lambda_q2", "lambda_k2")):
                load(lamv[:, n, :], a[name].broadcast_to([P, 64]), "lam_in")
            load(rope_cos[:], a["rope_cos"].rearrange("(t p) c -> p t c", p=P), "rope_in")
            load(rope_sin[:], a["rope_sin"].rearrange("(t p) c -> p t c", p=P), "rope_in")
            for k in range(KD):
                b = take(act, f"hT{k}")
                step(act.activation(hT[:, k, :], b[:], ACT.Copy), tile=f"hT{k}")
            for k in range(SPLIT_FROM, KD):
                if k == SPLIT_FROM:
                    act.wait_ge(sem("ring_freed"), KD)
                ring_wait(act, ("w_in", k))
                step(act.activation(in_hi(k).bitcast(F32R), slot(("w_in", k))[:, 0:IN_COLS], ACT.Copy), "in_rounded",
                     wait=False)
                act.wait_ge(sem("hT_done"), 2 * k + 2)
                if k == SPLIT_FROM:
                    act.wait_ge(full("hT7"), use("hT7") + 1)
                step(act.activation(tok_hi[:, k, :].bitcast(F32R), hT[:, k, :], ACT.Copy), "in_rounded", wait=False)
            act.wait_ge(sem("lam_sums"), 1)
            step(act.activation(lam[:, 2:4], lam[:, 0:2], ACT.Exp), "lam_exp")

            for t in range(4):
                if t == 2:
                    act.wait_ge(sem("lat_ms"), 1)
                    step(act.activation(stat[:, 24:30], stat[:, 18:24], ACT.Sqrt), "lat_root")
                if t < 2:
                    step(act.activation(dk[:, t, :], take(act, f"proj{t}_1")[:], ACT.Copy), tile=f"proj{t}_1")
                step(act.activation(dv[:, t, :], take(act, f"proj{t}_2")[:], ACT.Copy), tile=f"proj{t}_2")
            for h in range(H):
                b = take(act, f"dkT{h}")
                step(act.activation(dkT[:, h, :], b[:], ACT.Copy), tile=f"dkT{h}")
            for j in range(2):
                b = take(act, f"dqT{j}")
                step(act.activation(dqT[:, 2 * j:2 * j + 2, :], b[:].rearrange("p (h t) -> p h t", h=2),
                                    ACT.Copy, scale=DIFF_SCALE), tile=f"dqT{j}")
            for j in range(2):
                b = take(act, f"qnope{j}")
                if j == 0:
                    act.wait_ge(full("proj3_2"), use("proj3_2") + 1)
                    load(bc[:, 2, :], a["ffn_norm_w"].broadcast_to([P, D]), "ffnw_in")
                step(act.activation(qnT[:, 2 * j:2 * j + 2, :], b[:].rearrange("p (h t) -> p h t", h=2),
                                    ACT.Copy, scale=MLA_SCALE), tile=f"qnope{j}")
            act.wait_ge(full("proj3_2"), use("proj3_2") + 1)
            for h in range(H):
                b = take(act, f"knope{h}")
                step(act.activation(knT[:, h, :], b[:], ACT.Copy), tile=f"knope{h}")

            for what, u in attention_order(len(UNITS)):
                kind, h, t = UNITS[u]
                if what == "score":
                    for c in range(2 if kind == "d" else 1):
                        b = take(act, f"s{u}_{c}")
                        act.wait_ge(sem("neg_max"), max_no(u, c))
                        if u >= 2 and c == 0:
                            act.wait_ge(full(f"pT{u - 2}"), use(f"pT{u - 2}") + 1)
                        step(act.activation(prob[:, u % 2, c, :], b[:], ACT.Exp, bias=psum_sum[:, u, c:c + 1],
                                            accum_out=psum_sum[:, u, 2 + c:3 + c]), tile=f"s{u}_{c}")
                elif what == "turn":
                    b = take(act, f"pT{u}")
                    if u >= 2:
                        act.wait_ge(full(f"av{u - 2}"), use(f"av{u - 2}") + 1)
                    step(act.activation(probT[:, u % 2, :], b[:], ACT.Copy), tile=f"pT{u}")
                elif u == 9:
                    act.wait_ge(sem("sub_ms"), 1)
                    step(act.activation(stat[:, 48:56], stat[:, 40:48], ACT.Sqrt), "sub_root")
            for j in (2, 3):
                b = take(act, f"mixT{j}")
                step(act.activation(mixT[:, 2 * j:2 * j + 2, :], b[:].rearrange("p (k t) -> p k t", k=2), ACT.Copy),
                     tile=f"mixT{j}")
            act.wait_ge(sem("x1_done"), 2)
            step(act.activation(xn[:, 0, :], xc[:, 2, :], ACT.Square, accum_out=stat[:, 0:1]), "ss2_done")
            act.wait_ge(sem("ms2_done"), 1)
            step(act.activation(stat[:, 4:5], stat[:, 2:3], ACT.Sqrt), "root2_done")
            def feed_forward_turned(t):
                for j in range(4):
                    b = take(act, f"hfT{t}_{j}")
                    step(act.activation(hfT[:, 2 * j:2 * j + 2, t * P:(t + 1) * P],
                                        b[:, 0:2 * P].rearrange("p (k t) -> p k t", k=2), ACT.Copy), tile=f"hfT{t}_{j}")

            feed_forward_turned(0)
            for n in range(2):
                act.wait_ge(sem("x1_done"), 3 + n)
                step(act.activation(xn[:, 0, 0:512], xc[:, 3, n * 512:n * 512 + 512], ACT.Square,
                                    accum_out=stat[:, 8 + n:9 + n]), "ss2_done")
            act.wait_ge(sem("ms2_done"), 2)
            step(act.activation(stat[:, 5:6], stat[:, 3:4], ACT.Sqrt), "root2_done")
            feed_forward_turned(1)
            for t in range(NT):
                act.wait_ge(sem("top_done"), t + 1)
                step(act.activation(topx[:, t, 4:8], top[:, t, 0:TOP_K], ACT.Exp, bias=topx[:, t, 0:1],
                                    accum_out=topx[:, t, 1:2]), "topx_done")

            gather_out(act, 0, MAIN)
            with act.Fori(0, PAIRS) as pair:
                load_b1(act, pair, pair, MAIN)
                sigmoids(act, pair, MAIN)
                gather_out(act, pair + 1, MAIN)
                load_b2(act, pair, pair, MAIN)
                act_rest(act, pair, MAIN)
            most_act = load_most(act)
            with act.If(most_act > CAP):
                with act.Fori(1, ROUNDS) as r:
                    with act.If(most_act > r * CAP):
                        with act.Fori(0, PAIRS) as pair:
                            n = (r - 1) * PAIRS + pair
                            load_b1(act, n, pair, OVER)
                            gather_out(act, n, OVER)
                            sigmoids(act, n, OVER)
                            load_b2(act, n, pair, OVER)
                            act_rest(act, n, OVER)

            def preload_sqrt():
                step(act.activation(stat[:, 56:57], stat[:, 4:5], ACT.Sqrt))

            preload_sqrt()
            act.wait_ge(sem("moe_used"), 1)
            step(act.activation(xn[:, 0, :], x2[:, 0, :], ACT.Square, accum_out=stat[:, 0:1]), "ss3_done")
            act.wait_ge(sem("ms3_done"), 1)
            step(act.activation(stat[:, 4:6], stat[:, 2:4], ACT.Sqrt), "root3_done")

            def transposed(name, dst, k, scale=1.0):
                b = take(act, name)
                step(act.activation(dst, b[:].rearrange("p (k t) -> p k t", k=k), ACT.Copy, scale=scale), tile=name)

            def rounded(name, dst, k=2):
                b = take(act, name)
                step(act.activation(dst.bitcast(F32R), b[:].rearrange("p (k t) -> p k t", k=k), ACT.Copy), "tile_rounded",
                     wait=False)

            for n in range(ROUNDED - 1):
                round_weights(act, n)
            for j in range(4):
                rounded(f"xT{j}", x_hi[:, 2 * j:2 * j + 2, :])
            for n in range(ROUNDED - 1, 8):
                round_weights(act, n)
            for t in range(NT):
                b = take(act, f"in{t}_0")
                step(act.activation(u_tok[:, t, :], b[:], ACT.Copy), tile=f"in{t}_0")
                b = take(act, f"in{t}_1")
                step(act.activation(q_tok[:, t, :], b[:], ACT.Copy), tile=f"in{t}_1")
            transposed("kT", k2T, 2)
            transposed("qT0", q2T[:, 0:2, :], 2, HD ** -0.5)
            transposed("qT1", q2T[:, 2:4, :], 2, HD ** -0.5)
            transposed("pd0", pool_dT[:, 0:2, :], 2)
            transposed("pd1", pool_dT[:, 2:4, :], 2)
            for what, u in attention_order(len(UNITS2)):
                h, blk = UNITS2[u]
                w = (blk + 1) * P
                if what == "score":
                    for i in range(2):
                        act.wait_ge(sem("masked"), u + 1)
                        step(act.activation(prob2[:, u % 2, i * w:(i + 1) * w], prob2[:, u % 2, i * w:(i + 1) * w], ACT.Exp,
                                            bias=soft[:, u, 4 + i:5 + i], accum_out=soft[:, u, 8 + i:9 + i]), wait=False)
                    step(act.activation(soft[:, u, 10:12], soft[:, u, 6:8], ACT.Exp), "exp2_done")
                    if u % 2:
                        round_weights(act, 8 + u // 2)
                elif what == "turn":
                    b = take(act, f"tw{u}")
                    step(act.activation(prob2T[u % 2][:, 0:2 * w], b[:, 0:2 * w], ACT.Copy), tile=f"tw{u}")
            rounded("oT0", x_hi[:, 4:6, :])
            rounded("oT1", x_hi[:, 6:8, :])
            for t in range(NT):
                act.wait_ge(sem("var1"), t + 1)
                step(act.activation(stat[:, 16 + t:17 + t], stat[:, 12 + t:13 + t], ACT.Sqrt), "root4_done")
                if t == 0:
                    for n in range(12, 15):
                        round_weights(act, n)
            transposed("plT", pT, 2)
            for j in range(4):
                rounded(f"h1T{j}", x_hi[:, 2 * j:2 * j + 2, :])
            for j in range(16):
                b = take(act, f"part{j}")
                if j >= 2:
                    act.wait_ge(sem("wide_done"), j - 1)
                step(act.activation(wide[:, j % 2, :], b[:], ACT.Relu), tile=f"part{j}")
                act.wait_ge(sem("squared"), j + 1)
                if j >= 2:
                    act.wait_ge(sem("wide_used"), j - 1)
                step(act.activation(wide_hi[:, j % 2, :].bitcast(F32R), wide[:, j % 2, :], ACT.Copy), "wide_rounded",
                     wait=False)
                for n in splits_at(j):
                    round_weights(act, n)
            for n in range(44, 47):
                round_weights(act, n)
            preload_sqrt()
            for t in range(NT):
                act.wait_ge(sem("var2"), t + 1)
                step(act.activation(stat[:, 26 + t:27 + t], stat[:, 22 + t:23 + t], ACT.Sqrt), "root5_done")
                if t == 0:
                    round_weights(act, 47)
            for j in range(4):
                rounded(f"h2T{j}", x_hi[:, 2 * j:2 * j + 2, :])
            for n in range(4):
                act.wait_ge(sem("gate_in"), n + 1)
                step(act.activation(gate_z[:, n, :], gate_z[:, n, :], ACT.Sigmoid), "gate_done")

        @block.vector
        def _(dve):
            step = stepper(dve, "dve_link")
            V = nc.vector

            dve.wait_ge(sem("csig_done"), 1)
            step(V.tensor_tensor(small[0:16, :], small[0:16, :], csig[:], ALU.mult), "silu_done")
            b = take(dve, "cT")
            dve.wait_ge(sem("consts"), 3)
            step(V.tensor_copy(cT[:, :, 0:2], b[:, 0:16].rearrange("p (i k) -> p k i", i=2)), tile="cT")

            dve.wait_ge(sem("ss_done"), 4)
            step(V.tensor_scalar(stat[:, 4:8], stat[:, 0:4], 1.0 / D, EPS, ALU.mult, ALU.add), "ms_done")
            dve.wait_ge(sem("root_done"), 1)
            step(V.reciprocal(stat[:, 12:16], stat[:, 8:12]))
            for t in range(4):
                step(V.tensor_scalar(xn[:, t, :], xc[:, t, :], stat[:, 12 + t:13 + t], None, ALU.mult), "xn_done",
                     wait=t == 3)
            step(V.tensor_copy(vecT[:], take(dve, "vecT")[:, 0:16]), tile="vecT")

            b = take(dve, "ada0")
            dve.wait_ge(sem("bada0_in"), 32)
            step(V.tensor_tensor(mrows[:, 0, :], b[:], mrows[:, 0, :], ALU.add), tile="ada0")
            b = take(dve, "modT")[:].rearrange("p (b q r) -> p r q b", b=4, q=4)
            for i in range(2):
                step(V.tensor_copy(modT[:, i, :].rearrange("p (q b) -> p q b", q=4), b[:, i]),
                     tile="modT" if i else None)
            for i in range(2):
                step(V.scalar_tensor_tensor(out=scol[:, i, :], in0=modT[:, i, 8:16], scalar=1.0, in1=vecT[:, 0:8],
                                            op0=ALU.add, op1=ALU.mult))
            def modulate(k):
                wait_read(dve, f"hT{k}")
                for i in (1, 0):
                    at = hT[:, k, 0:T] if i else hT[:, k, T:KEYS]
                    step(V.tensor_scalar(at, at, scol[:, i, k:k + 1], modT[:, i, k:k + 1], ALU.mult, ALU.add),
                         "hT_done", wait=False)

            for k in range(SPLIT_FROM + 1):
                modulate(k)
            for k in range(SPLIT_FROM, KD):
                if k + 1 < KD:
                    modulate(k + 1)
                n = 2 * (k - SPLIT_FROM)
                w = slot(("w_in", k))[:, 0:IN_COLS]
                dve.wait_ge(sem("in_rounded"), n + 1)
                step(V.tensor_tensor(in_lo[k][:, 0:IN_COLS].bitcast(F32R), w, in_hi(k), ALU.subtract),
                     "in_split", wait=False)
                dve.wait_ge(sem("in_rounded"), n + 2)
                dve.wait_ge(sem("hT_done"), 2 * k + 2)
                step(V.tensor_tensor(tok_lo[:, k, :].bitcast(F32R), hT[:, k, :], tok_hi[:, k, :], ALU.subtract),
                     "in_split", wait=False)
            dve.wait_ge(sem("lam_in"), 64)
            for n in range(2):
                step(V.tensor_tensor_reduce(lamv[:, 2 * n, :], lamv[:, 2 * n, :], lamv[:, 2 * n + 1, :], 1.0, 0.0,
                                            ALU.mult, ALU.add, lam[:, n:n + 1]), "lam_sums" if n else None)
            dve.wait_ge(sem("lam_exp"), 1)
            step(V.tensor_tensor(lam[:, 4:5], lam[:, 3:4], lam[:, 2:3], ALU.subtract))
            step(V.tensor_scalar(lam[:, 5:6], lam[:, 4:5], -LAM_INIT, None, ALU.add))

            def rotate(dst, src, t, n, last):
                w = n * 64
                cos = rope_cos[:, t, :].unsqueeze(1).broadcast_to([P, n, 64])
                step(V.tensor_tensor(ropet[:, 0, 0:w].rearrange("p (n c) -> p n c", n=n),
                                     src.rearrange("p (n c) -> p n c", n=n), cos, ALU.mult))
                s = src.rearrange("p (n f c) -> p n f c", f=2, c=16)
                r = ropet[:, 1, 0:w].rearrange("p (n f c) -> p n f c", f=2, c=16)
                for half in range(2):
                    for axis in range(2):
                        sin = rope_sin[:, t, axis * 16:axis * 16 + 16].unsqueeze(1).broadcast_to([P, n, 16])
                        step(V.tensor_tensor(r[:, axis::2, half, :], s[:, axis::2, 1 - half, :], sin, ALU.mult),
                             wait=half == 1 and axis == 1)
                o0 = ropet[:, 0, 0:w].rearrange("p (n f c) -> p n f c", f=2, c=16)
                d = dst.rearrange("p (n f c) -> p n f c", f=2, c=16)
                step(V.tensor_tensor(d[:, :, 0, :], o0[:, :, 0, :], r[:, :, 0, :], ALU.subtract))
                step(V.tensor_tensor(d[:, :, 1, :], o0[:, :, 1, :], r[:, :, 1, :], ALU.add), **last)

            dve.wait_ge(sem("rope_in"), 32)
            for t in range(4):
                name = f"proj{t}_3"
                b = take(dve, name)
                at = 0 if t < 2 else Q_RANK
                if t >= 2:
                    step(V.tensor_copy(cq[:, t - 2, :], b[:, 0:Q_RANK]))
                step(V.tensor_copy(ckv[:, t, :], b[:, at:at + KV_RANK]))
                krs = b[:, at + KV_RANK:at + KV_RANK + ROPE]
                if t < 2:
                    step(V.tensor_copy(kr[:, t, 0, :], krs), tile=name)
                else:
                    rotate(kr[:, t, 0, :], krs, t - 2, 1, {"tile": name})
                step(V.tensor_copy(kr[:, t, 1, :], kr[:, t, 0, :]), "kr_done")
            for t in range(4):
                step(V.tensor_tensor_reduce(sq[:, 0:KV_RANK], ckv[:, t, :], ckv[:, t, :], 1.0, 0.0, ALU.mult, ALU.add,
                                            stat[:, 12 + t:13 + t]))
            for t in range(2):
                step(V.tensor_tensor_reduce(sq[:, 0:Q_RANK], cq[:, t, :], cq[:, t, :], 1.0, 0.0, ALU.mult, ALU.add,
                                            stat[:, 16 + t:17 + t]))
            step(V.tensor_scalar(stat[:, 18:22], stat[:, 12:16], 1.0 / KV_RANK, EPS, ALU.mult, ALU.add))
            step(V.tensor_scalar(stat[:, 22:24], stat[:, 16:18], 1.0 / Q_RANK, EPS, ALU.mult, ALU.add), "lat_ms")
            dve.wait_ge(sem("lat_root"), 1)
            step(V.reciprocal(stat[:, 30:36], stat[:, 24:30]))
            for t in range(4):
                step(V.tensor_scalar(ckv[:, t, :], ckv[:, t, :], stat[:, 30 + t:31 + t], None, ALU.mult), "lat_done")
            for t in range(2):
                step(V.tensor_scalar(cq[:, t, :], cq[:, t, :], stat[:, 34 + t:35 + t], None, ALU.mult), "lat_done")
            for t in (2, 3):
                for c in range(2):
                    name = f"proj{t}_{c}"
                    rotate((dq[:, t - 2, :] if c == 0 else dk[:, t, :]), take(dve, name)[:], t - 2, 8, {"tile": name})
            b = take(dve, "ckvT")
            step(V.tensor_scalar(ckvT, b[:], vecT[:, 10:11], None, ALU.mult), tile="ckvT")
            b = take(dve, "krT")
            step(V.tensor_copy(krT, b[:]), tile="krT")
            b = take(dve, "cqT")
            for k in range(2):
                step(V.tensor_scalar(cqT[:, k, :], b[:, k * T:(k + 1) * T], vecT[:, 8 + k:9 + k], None, ALU.mult),
                     tile="cqT" if k else None)
            b = take(dve, "qrope")
            for t in range(NT):
                rotate(qr[:, t, :], b[:, t * 256:(t + 1) * 256], t, H, {"tile": "qrope"} if t else {})
            for t in range(4):
                b = take(dve, f"mv{t}")
                step(V.tensor_copy(mv[:, t, :], b[:]), tile=f"mv{t}")
            b = take(dve, "qrT")
            step(V.tensor_scalar(qrT, b[:].rearrange("p (j t) -> p j t", j=2), MLA_SCALE, None, ALU.mult), tile="qrT")

            for what, u in attention_order(len(UNITS)):
                kind, h, t = UNITS[u]
                if what == "score":
                    for c in range(2 if kind == "d" else 1):
                        b = take(dve, f"s{u}_{c}")
                        step(V.tensor_reduce(psum_sum[:, u, c:c + 1], b[:], AX, ALU.max, negate=True), "neg_max")
                elif what == "turn":
                    continue
                else:
                    b = take(dve, f"av{u}")
                    at = h * P + (0 if kind == "d" else 512)
                    step(V.tensor_scalar(o[:, t, at:at + P], b[:, 0:P], psum_sum[:, u, 4:5], None, ALU.mult),
                         tile=f"av{u}")
                if what == "score":
                    last = f"s{u}_1" if kind == "d" else f"s{u}_0"
                    wait_read(dve, f"s{u}_0")
                    wait_read(dve, last)
                    step(V.reciprocal(psum_sum[:, u, 4:6] if kind == "d" else psum_sum[:, u, 4:5],
                                      psum_sum[:, u, 2:4] if kind == "d" else psum_sum[:, u, 2:3]),
                         "pmix_done" if kind == "m" else None)
                    if kind == "d":
                        step(V.scalar_tensor_tensor(out=psum_sum[:, u, 6:7], in0=psum_sum[:, u, 5:6],
                                                    scalar=psum_sum[:, u, 2:3], in1=lam[:, 5:6],
                                                    op0=ALU.mult, op1=ALU.mult))
                        step(V.scalar_tensor_tensor(out=prob[:, u % 2, 0, :], in0=prob[:, u % 2, 1, :],
                                                    scalar=psum_sum[:, u, 6:7], in1=prob[:, u % 2, 0, :],
                                                    op0=ALU.mult, op1=ALU.add), "pmix_done")
                if what == "value" and u == 9:
                    for t_ in range(NT):
                        for h_ in range(H):
                            n = t_ * H + h_
                            head = o[:, t_, h_ * P:(h_ + 1) * P]
                            step(V.tensor_tensor_reduce(sq[:, 0:P], head, head, 1.0, 0.0, ALU.mult, ALU.add,
                                                        stat[:, 32 + n:33 + n]))
                    step(V.tensor_scalar(stat[:, 40:48], stat[:, 32:40], 1.0 / P, EPS, ALU.mult, ALU.add), "sub_ms")
                if what == "value" and u == 12:
                    dve.wait_ge(sem("sub_root"), 1)
                    step(V.reciprocal(stat[:, 56:64], stat[:, 48:56]))
                    for t_ in range(NT):
                        heads = o[:, t_, 0:512].rearrange("p (h c) -> p h c", h=H)
                        by = stat[:, 56 + t_ * H:56 + t_ * H + H].unsqueeze(2).broadcast_to([P, H, P])
                        step(V.tensor_tensor(heads, heads, by, ALU.mult), "sub_done")
                    step(V.tensor_scalar(vecT[:, 11:12], vecT[:, 11:12], 1.0 - LAM_INIT, None, ALU.mult))
                if what == "value" and u == 3:
                    dve.wait_ge(sem("bada_in"), 64)
                    for i in (1, 2):
                        b = take(dve, f"ada{i}")
                        step(V.tensor_tensor(mrows[:, i, :], b[:], mrows[:, i, :], ALU.add), tile=f"ada{i}")
                    for n in range(8):
                        b = take(dve, f"bc{n}")
                        dst = bc[:, n // 2, (n % 2) * 512:(n % 2) * 512 + 512]
                        if n // 2 == 2:
                            dve.wait_ge(sem("ffnw_in"), 16)
                            step(V.scalar_tensor_tensor(out=dst, in0=b[:], scalar=1.0,
                                                        in1=dst,
                                                        op0=ALU.add, op1=ALU.mult), tile=f"bc{n}")
                        else:
                            step(V.tensor_copy(dst, b[:]), tile=f"bc{n}")

            for j in range(2):
                b = take(dve, f"mixT{j}")
                step(V.tensor_scalar(mixT[:, 2 * j:2 * j + 2, :], b[:].rearrange("p (k t) -> p k t", k=2),
                                     vecT[:, 11:12], None, ALU.mult), tile=f"mixT{j}")
            for t in range(NT):
                for n in range(2):
                    cols = slice(n * 512, n * 512 + 512)
                    b = take(dve, f"wo{t}_{n}")
                    step(V.tensor_tensor(sq[:, 0:512], b[:], bc[:, 0, cols], ALU.mult), tile=f"wo{t}_{n}")
                    step(V.tensor_tensor(xc[:, 2 + t, cols], xc[:, 2 + t, cols], sq[:, 0:512], ALU.add), "x1_done")
                dve.wait_ge(sem("ss2_done"), 2 * t + 1)
                if t:
                    step(V.tensor_tensor(stat[:, 1:2], stat[:, 8:9], stat[:, 9:10], ALU.add))
                step(V.tensor_scalar(stat[:, 2 + t:3 + t], stat[:, t:t + 1], 1.0 / D, EPS, ALU.mult, ALU.add), "ms2_done")
                dve.wait_ge(sem("root2_done"), t + 1)
                step(V.reciprocal(stat[:, 6 + t:7 + t], stat[:, 4 + t:5 + t]))
                for n in range(2):
                    cols = slice(n * 512, n * 512 + 512)
                    step(V.scalar_tensor_tensor(out=hf[:, t, cols], in0=xc[:, 2 + t, cols], scalar=stat[:, 6 + t:7 + t],
                                                in1=bc[:, 2, cols], op0=ALU.mult, op1=ALU.mult))
                    step(V.tensor_tensor(hf[:, t, cols], hf[:, t, cols], bc[:, 1, cols], ALU.add), "hf_done")

            dve.wait_ge(sem("iota_done"), 1)
            step(V.tensor_copy(iota_s, iota_i))
            step(V.tensor_copy(iota_e[:], iota_i[:, 0:E]))
            step(V.memset(gates[:], 0.0))
            step(V.memset(slots[:], -1.0))
            b = take(dve, "logits")
            step(V.tensor_copy(logit[:], b[:, 0:NT * E].rearrange("p (t e) -> p t e", t=NT)), tile="logits")
            for t in range(NT):
                step(V.max(top[:, t, :], logit[:, t, :]))
                step(V.tensor_scalar(topx[:, t, 0:1], top[:, t, 0:1], -1.0, None, ALU.mult), "top_done")
            for t in range(NT):
                step(V.max_index(top_at[:, t, :], top[:, t, :], logit[:, t, :]))
            step(V.tensor_copy(top_atf[:], top_at[:]))
            step(V.tensor_tensor(hot, iota_e[:].unsqueeze(1).unsqueeze(1).broadcast_to([P, NT, TOP_K, E]),
                                 top_atf[:, :, 0:TOP_K].unsqueeze(3).broadcast_to([P, NT, TOP_K, E]), ALU.is_equal))
            step(V.tensor_reduce(chosen[:], hot.rearrange("p t k e -> p t e k"), AX, ALU.add), "chosen_done")
            dve.wait_ge(sem("topx_done"), NT)
            step(V.reciprocal(topx[:, :, 2:3], topx[:, :, 1:2]))
            step(V.tensor_tensor(gate4[:], topx[:, :, 4:8], topx[:, :, 2:3].broadcast_to([P, NT, TOP_K]), ALU.mult))
            step(V.tensor_tensor(hot, hot, gate4[:].unsqueeze(3).broadcast_to([P, NT, TOP_K, E]), ALU.mult))
            step(V.tensor_reduce(gates[:, :, 0:E], hot.rearrange("p t k e -> p t e k"), AX, ALU.add))
            b = take(dve, "rank")
            step(V.scalar_tensor_tensor(out=slots[:, :, 0:E], in0=b[:, 0:NT * E].rearrange("p (t e) -> p t e", t=NT),
                                        scalar=1.0, in1=chosen[:], op0=ALU.add, op1=ALU.mult))
            step(V.tensor_scalar(slots[:, :, 0:E], slots[:, :, 0:E], -1.0, None, ALU.add))
            step(V.tensor_reduce(most[:, 0:1], b[:, 2 * E:3 * E], AX, ALU.max))
            step(V.tensor_copy(most_i[:], most[:, 0:1]), tile="rank")
            dve.sem_inc(moe("y_added", MAIN), 1)
            dve.sem_inc(moe("y_added", OVER), 1)
            select(dve, 0, 0, MAIN)
            with dve.Fori(0, PAIRS) as pair:
                dve.wait_ge(moe("xt_full", MAIN), pair + 1)
                select(dve, pair + 1, pair + 1, MAIN)
                dve_pair(dve, pair, pair, MAIN)
            most_dve = load_most(dve)
            with dve.If(most_dve > CAP):
                with dve.Fori(1, ROUNDS) as r:
                    with dve.If(most_dve > r * CAP):
                        V.tensor_scalar(iota_s, iota_s, float(CAP), None, ALU.add).then_inc(moe("next_round", OVER), 1)
                        with dve.Fori(0, PAIRS) as pair:
                            n = (r - 1) * PAIRS + pair
                            dve.wait_ge(moe("next_round", OVER), r)
                            select(dve, n, pair, OVER)
                            dve_pair(dve, n, pair, OVER)

            dve.wait_ge(sem("moe_used"), 1)
            step(V.tensor_tensor_reduce(xn[:, 1, :], x2[:, 1, :], x2[:, 1, :], 1.0, 0.0, ALU.mult, ALU.add, stat[:, 1:2]))
            dve.wait_ge(sem("ss3_done"), 1)
            step(V.tensor_scalar(stat[:, 2:4], stat[:, 0:2], 1.0 / D, EPS, ALU.mult, ALU.add), "ms3_done")
            dve.wait_ge(sem("root3_done"), 1)
            step(V.reciprocal(stat[:, 6:8], stat[:, 4:6]))
            dve.wait_ge(sem("norm_in"), 48)
            for half in range(2):
                for t in range(NT):
                    cols = slice(half * 512, half * 512 + 512)
                    step(V.scalar_tensor_tensor(out=x2[:, t, cols], in0=x2[:, t, cols], scalar=stat[:, 6 + t:7 + t],
                                                in1=final_w[:, cols], op0=ALU.mult, op1=ALU.mult), "x2_done", wait=False)
            def rest_of(name, dst, hi, k=2):
                b = take(dve, name)
                count["rests"] = count.get("rests", 0) + 1
                dve.wait_ge(sem("tile_rounded"), count["rests"])
                step(V.tensor_tensor(dst.bitcast(F32R), b[:].rearrange("p (k t) -> p k t", k=k), hi, ALU.subtract),
                     tile=name)

            for j in range(4):
                if j < ROUNDED - 1:
                    rest_of_weights(dve, j)
                rest_of(f"xT{j}", x_lo[:, 2 * j:2 * j + 2, :], x_hi[:, 2 * j:2 * j + 2, :])
            for n in range(ROUNDED - 1, 8):
                rest_of_weights(dve, n)
            for t in range(NT):
                b = take(dve, f"in{t}_2")
                for i in range(2):
                    step(V.tensor_copy(k_tok[:, t, :, i, :], b[:, 0:P].rearrange("p (h c) -> p h c", h=KVH)))
                step(V.tensor_copy(v_tok[:, t, :], b[:, P:2 * P]), tile=f"in{t}_2")
            dve.wait_ge(sem("mix_in"), 80)
            for what, u in attention_order(len(UNITS2)):
                h, blk = UNITS2[u]
                w = (blk + 1) * P
                if what == "score":
                    if u >= 2:
                        dve.wait_ge(full(f"tw{u - 2}"), use(f"tw{u - 2}") + 1)
                    for i in range(2):
                        b = take(dve, f"sw{u}_{i}")
                        step(V.scalar_tensor_tensor(out=prob2[:, u % 2, i * w:(i + 1) * w], in0=neg_dist[:, 2 * P - w:2 * P],
                                                    scalar=SLOPES[2 * h + i], in1=b[:, 0:w],
                                                    op0=ALU.mult, op1=ALU.add), tile=f"sw{u}_{i}")
                    step(V.tensor_reduce(soft[:, u, 0:2], prob2[:, u % 2, 0:2 * w].rearrange("p (i k) -> p i k", i=2),
                                         AX, ALU.max))
                    sink = sinks[:, 2 * h:2 * h + 2]
                    step(V.tensor_tensor(soft[:, u, 2:4], soft[:, u, 0:2], sink, ALU.max))
                    step(V.tensor_scalar(soft[:, u, 4:6], soft[:, u, 2:4], -1.0, None, ALU.mult), wait=False)
                    step(V.tensor_tensor(soft[:, u, 6:8], sink, soft[:, u, 2:4], ALU.subtract), "masked")
                    if u in (2, 4, 6):
                        rest_of_weights(dve, 7 + u // 2)
                    if u == 1:
                        for j in range(2):
                            b = take(dve, f"py{j}")
                            for i in range(2):
                                g = 2 * j + i
                                src = b[:, i * T:(i + 1) * T]
                                step(V.tensor_scalar(x_hi[:, g, :].bitcast(F32R), src, vecT[:, 12 + g:13 + g], None, ALU.mult))
                                step(V.scalar_tensor_tensor(out=x_lo[:, g, :].bitcast(F32R), in0=src, scalar=vecT[:, 12 + g:13 + g],
                                                            in1=x_hi[:, g, :], op0=ALU.mult, op1=ALU.subtract),
                                     tile=f"py{j}" if i else None)
                elif what == "value":
                    step(V.tensor_tensor(soft[:, u, 12:14], soft[:, u, 8:10], soft[:, u, 10:12], ALU.add))
                    step(V.reciprocal(soft[:, u, 14:16], soft[:, u, 12:14]))
                    b = take(dve, f"vw{u}")
                    step(V.tensor_tensor(o2[:, blk, h * P:(h + 1) * P].rearrange("p (i c) -> p i c", i=2),
                                         b[:, 0:P].rearrange("p (i c) -> p i c", i=2),
                                         soft[:, u, 14:16].unsqueeze(2).broadcast_to([P, 2, HD]), ALU.mult),
                         tile=f"vw{u}")
            rest_of_weights(dve, 11)
            for j in range(2):
                rest_of(f"oT{j}", x_lo[:, 4 + 2 * j:6 + 2 * j, :], x_hi[:, 4 + 2 * j:6 + 2 * j, :])

            def layer_norm(t, tiles, at, var, root, g, b_, done):
                for c in range(2):
                    cols = slice(c * 512, c * 512 + 512)
                    bk = take(dve, f"{tiles}{t}_{c}")
                    step(V.scalar_tensor_tensor(out=x2[:, t, cols], in0=x2[:, t, cols], scalar=DEEPNORM, in1=bk[:],
                                                op0=ALU.mult, op1=ALU.add), tile=f"{tiles}{t}_{c}")
                    step(V.bn_stats(bn[:, t, c, :], x2[:, t, cols]))
                step(V.bn_aggr(stat[:, 40 + 2 * t:42 + 2 * t], bn[:, t, :, :].rearrange("p c s -> p (c s)")))
                step(V.tensor_scalar(stat[:, at + t:at + t + 1], stat[:, 41 + 2 * t:42 + 2 * t], LN_EPS, None, ALU.add),
                     var)
                for c in range(2):
                    cols = slice(c * 512, c * 512 + 512)
                    step(V.scalar_tensor_tensor(out=x2[:, t, cols], in0=x2[:, t, cols], scalar=stat[:, 40 + 2 * t:41 + 2 * t],
                                                in1=g[:, cols], op0=ALU.subtract, op1=ALU.mult))
                    if c == 0:
                        dve.wait_ge(sem(root), t + 1)
                        step(V.reciprocal(stat[:, at + 8 + t:at + 9 + t], stat[:, at + 4 + t:at + 5 + t]))
                    step(V.scalar_tensor_tensor(out=x2[:, t, cols], in0=x2[:, t, cols], scalar=stat[:, at + 8 + t:at + 9 + t],
                                                in1=b_[:, cols], op0=ALU.mult, op1=ALU.add), done)

            layer_norm(0, "wo2", 12, "var1", "root4_done", ln1g, ln1b, "h1_done")
            rest_of_weights(dve, 12)
            rest_of_weights(dve, 13)
            layer_norm(1, "wo2", 12, "var1", "root4_done", ln1g, ln1b, "h1_done")
            for j in range(4):
                rest_of(f"h1T{j}", h_lo[:, 2 * j:2 * j + 2, :], x_hi[:, 2 * j:2 * j + 2, :])
            rest_of_weights(dve, 14)
            for j in range(16):
                wait_read(dve, f"part{j}")
                step(V.tensor_tensor(wide[:, j % 2, :], wide[:, j % 2, :], wide[:, j % 2, :], ALU.mult), "squared")
                dve.wait_ge(sem("wide_rounded"), j + 1)
                step(V.tensor_tensor(wide_lo[:, j % 2, :].bitcast(F32R), wide[:, j % 2, :], wide_hi[:, j % 2, :],
                                     ALU.subtract), "wide_done")
                for n in splits_at(j):
                    rest_of_weights(dve, n)
            for n in range(44, 47):
                rest_of_weights(dve, n)
            dve.wait_ge(sem("norm2_in"), 32)
            for t in range(NT):
                layer_norm(t, "wide", 22, "var2", "root5_done", ln2g, ln2b, "h2_done")
            for j in range(4):
                rest_of(f"h2T{j}", h_lo[:, 2 * j:2 * j + 2, :], x_hi[:, 2 * j:2 * j + 2, :])
            rest_of_weights(dve, 47)
            dve.wait_ge(sem("b_gate_in"), 16)
            for n in range(5):
                if n < 4:
                    t, c = divmod(n, 2)
                    b = take(dve, f"gate{t}_{c}")
                    step(V.tensor_tensor(gate_z[:, n, :], b[:], b_gate[:, c * 512:(c + 1) * 512], ALU.add), "gate_in",
                         wait=False)
                if n >= 1:
                    t, c = divmod(n - 1, 2)
                    cols = slice(c * 512, c * 512 + 512)
                    dve.wait_ge(sem("gate_done"), n)
                    b = take(dve, f"ple{t}_{c}")
                    step(V.tensor_tensor(gate_z[:, n - 1, :], gate_z[:, n - 1, :], b[:], ALU.mult))
                    step(V.tensor_tensor(x2[:, t, cols], x2[:, t, cols], gate_z[:, n - 1, :], ALU.add), "out_done")

        @block.tensor
        def _(pe):
            def mm(out_, lhsT, rhs, first, last):
                return pe.matmul(out_, lhsT, rhs, start=first, stop=last, skip_group_check=True)

            def mm3(out_, lhsT, rhs, first, last):
                (ah, al), (bh, bl) = lhsT, rhs
                mm(out_, ah, bh, first, False)
                mm(out_, ah, bl, False, False)
                return mm(out_, al, bh, False, last)

            freed = sem("ring_freed")

            pe.wait_ge(sem("consts"), 4)
            pe.wait_ge(sem("silu_done"), 1)
            b = claim(pe, "cT")
            pe.transpose(b[:, 0:16], small[0:16, :], ident[0:16, 0:16]).then_inc(full("cT"), 1)

            def ada(t, ks=range(KD)):
                name = f"ada{t}"
                b = claim(pe, name) if ks[0] == 0 else bank(name)
                for k in ks:
                    n = (name, k)
                    ring_wait(pe, n)
                    for q in range(4):
                        m = mm(b[32 * q:32 * q + 32, :], cT[:, k, :], slot(n)[:, q * 512:(q + 1) * 512],
                               k == 0, k == KD - 1)
                    if k < KD - 1:
                        m.then_inc(freed, 1)
                if ks[-1] == KD - 1:
                    m.then_inc(full(name), 1)
                    pe.wait_ge(full(name), use(name) + 1)
                    pe.sem_inc(freed, 1)

            wait_read(pe, "cT")
            pe.wait_ge(sem("xn_done"), 4)
            for k in range(KD):
                b = claim(pe, f"hT{k}")
                for t in range(4):
                    m = pe.transpose(b[:, t * P:(t + 1) * P], xn[:, t, k * P:(k + 1) * P], ident[:])
                m.then_inc(full(f"hT{k}"), 1)
            ada(0, range(0, 4))
            pe.wait_ge(sem("vec_in"), 16 * 5)
            b = claim(pe, "vecT")
            pe.transpose(b[:, 0:16], small[32:48, :], ident[32:48, 32:48]).then_inc(full("vecT"), 1)
            ada(0, range(4, KD))
            wait_read(pe, "ada0")
            b = claim(pe, "modT")
            for blk in range(4):
                m = pe.transpose(b[:, blk * P:(blk + 1) * P], mrows[:, 0, blk * P:(blk + 1) * P], ident[:])
            m.then_inc(full("modT"), 1)

            def proj(b, t, c, k):
                lo = 512 * c if c < 3 else (CKV if t < 2 else CQ)
                hi = 512 * (c + 1) if c < 3 else IN_COLS
                out_ = b[:, 0:hi - lo]
                if k < SPLIT_FROM:
                    return mm(out_, hT[:, k, t * P:(t + 1) * P], slot(("w_in", k))[:, lo:hi], k == 0, False)
                w = (in_hi(k)[:, lo:hi], in_lo[k][:, lo:hi])
                return mm3(out_, [v[:, k, t * P:(t + 1) * P].bitcast(F32R) for v in (tok_hi, tok_lo)],
                           [v.bitcast(F32R) for v in w], False, k == KD - 1)

            of_ctx = {(t, c): claim(pe, f"proj{t}_{c}") for t in range(2) for c in (1, 2, 3)}
            for k in range(KD):
                if k < SPLIT_FROM:
                    ring_wait(pe, ("w_in", k))
                    pe.wait_ge(sem("hT_done"), 2 * k + 2)
                else:
                    pe.wait_ge(sem("in_split"), 2 * (k - SPLIT_FROM) + 2)
                for (t, c), b in of_ctx.items():
                    m = proj(b, t, c, k)
                    if k == KD - 1:
                        m.then_inc(full(f"proj{t}_{c}"), 1)
            for t, c in [(2, 3), (3, 3)] + [(t, c) for t in (2, 3) for c in range(3)]:
                b = claim(pe, f"proj{t}_{c}")
                for k in range(KD):
                    m = proj(b, t, c, k)
                m.then_inc(full(f"proj{t}_{c}"), 1)
            pe.wait_ge(full("proj3_2"), use("proj3_2") + 1)
            pe.sem_inc(freed, KD)

            wait_read(pe, "proj0_1")
            wait_read(pe, "proj1_1")
            wait_read(pe, "proj2_1")
            wait_read(pe, "proj3_1")
            for h in range(H):
                b = claim(pe, f"dkT{h}")
                for t in range(4):
                    m = pe.transpose(b[:, t * P:(t + 1) * P], dk[:, t, h * P:(h + 1) * P], ident[:])
                m.then_inc(full(f"dkT{h}"), 1)
            wait_read(pe, "proj2_0")
            wait_read(pe, "proj3_0")
            for j in range(2):
                b = claim(pe, f"dqT{j}")
                for hh in range(2):
                    for t in range(NT):
                        h = 2 * j + hh
                        m = pe.transpose(b[:, hh * T + t * P:hh * T + (t + 1) * P], dq[:, t, h * P:(h + 1) * P], ident[:])
                m.then_inc(full(f"dqT{j}"), 1)

            pe.wait_ge(sem("lat_done"), 6)
            b = claim(pe, "ckvT")
            for t in range(4):
                m = pe.transpose(b[:, t * P:(t + 1) * P], ckv[:, t, :], ident[:])
            m.then_inc(full("ckvT"), 1)
            pe.wait_ge(sem("kr_done"), 4)
            b = claim(pe, "krT")
            for t in range(4):
                m = pe.transpose(b[:, t * P:(t + 1) * P], kr[:, t, :, :].rearrange("p a c -> p (a c)"), ident[:])
            m.then_inc(full("krT"), 1)
            b = claim(pe, "cqT")
            for k in range(2):
                for t in range(NT):
                    m = pe.transpose(b[:, k * T + t * P:k * T + (t + 1) * P], cq[:, t, k * P:(k + 1) * P], ident[:])
            m.then_inc(full("cqT"), 1)

            nq = ("w_uq", 0)
            ring_wait(pe, nq)
            wq = slot(nq)[:, 0:2 * 768].rearrange("p (k h c) -> p k h c", k=2, h=H)
            wait_read(pe, "cqT")
            b = claim(pe, "qrope")
            for t in range(NT):
                for k in range(2):
                    m = mm(b[:, t * 256:(t + 1) * 256], cqT[:, k, t * P:(t + 1) * P], wq[:, k, :, NOPE:NOPE + ROPE],
                           k == 0, k == 1)
            m.then_inc(full("qrope"), 1)
            for j in range(2):
                b = claim(pe, f"qnope{j}")
                for hh in range(2):
                    for k in range(2):
                        m = mm(b[:, hh * T:(hh + 1) * T], wq[:, k, 2 * j + hh, 0:NOPE], cqT[:, k, :], k == 0, k == 1)
                m.then_inc(full(f"qnope{j}"), 1)
            pe.wait_ge(full("qnope1"), use("qnope1") + 1)
            pe.sem_inc(freed, 1)
            nk = ("w_ukv", 0)
            ring_wait(pe, nk)
            wkv = slot(nk)[:, 0:1024].rearrange("p (h c) -> p h c", h=H)
            wait_read(pe, "ckvT")
            for h in range(H):
                b = claim(pe, f"knope{h}")
                mm(b[:], wkv[:, h, 0:NOPE], ckvT, True, True).then_inc(full(f"knope{h}"), 1)
            for t in range(4):
                b = claim(pe, f"mv{t}")
                m = mm(b[:], ckvT[:, t * P:(t + 1) * P], wkv[:, :, NOPE:2 * NOPE], True, True)
                m.then_inc(full(f"mv{t}"), 1)
            pe.wait_ge(full("mv3"), use("mv3") + 1)
            pe.sem_inc(freed, 1)
            wait_read(pe, "qrope")
            b = claim(pe, "qrT")
            for j in range(2):
                for t in range(NT):
                    m = pe.transpose(b[:, j * T + t * P:j * T + (t + 1) * P], qr[:, t, j * P:(j + 1) * P], ident[:])
            m.then_inc(full("qrT"), 1)

            for what, u in attention_order(len(UNITS)):
                kind, h, t = UNITS[u]
                if what == "score" and kind == "d":
                    if u == 0:
                        for x in ("dkT3", "dqT1", "proj3_2", "proj2_2", "proj1_2", "proj0_2"):
                            wait_read(pe, x)
                    for c in range(2):
                        b = claim(pe, f"s{u}_{c}")
                        rows = slice(64 * c, 64 * c + 64)
                        mm(b[:], dqT[rows, h, t * P:(t + 1) * P], dkT[rows, h, :], True, True)\
                            .then_inc(full(f"s{u}_{c}"), 1)
                elif what == "score":
                    if UNITS[u - 1][0] == "d":
                        for x in ("knope3", "qnope1", "krT", "qrT", "mv3"):
                            wait_read(pe, x)
                    b = claim(pe, f"s{u}_0")
                    rows = slice(64 * (h % 2), 64 * (h % 2) + 64)
                    mm(b[:], qnT[:, h, t * P:(t + 1) * P], knT[:, h, :], True, False)
                    mm(b[:], qrT[rows, h // 2, t * P:(t + 1) * P], krT[rows, :], False, True)\
                        .then_inc(full(f"s{u}_0"), 1)
                elif what == "turn":
                    pe.wait_ge(sem("pmix_done"), u + 1)
                    b = claim(pe, f"pT{u}")
                    for n in range(4):
                        m = pe.transpose(b[:, n * P:(n + 1) * P], prob[:, u % 2, 0, n * P:(n + 1) * P], ident[:])
                    m.then_inc(full(f"pT{u}"), 1)
                else:
                    wait_read(pe, f"pT{u}")
                    b = claim(pe, f"av{u}")
                    vals = dv if kind == "d" else mv
                    for n in range(4):
                        m = mm(b[:, 0:P], probT[:, u % 2, n * P:(n + 1) * P], vals[:, n, h * P:(h + 1) * P],
                               n == 0, n == 3)
                    m.then_inc(full(f"av{u}"), 1)
                if what == "value" and u == 3:
                    ada(1)
                    ada(2)
                    wait_read(pe, "ada1")
                    wait_read(pe, "ada2")
                    for n, (third, q) in enumerate(((1, 0), (1, 1), (1, 2), (1, 3), (2, 0), (2, 1), (2, 2), (2, 3))):
                        b = claim(pe, f"bc{n}")
                        mm(b[:], ones[32 * q:32 * q + 1, :], mrows[32 * q:32 * q + 1, third, :], True, True)\
                            .then_inc(full(f"bc{n}"), 1)

            for j in range(4):
                if j == 0:
                    pe.wait_ge(sem("sub_done"), NT)
                elif j >= 2:
                    for u in range(8 + 4 * (j - 2), 12 + 4 * (j - 2)):
                        wait_read(pe, f"av{u}")
                b = claim(pe, f"mixT{j}")
                for kk in range(2):
                    for t in range(NT):
                        k = 2 * j + kk
                        m = pe.transpose(b[:, kk * T + t * P:kk * T + (t + 1) * P], o[:, t, k * P:(k + 1) * P], ident[:])
                m.then_inc(full(f"mixT{j}"), 1)
            bw = {(t, n): claim(pe, f"wo{t}_{n}") for t in range(NT) for n in range(2)}
            for t in range(NT):
                for j in range(4):
                    n_ = ("w_out", j)
                    if t == 0:
                        ring_wait(pe, n_)
                        wait_read(pe, f"mixT{j}")
                    w = slot(n_).rearrange("p (k n) -> p k n", k=2)
                    for n in range(2):
                        for kk in range(2):
                            k = 2 * j + kk
                            m = mm(bw[t, n][:], mixT[:, k, t * P:(t + 1) * P], w[:, kk, n * 512:(n + 1) * 512],
                                   k == 0, k == KD - 1)
                        if j == 3:
                            m.then_inc(full(f"wo{t}_{n}"), 1)
                        elif t == 1 and n == 1:
                            m.then_inc(freed, 1)

            for t in range(NT):
                for j in range(4):
                    pe.wait_ge(sem("hf_done"), 2 * t + 1 + j // 2)
                    b = claim(pe, f"hfT{t}_{j}")
                    for kk in range(2):
                        k = 2 * j + kk
                        m = pe.transpose(b[:, kk * P:(kk + 1) * P], hf[:, t, k * P:(k + 1) * P], ident[:])
                    m.then_inc(full(f"hfT{t}_{j}"), 1)
                if t == 0:
                    pe.wait_ge(full("wo1_1"), use("wo1_1") + 1)
                    pe.sem_inc(freed, 1)
                    pe.wait_ge(sem("router_in"), 32)
                    b_logits = claim(pe, "logits")
                for k in range(KD):
                    if k % 2 == 0:
                        wait_read(pe, f"hfT{t}_{k // 2}")
                    mm(b_logits[:, t * E:(t + 1) * E], hfT[:, k, t * P:(t + 1) * P], rw[:, k, :], k == 0, False)
                m = mm(b_logits[:, t * E:(t + 1) * E], ones[0:1, :], rb[:], False, True)
            m.then_inc(full("logits"), 1)
            pe.wait_ge(sem("chosen_done"), 1)
            pe.wait_ge(sem("below_done"), 1)
            b = claim(pe, "rank")
            mm(b[:, 0:E], below, chosen[:, 0, :], True, True)
            mm(b[:, E:2 * E], ones[:], chosen[:, 0, :], True, False)
            mm(b[:, E:2 * E], below, chosen[:, 1, :], False, True)
            mm(b[:, 2 * E:3 * E], ones[:], chosen[:, 0, :], True, False)
            mm(b[:, 2 * E:3 * E], ones[:], chosen[:, 1, :], False, True).then_inc(full("rank"), 1)
            for name in FRONT_TILES[-8:]:
                wait_read(pe, name)

            pe.wait_ge(sem("pick_done"), 1)
            gather(pe, 0, MAIN, None)
            with pe.Fori(0, PAIRS) as pair:
                hidden(pe, pair, MAIN)
                gather(pe, pair + 1, MAIN, pair * 4 + 1)
                pe_rest(pe, pair, MAIN, 1)
            pe.wait_ge(moe("y_added", MAIN), 4 * PAIRS + 1)
            most_pe = load_most(pe)
            pe.sem_inc(moe("ring_freed", OVER), SLOTS)
            with pe.If(most_pe > CAP):
                with pe.Fori(1, ROUNDS) as r:
                    with pe.If(most_pe > r * CAP):
                        with pe.Fori(0, PAIRS) as pair:
                            n = (r - 1) * PAIRS + pair
                            gather(pe, n, OVER, n * 4 + 1)
                            hidden(pe, n, OVER)
                            pe_rest(pe, n, OVER, 0)
                            pe.wait_ge(moe("y_added", OVER), 4 * n + 5)

            pe.wait_ge(moe("mixed", MAIN), 4 * PAIRS)
            pe.sem_inc(sem("moe_used"), 1)

            def turn_tokens(name, src, ready, by_tile=True):
                for j in range(4):
                    pe.wait_ge(sem(ready), NT + 1 + j // 2 if by_tile else NT * (1 + j // 2))
                    b = claim(pe, f"{name}{j}")
                    for kk in range(2):
                        for t in range(NT):
                            k = 2 * j + kk
                            m = pe.transpose(b[:, kk * T + t * P:kk * T + (t + 1) * P], src[:, t, k * P:(k + 1) * P], ident[:])
                    m.then_inc(full(f"{name}{j}"), 1)

            turn_tokens("xT", x2, "x2_done", False)
            parts = [(0, 512), (512, 1024), (1024, 1280)]
            bi = {(t, n): claim(pe, f"in{t}_{n}") for t in range(NT) for n in range(3)}
            for k in range(KD):
                w = split_weights(pe, ("w_in2", k))
                wait_read(pe, f"xT{k // 2}")
                for t in range(NT):
                    for n, (lo, hi) in enumerate(parts):
                        m = mm3(bi[t, n][:, 0:hi - lo], [v[:, k, t * P:(t + 1) * P].bitcast(F32R) for v in (x_hi, x_lo)],
                                [v[:, lo:hi] for v in w], k == 0, k == KD - 1)
                        if k == KD - 1:
                            m.then_inc(full(f"in{t}_{n}"), 1)
                if k < KD - 1:
                    m.then_inc(freed, 1)
            wait_read(pe, "in1_2")
            pe.sem_inc(freed, 1)
            wait_read(pe, "in0_2")
            b = claim(pe, "kT")
            for h in range(KVH):
                for t in range(NT):
                    m = pe.transpose(b[:, h * T + t * P:h * T + (t + 1) * P],
                                     k_tok[:, t, h].rearrange("p a c -> p (a c)"), ident[:])
            m.then_inc(full("kT"), 1)
            wait_read(pe, "in0_1")
            wait_read(pe, "in1_1")
            for j in range(2):
                b = claim(pe, f"qT{j}")
                for i in range(2):
                    for t in range(NT):
                        k = 2 * j + i
                        m = pe.transpose(b[:, i * T + t * P:i * T + (t + 1) * P], q_tok[:, t, k * P:(k + 1) * P], ident[:])
                m.then_inc(full(f"qT{j}"), 1)
            wait_read(pe, "in0_0")
            wait_read(pe, "in1_0")
            pe.wait_ge(sem("mix_in"), 80)
            for j in range(2):
                b = claim(pe, f"pd{j}")
                for i in range(2):
                    g = 2 * j + i
                    for t in range(NT):
                        m = mm(b[:, i * T:(i + 1) * T], u_tok[:, t, g * P:(g + 1) * P], bands[:, g, t, :], t == 0, t == 1)
                m.then_inc(full(f"pd{j}"), 1)
            for j in range(2):
                wait_read(pe, f"pd{j}")
                b = claim(pe, f"py{j}")
                for i in range(2):
                    g = 2 * j + i
                    m = mm(b[:, i * T:(i + 1) * T], w_pool[:, g, :], pool_dT[:, g, :], True, True)
                m.then_inc(full(f"py{j}"), 1)
            wait_read(pe, "kT")
            wait_read(pe, "qT1")
            for what, u in attention_order(len(UNITS2)):
                h, blk = UNITS2[u]
                w = (blk + 1) * P
                if what == "score":
                    for i in range(2):
                        b = claim(pe, f"sw{u}_{i}")
                        rows = slice(HD * i, HD * i + HD)
                        mm(b[:, 0:w], q2T[rows, h, blk * P:(blk + 1) * P], k2T[rows, h // 2, 0:w], True, True)\
                            .then_inc(full(f"sw{u}_{i}"), 1)
                elif what == "turn":
                    pe.wait_ge(sem("exp2_done"), u + 1)
                    b = claim(pe, f"tw{u}")
                    for n in range(2 * (blk + 1)):
                        m = pe.transpose(b[:, n * P:(n + 1) * P], prob2[:, u % 2, n * P:(n + 1) * P], ident[:])
                    m.then_inc(full(f"tw{u}"), 1)
                else:
                    wait_read(pe, f"tw{u}")
                    b = claim(pe, f"vw{u}")
                    kv = (h // 2) * HD
                    for i in range(2):
                        for n in range(blk + 1):
                            m = mm(b[:, i * HD:(i + 1) * HD], prob2T[u % 2][:, i * w + n * P:i * w + (n + 1) * P],
                                   v_tok[:, n, kv:kv + HD], n == 0, n == blk)
                    m.then_inc(full(f"vw{u}"), 1)
            for j in range(2):
                for u in range(4 * j, 4 * j + 4):
                    wait_read(pe, f"vw{u}")
                b = claim(pe, f"oT{j}")
                for i in range(2):
                    for t in range(NT):
                        k = 2 * j + i
                        m = pe.transpose(b[:, i * T + t * P:i * T + (t + 1) * P], o2[:, t, k * P:(k + 1) * P], ident[:])
                m.then_inc(full(f"oT{j}"), 1)

            def by_pairs(kind, tiles, src, ready, by_tile=False):
                bw = {(t, n): claim(pe, f"{tiles}{t}_{n}") for t in range(NT) for n in range(2)}
                order = ([(t, n, j) for t in range(NT) for n in range(2) for j in range(4)] if by_tile else
                         [(t, n, j) for t in range(NT) for j in range(4) for n in range(2)])
                for t, n, j in order:
                    if t == 0 and n == 0:
                        for name in ready(j):
                            wait_read(pe, name)
                    w = [v.rearrange("p (k n) -> p k n", k=2) for v in split_weights(pe, (kind, j))]
                    for kk in range(2):
                        k = 2 * j + kk
                        m = mm3(bw[t, n][:], [v[:, k, t * P:(t + 1) * P].bitcast(F32R) for v in src],
                                [v[:, kk, n * 512:(n + 1) * 512] for v in w], k == 0, k == KD - 1)
                    if j == 3:
                        m.then_inc(full(f"{tiles}{t}_{n}"), 1)
                    elif t == 1 and n == 1:
                        m.then_inc(freed, 1)

            by_pairs("w_out2", "wo2", (x_hi, x_lo), lambda j: [["py0"], ["py1"], ["oT0"], ["oT1"]][j])
            b = claim(pe, "plT")
            for k in range(2):
                for t in range(NT):
                    m = pe.transpose(b[:, k * T + t * P:k * T + (t + 1) * P], p_tok[:, t, k * P:(k + 1) * P], ident[:])
            m.then_inc(full("plT"), 1)
            turn_tokens("h1T", x2, "h1_done")
            sums = {(t, c): claim(pe, f"wide{t}_{c}") for t in range(NT) for c in range(2)}

            def wide_part(j):
                if j == 0:
                    for i in range(4):
                        wait_read(pe, f"h1T{i}")
                w = [v.rearrange("p (k n) -> p k n", k=KD) for v in split_weights(pe, ("ff1", j))]
                b = claim(pe, f"part{j}")
                for i in range(2):
                    for k in range(KD):
                        m = mm3(b[:, i * T:(i + 1) * T], [v[:, k, i * P:(i + 1) * P] for v in w],
                                [v[:, k, :].bitcast(F32R) for v in (x_hi, h_lo)], k == 0, k == KD - 1)
                m.then_inc(full(f"part{j}"), 1)

            def wide_sum(j):
                pe.wait_ge(sem("wide_done"), j + 1)
                w = [v.rearrange("p (k n) -> p k n", k=2) for v in split_weights(pe, ("ff2", j))]
                for t in range(NT):
                    for c in range(2):
                        for kk in range(2):
                            at = kk * T + t * P
                            m = mm3(sums[t, c][:], [v[:, j % 2, at:at + P].bitcast(F32R) for v in (wide_hi, wide_lo)],
                                    [v[:, kk, c * 512:(c + 1) * 512] for v in w], j == 0 and kk == 0, j == 15 and kk == 1)
                        if j == 15:
                            m.then_inc(full(f"wide{t}_{c}"), 1)
                        elif t == 1 and c == 1:
                            m.then_inc(sem("wide_used"), 1)

            wide_part(0)
            for j in range(16):
                if j < 15:
                    wide_part(j + 1)
                wide_sum(j)

            ring_wait(pe, ("w_ple", 0))
            wait_read(pe, "plT")
            w = slot(("w_ple", 0)).rearrange("p (k n) -> p k n", k=2)
            for t in range(NT):
                for c in range(2):
                    b = claim(pe, f"ple{t}_{c}")
                    for k in range(2):
                        m = mm(b[:], pT[:, k, t * P:(t + 1) * P], w[:, k, c * 512:(c + 1) * 512], k == 0, k == 1)
                    m.then_inc(full(f"ple{t}_{c}"), 1)
            turn_tokens("h2T", x2, "h2_done")
            by_pairs("gate", "gate", (x_hi, h_lo), lambda j: [f"h2T{j}"], by_tile=True)


INPUTS = [
    "x", "c", "ctx", "c_ctx", "w_ada", "b_ada", "attn_norm_w", "w_in", "q_norm_w", "kv_norm_w", "w_uq", "w_ukv",
    "lambda_q1", "lambda_k1", "lambda_q2", "lambda_k2", "subln_w", "w_out", "ffn_norm_w", "router_w", "router_b",
    "w1", "b1", "w2", "b2", "final_norm_w", "p_2", "w_in_2", "w_pool_2", "pool_scale_2", "attn_sinks_2", "w_out_2",
    "ln1_g_2", "ln1_b_2", "w_ff1_2", "w_ff2_2", "ln2_g_2", "ln2_b_2", "w_ple_2", "w_ple_gate_2", "b_ple_gate_2",
]


def shape_tables():
    import numpy as np

    pairs, grid_w = 16, 64
    row = np.repeat(np.arange(T // grid_w, dtype=np.float32), grid_w)
    col = np.tile(np.arange(grid_w, dtype=np.float32), T // grid_w)
    inv = (np.float32(10000.0) ** (-np.arange(pairs, dtype=np.float32) / np.float32(pairs))).astype(np.float32)
    ang = np.stack([row[:, None] * inv, col[:, None] * inv], axis=1).astype(np.float32)
    cos = np.cos(ang).astype(np.float32)
    sin = np.sin(ang).astype(np.float32)
    dist = np.arange(P)[:, None] + P - np.arange(2 * P)[None, :]
    neg_dist = np.where((dist >= 0) & (dist < P), -dist, -1e32).astype(np.float32)
    pool_bands = np.zeros((4, T, T), np.float32)
    for g, w in enumerate((2, 4, 8, 16)):
        for t in range(T):
            lo = max(t + 1 - w, 0)
            pool_bands[g, lo:t + 1, t] = np.float32(1.0) / np.float32(t + 1 - lo)
            pool_bands[g, t, t] -= np.float32(1.0)
    return {
        "rope_cos": np.ascontiguousarray(np.concatenate([cos, cos], axis=2).reshape(T, 64)),
        "rope_sin": np.ascontiguousarray(sin.reshape(T, 32)),
        "neg_dist": neg_dist,
        "pool_bands": pool_bands,
    }


def kernel(**inputs):
    import numpy as np
    import concourse.bacc as bacc
    from concourse.bass_utils import run_bass_kernel_spmd as run

    nc = bacc.Bacc("TRN2", target_bir_lowering=False, num_devices=1)
    arrays, args = {}, {}
    tables = shape_tables()
    for name in INPUTS + list(tables):
        v = np.ascontiguousarray(inputs[name] if name in inputs else tables[name])
        arrays[f"in_{name}"] = v
        args[name] = nc.dram_tensor(f"in_{name}", v.shape, mybir.dt.from_np(v.dtype), kind="ExternalInput").ap()
    out = nc.dram_tensor("out", (1, T, D), F32, kind="ExternalOutput").ap()
    build(nc, args, out)
    return run(nc, [arrays], core_ids=[0]).results[0]["out"]
```
